# Optimizing a Trainium2 kernel written in Bass

```python
import math
import jax, jax.numpy as jnp
from jax import lax
import numpy as np

D_MODEL = 1024
BATCH = 1
SEQ = 256
DEPTH = 2

N_A_LAYERS = DEPTH // 2
N_B_LAYERS = DEPTH - N_A_LAYERS
RET_HEADS = 4
RET_QK_DIM = D_MODEL // RET_HEADS
RET_V_DIM = 2 * RET_QK_DIM
RET_CHUNK = 128
RET_THETA = 10000.0
RET_IN_WIDTH = 2 * RET_HEADS * RET_QK_DIM + 2 * RET_HEADS * RET_V_DIM
DIFF_HEADS = 8
DIFF_HEAD_DIM = D_MODEL // (2 * DIFF_HEADS)
DIFF_V_DIM = 2 * DIFF_HEAD_DIM
ROPE_THETA = 500000.0
ROPE_DIM = DIFF_HEAD_DIM // 4
Q_BLOCK = 128
PEER_HEADS = 8
PEER_N_KEYS = 128
PEER_N_EXPERTS = PEER_N_KEYS * PEER_N_KEYS
PEER_KEY_DIM = 256
PEER_TOPK = 16
PEER_CHUNK = 128
DN_ALPHA = (2 * DEPTH) ** 0.25
DN_BETA = (8 * DEPTH) ** -0.25
LN_EPS = 1e-5


def layer_norm(x, g, b):
    xf = x.astype(jnp.float32)
    mu = jnp.mean(xf, axis=-1, keepdims=True)
    var = jnp.mean(jnp.square(xf - mu), axis=-1, keepdims=True)
    y = (xf - mu) * lax.rsqrt(var + LN_EPS)
    return (y * g.astype(jnp.float32) + b.astype(jnp.float32)).astype(x.dtype)

def rope(x, angles):
    r2 = angles.shape[-1]
    r = 2 * r2
    shape = (1, angles.shape[0]) + (1,) * (x.ndim - 3) + (r2,)
    cos = jnp.cos(angles).reshape(shape)
    sin = jnp.sin(angles).reshape(shape)
    xf = x.astype(jnp.float32)
    x1 = xf[..., :r2]
    x2 = xf[..., r2:r]
    out = jnp.concatenate([x1 * cos - x2 * sin, x1 * sin + x2 * cos, xf[..., r:]], axis=-1)
    return out.astype(x.dtype)

def retention(x, w_in, w_out, angles):
    b, s, _ = x.shape
    nc = s // RET_CHUNK
    hq = RET_HEADS * RET_QK_DIM
    hv = RET_HEADS * RET_V_DIM
    proj = x @ w_in
    q = proj[..., :hq].reshape(b, s, RET_HEADS, RET_QK_DIM)
    k = proj[..., hq:2 * hq].reshape(b, s, RET_HEADS, RET_QK_DIM)
    v = proj[..., 2 * hq:2 * hq + hv].reshape(b, s, RET_HEADS, RET_V_DIM)
    g = proj[..., 2 * hq + hv:]
    q = rope(q, angles)
    k = rope(k, angles) * (RET_QK_DIM ** -0.5)

    def to_chunks(t):
        return t.astype(jnp.float32).reshape(b, nc, RET_CHUNK, RET_HEADS, -1).transpose(1, 0, 3, 2, 4)

    qc, kc, vc = to_chunks(q), to_chunks(k), to_chunks(v)
    log_g = jnp.log(1.0 - jnp.exp2(-5.0 - jnp.arange(RET_HEADS, dtype=jnp.float32)))
    ar = jnp.arange(RET_CHUNK, dtype=jnp.float32)
    rel = ar[:, None] - ar[None, :]
    decay_mask = jnp.where(rel[None] >= 0, jnp.exp(jnp.maximum(rel, 0.0)[None] * log_g[:, None, None]), 0.0)
    q_decay = jnp.exp((ar + 1.0)[None] * log_g[:, None])[None, :, :, None]
    k_decay = jnp.exp((RET_CHUNK - 1.0 - ar)[None] * log_g[:, None])[None, :, :, None]
    chunk_decay = jnp.exp(RET_CHUNK * log_g)[None, :, None, None]

    def step(state, inp):
        qi, ki, vi = inp
        sc = jnp.einsum('bhid,bhjd->bhij', qi, ki) * decay_mask
        intra = jnp.einsum('bhij,bhje->bhie', sc, vi)
        inter = jnp.einsum('bhid,bhde->bhie', qi, state) * q_decay
        state = state * chunk_decay + jnp.einsum('bhjd,bhje->bhde', ki * k_decay, vi)
        return state, intra + inter

    state0 = jnp.zeros((b, RET_HEADS, RET_QK_DIM, RET_V_DIM), jnp.float32)
    _, y = lax.scan(step, state0, (qc, kc, vc))
    y = y.transpose(1, 0, 3, 2, 4).reshape(b, s, RET_HEADS, RET_V_DIM)
    mu = jnp.mean(y, axis=-1, keepdims=True)
    var = jnp.mean(jnp.square(y - mu), axis=-1, keepdims=True)
    y = ((y - mu) * lax.rsqrt(var + LN_EPS)).reshape(b, s, hv)
    return (jax.nn.silu(g) * y.astype(x.dtype)) @ w_out

def diff_attention(x, w_q, lam_p, subln_g, w_out, k_sh, v_sh, layer_idx, angles):
    b, s, _ = x.shape
    q = (x @ w_q).reshape(b, s, DIFF_HEADS, 2, DIFF_HEAD_DIM)
    q = rope(q, angles) * (DIFF_HEAD_DIM ** -0.5)
    lam_init = 0.8 - 0.6 * math.exp(-0.3 * layer_idx)
    lp = lam_p.astype(jnp.float32)
    lam = jnp.exp(jnp.sum(lp[0] * lp[1])) - jnp.exp(jnp.sum(lp[2] * lp[3])) + lam_init
    outs = []
    for i in range(s // Q_BLOCK):
        s0 = i * Q_BLOCK
        end = s0 + Q_BLOCK
        qb = q[:, s0:end]
        kb = k_sh[:, :end]
        vb = v_sh[:, :end]
        sc = jnp.einsum('bqhmd,bkhmd->bhmqk', qb, kb).astype(jnp.float32)
        mask = jnp.arange(end)[None, :] <= (s0 + jnp.arange(Q_BLOCK))[:, None]
        p = jax.nn.softmax(jnp.where(mask, sc, -jnp.inf), axis=-1)
        a = p[:, :, 0] - lam * p[:, :, 1]
        outs.append(jnp.einsum('bhqk,bkhe->bqhe', a.astype(vb.dtype), vb))
    o = jnp.concatenate(outs, axis=1).astype(jnp.float32)
    o = o * lax.rsqrt(jnp.mean(jnp.square(o), axis=-1, keepdims=True) + LN_EPS)
    o = o * subln_g.astype(jnp.float32) * (1.0 - lam_init)
    return o.reshape(b, s, DIFF_HEADS * DIFF_V_DIM).astype(x.dtype) @ w_out

def peer_ffn(x, w_q, subkeys, u, v):
    b, s, d = x.shape
    xs = x.reshape(b * s // PEER_CHUNK, PEER_CHUNK, d)
    half = PEER_KEY_DIM // 2
    ncand = PEER_TOPK * PEER_TOPK

    def block(xc):
        q = (xc @ w_q).reshape(PEER_CHUNK, PEER_HEADS, 2, half)
        sc = jnp.einsum('thpd,hpnd->thpn', q, subkeys).astype(jnp.float32)
        s1, i1 = lax.top_k(sc[:, :, 0], PEER_TOPK)
        s2, i2 = lax.top_k(sc[:, :, 1], PEER_TOPK)
        cand = (s1[..., :, None] + s2[..., None, :]).reshape(PEER_CHUNK, PEER_HEADS, ncand)
        cidx = (i1[..., :, None] * PEER_N_KEYS + i2[..., None, :]).reshape(PEER_CHUNK, PEER_HEADS, ncand)
        top, pos = lax.top_k(cand, PEER_TOPK)
        idx = jnp.take_along_axis(cidx, pos, axis=-1).reshape(PEER_CHUNK, PEER_HEADS * PEER_TOPK)
        gate = jax.nn.softmax(top, axis=-1).reshape(PEER_CHUNK, PEER_HEADS * PEER_TOPK)
        u_e = jnp.take(u, idx, axis=0)
        v_e = jnp.take(v, idx, axis=0)
        act = jax.nn.gelu(jnp.einsum('ted,td->te', u_e, xc).astype(jnp.float32))
        return jnp.einsum('te,ted->td', (gate * act).astype(v_e.dtype), v_e)

    return lax.map(block, xs).reshape(b, s, d).astype(x.dtype)

def first_inputs(seed: int = 0) -> dict:
    key = jax.random.key(seed)
    ks = jax.random.split(key, 14)
    f32 = jnp.float32
    d = D_MODEL
    nrm = lambda k, shape, scale: jax.random.normal(k, shape, f32) * scale
    return {
        "x": nrm(ks[0], (BATCH, SEQ, d), 1.0),
        "ret_w_in": nrm(ks[1], (N_A_LAYERS, d, RET_IN_WIDTH), d ** -0.5),
        "ret_w_out": nrm(ks[2], (N_A_LAYERS, RET_HEADS * RET_V_DIM, d), DN_BETA * (RET_HEADS * RET_V_DIM) ** -0.5),
        "kv_w": nrm(ks[3], (d, DIFF_HEADS * 2 * DIFF_HEAD_DIM + DIFF_HEADS * DIFF_V_DIM), d ** -0.5),
        "diff_w_q": nrm(ks[4], (N_B_LAYERS, d, DIFF_HEADS * 2 * DIFF_HEAD_DIM), d ** -0.5),
        "diff_lambda": nrm(ks[5], (N_B_LAYERS, 4, DIFF_HEAD_DIM), 0.1),
        "diff_subln_g": 1.0 + nrm(ks[6], (N_B_LAYERS, DIFF_V_DIM), 0.02),
        "diff_w_out": nrm(ks[7], (N_B_LAYERS, DIFF_HEADS * DIFF_V_DIM, d), DN_BETA * (DIFF_HEADS * DIFF_V_DIM) ** -0.5),
        "peer_w_q": nrm(ks[8], (DEPTH, d, PEER_HEADS * PEER_KEY_DIM), d ** -0.5),
        "peer_subkeys": nrm(ks[9], (DEPTH, PEER_HEADS, 2, PEER_N_KEYS, PEER_KEY_DIM // 2), (PEER_KEY_DIM // 2) ** -0.5),
        "peer_u": nrm(ks[10], (DEPTH, PEER_N_EXPERTS, d), d ** -0.5),
        "peer_v": nrm(ks[11], (DEPTH, PEER_N_EXPERTS, d), DN_BETA * PEER_HEADS ** -0.5),
        "ln_g": 1.0 + nrm(ks[12], (DEPTH, 2, d), 0.02),
        "ln_b": nrm(ks[13], (DEPTH, 2, d), 0.02),
    }

def first_block(x, ret_w_in, ret_w_out, kv_w, diff_w_q, diff_lambda, diff_subln_g, diff_w_out,
              peer_w_q, peer_subkeys, peer_u, peer_v, ln_g, ln_b):
    b, s, _ = x.shape
    pos = jnp.arange(s, dtype=jnp.float32)
    ret_freqs = 1.0 / (RET_THETA ** jnp.linspace(0.0, 1.0, RET_QK_DIM // 2, dtype=jnp.float32))
    ret_angles = pos[:, None] * ret_freqs[None, :]
    diff_freqs = ROPE_THETA ** (-jnp.arange(0, ROPE_DIM, 2, dtype=jnp.float32) / ROPE_DIM)
    diff_angles = pos[:, None] * diff_freqs[None, :]
    kw = DIFF_HEADS * 2 * DIFF_HEAD_DIM
    k_sh = None
    v_sh = None
    for l in range(DEPTH):
        if l < N_A_LAYERS:
            mix = retention(x, ret_w_in[l], ret_w_out[l], ret_angles)
        else:
            j = l - N_A_LAYERS
            mix = diff_attention(x, diff_w_q[j], diff_lambda[j], diff_subln_g[j], diff_w_out[j],
                                 k_sh, v_sh, l, diff_angles)
        x = layer_norm(DN_ALPHA * x + mix, ln_g[l, 0], ln_b[l, 0])
        x = layer_norm(DN_ALPHA * x + peer_ffn(x, peer_w_q[l], peer_subkeys[l], peer_u[l], peer_v[l]),
                       ln_g[l, 1], ln_b[l, 1])
        if l == N_A_LAYERS - 1:
            kv = x @ kv_w
            k_sh = rope(kv[..., :kw].reshape(b, s, DIFF_HEADS, 2, DIFF_HEAD_DIM), diff_angles)
            v_sh = kv[..., kw:].reshape(b, s, DIFF_HEADS, DIFF_V_DIM)
    return x


CHUNK = 64
N_MIXERS = 2
N_MLA_LAYERS = (DEPTH + 1) // 2
N_FOX_LAYERS = DEPTH // 2
D_FF = 256 * ((8 * D_MODEL // 3 + 255) // 256)
PLE_DIM = 256
MLA_HEADS = 8
MLA_NOPE = 128
MLA_ROPE = 64
MLA_V = 128
MLA_Q_LORA = 256
MLA_KV_LORA = 128
ROPE_THETA_2 = 10000.0
FOX_HEADS = 8
FOX_HEAD_DIM = 128
NORM_EPS = 1e-6
NEG_INF = -1e30


def rms_norm(x, g):
    xf = x.astype(jnp.float32)
    y = xf * lax.rsqrt(jnp.mean(xf * xf, axis=-1, keepdims=True) + NORM_EPS)
    return (y * g.astype(jnp.float32)).astype(x.dtype)

def swiglu(x, w_in, w_out):
    gate, up = jnp.split(x @ w_in, 2, axis=-1)
    return (jax.nn.silu(gate) * up) @ w_out

def apply_rope(x, cos, sin):
    x1, x2 = jnp.split(x, 2, axis=-1)
    return jnp.concatenate([x1 * cos - x2 * sin, x2 * cos + x1 * sin], axis=-1)

def causal_block_attention(scores_fn, v, chunk_causal):
    seq = v.shape[1]
    outs = []
    for q0 in range(0, seq, Q_BLOCK):
        q1 = q0 + Q_BLOCK
        s = scores_fn(q0, q1)
        q_pos = jnp.arange(q0, q1)
        k_pos = jnp.arange(q1)
        if chunk_causal:
            allowed = (k_pos[None, :] // CHUNK) <= (q_pos[:, None] // CHUNK)
        else:
            allowed = k_pos[None, :] <= q_pos[:, None]
        s = jnp.where(allowed, s, NEG_INF)
        probs = jax.nn.softmax(s, axis=-1).astype(v.dtype)
        outs.append(jnp.einsum('bhqk,bkhd->bqhd', probs, v[:, :q1]))
    return jnp.concatenate(outs, axis=1)

def mla_mixer(u, cos, sin, w_down, q_norm, w_uq, kv_norm, w_ukv, w_o):
    b, s, _ = u.shape
    c = u @ w_down
    c_q, c_kv, k_rope = jnp.split(c, [MLA_Q_LORA, MLA_Q_LORA + MLA_KV_LORA], axis=-1)
    q = (rms_norm(c_q, q_norm) @ w_uq).reshape(b, s, MLA_HEADS, MLA_NOPE + MLA_ROPE)
    q_nope, q_rope = jnp.split(q, [MLA_NOPE], axis=-1)
    q_rope = apply_rope(q_rope, cos[:, :, None, :], sin[:, :, None, :])
    k_rope = apply_rope(k_rope, cos, sin)
    kv = (rms_norm(c_kv, kv_norm) @ w_ukv).reshape(b, s, MLA_HEADS, MLA_NOPE + MLA_V)
    k_nope, v = jnp.split(kv, [MLA_NOPE], axis=-1)
    scale = (MLA_NOPE + MLA_ROPE) ** -0.5

    def scores(q0, q1):
        sc = (jnp.einsum('bqhd,bkhd->bhqk', q_nope[:, q0:q1], k_nope[:, :q1])
              + jnp.einsum('bqhr,bkr->bhqk', q_rope[:, q0:q1], k_rope[:, :q1]))
        return sc.astype(jnp.float32) * scale

    o = causal_block_attention(scores, v, chunk_causal=True)
    return o.reshape(b, s, MLA_HEADS * MLA_V) @ w_o

def fox_mixer(u, w_in, b_f, w_o):
    b, s, _ = u.shape
    hd = FOX_HEADS * FOX_HEAD_DIM
    proj = u @ w_in
    q, k, v, f_logit = jnp.split(proj, [hd, 2 * hd, 3 * hd], axis=-1)
    q = q.reshape(b, s, FOX_HEADS, FOX_HEAD_DIM)
    k = k.reshape(b, s, FOX_HEADS, FOX_HEAD_DIM)
    v = v.reshape(b, s, FOX_HEADS, FOX_HEAD_DIM)
    log_f = jax.nn.log_sigmoid(f_logit.astype(jnp.float32) + b_f.astype(jnp.float32))
    cum = jnp.cumsum(log_f, axis=1).transpose(0, 2, 1)
    scale = FOX_HEAD_DIM ** -0.5

    def scores(q0, q1):
        sc = jnp.einsum('bqhd,bkhd->bhqk', q[:, q0:q1], k[:, :q1]).astype(jnp.float32) * scale
        return sc + cum[:, :, q0:q1, None] - cum[:, :, None, :q1]

    o = causal_block_attention(scores, v, chunk_causal=False)
    return o.reshape(b, s, hd) @ w_o

def second_inputs(seed: int = 0) -> dict:
    key = jax.random.key(seed)
    ks = jax.random.split(key, 20)
    f32 = jnp.float32

    def dense(k, shape, fan_in):
        return jax.random.normal(k, shape, f32) * (fan_in ** -0.5)

    def gain(k, shape):
        return 1.0 + 0.05 * jax.random.normal(k, shape, f32)

    x = jax.random.normal(ks[0], (BATCH, SEQ, D_MODEL), f32)
    p = jax.random.normal(ks[1], (DEPTH, BATCH, SEQ, PLE_DIM), f32)
    offset = jax.random.randint(ks[2], (BATCH, 1), 0, 4096, dtype=jnp.int32)
    positions = (offset + jnp.arange(SEQ, dtype=jnp.int32)[None, :]).astype(jnp.int32)

    ffn_norm = gain(ks[3], (DEPTH, 2, D_MODEL))
    ffn_w_in = dense(ks[4], (DEPTH, 2, D_MODEL, 2 * D_FF), D_MODEL)
    ffn_w_out = dense(ks[5], (DEPTH, 2, D_FF, D_MODEL), D_FF)
    mix_norm = gain(ks[6], (DEPTH, D_MODEL))

    mla_w_down = dense(ks[7], (N_MLA_LAYERS, D_MODEL, MLA_Q_LORA + MLA_KV_LORA + MLA_ROPE), D_MODEL)
    mla_q_norm = gain(ks[8], (N_MLA_LAYERS, MLA_Q_LORA))
    mla_w_uq = dense(ks[9], (N_MLA_LAYERS, MLA_Q_LORA, MLA_HEADS * (MLA_NOPE + MLA_ROPE)), MLA_Q_LORA)
    mla_kv_norm = gain(ks[10], (N_MLA_LAYERS, MLA_KV_LORA))
    mla_w_ukv = dense(ks[11], (N_MLA_LAYERS, MLA_KV_LORA, MLA_HEADS * (MLA_NOPE + MLA_V)), MLA_KV_LORA)
    mla_w_o = dense(ks[12], (N_MLA_LAYERS, MLA_HEADS * MLA_V, D_MODEL), MLA_HEADS * MLA_V)

    fox_hd = FOX_HEADS * FOX_HEAD_DIM
    fox_w_in = dense(ks[13], (N_FOX_LAYERS, D_MODEL, 3 * fox_hd + FOX_HEADS), D_MODEL)
    fox_w_in = fox_w_in.at[..., 3 * fox_hd:].multiply(0.1)
    fox_b_f = jax.random.uniform(ks[14], (N_FOX_LAYERS, FOX_HEADS), f32, minval=1.0, maxval=6.0)
    fox_w_o = dense(ks[15], (N_FOX_LAYERS, fox_hd, D_MODEL), fox_hd)

    ple_norm = gain(ks[16], (DEPTH, D_MODEL))
    ple_w_gate = dense(ks[17], (DEPTH, D_MODEL, D_MODEL), D_MODEL)
    ple_w_proj = dense(ks[18], (DEPTH, PLE_DIM, D_MODEL), PLE_DIM)
    final_norm = gain(ks[19], (D_MODEL,))

    return {"x": x, "p": p, "positions": positions,
            "ffn_norm": ffn_norm, "ffn_w_in": ffn_w_in, "ffn_w_out": ffn_w_out,
            "mix_norm": mix_norm,
            "mla_w_down": mla_w_down, "mla_q_norm": mla_q_norm, "mla_w_uq": mla_w_uq,
            "mla_kv_norm": mla_kv_norm, "mla_w_ukv": mla_w_ukv, "mla_w_o": mla_w_o,
            "fox_w_in": fox_w_in, "fox_b_f": fox_b_f, "fox_w_o": fox_w_o,
            "ple_norm": ple_norm, "ple_w_gate": ple_w_gate, "ple_w_proj": ple_w_proj,
            "final_norm": final_norm}

def second_block(x, p, positions, ffn_norm, ffn_w_in, ffn_w_out, mix_norm,
              mla_w_down, mla_q_norm, mla_w_uq, mla_kv_norm, mla_w_ukv, mla_w_o,
              fox_w_in, fox_b_f, fox_w_o, ple_norm, ple_w_gate, ple_w_proj, final_norm):
    inv_freq = ROPE_THETA_2 ** (-jnp.arange(0, MLA_ROPE, 2, dtype=jnp.float32) / MLA_ROPE)
    ang = positions.astype(jnp.float32)[..., None] * inv_freq
    cos = jnp.cos(ang).astype(x.dtype)
    sin = jnp.sin(ang).astype(x.dtype)

    h = x
    for i in range(DEPTH):
        h = h + 0.5 * swiglu(rms_norm(h, ffn_norm[i, 0]), ffn_w_in[i, 0], ffn_w_out[i, 0])
        u = rms_norm(h, mix_norm[i])
        j = i // N_MIXERS
        if i % N_MIXERS == 0:
            h = h + mla_mixer(u, cos, sin, mla_w_down[j], mla_q_norm[j], mla_w_uq[j],
                              mla_kv_norm[j], mla_w_ukv[j], mla_w_o[j])
        else:
            h = h + fox_mixer(u, fox_w_in[j], fox_b_f[j], fox_w_o[j])
        h = h + 0.5 * swiglu(rms_norm(h, ffn_norm[i, 1]), ffn_w_in[i, 1], ffn_w_out[i, 1])
        gate = jax.nn.sigmoid(rms_norm(h, ple_norm[i]) @ ple_w_gate[i])
        h = h + gate * (p[i] @ ple_w_proj[i])
    return rms_norm(h, final_norm)


D_FF_3 = 2816
FFN_RES_WEIGHT = 0.5
ATT_HEADS = 8
ATT_HEAD_DIM = 64
ATT_WIDTH = ATT_HEADS * ATT_HEAD_DIM
KV_DIM = ATT_HEAD_DIM
IDX_HEADS = 8
IDX_DIM = 32
TOPK_MAX = 256
SC_WIDTH = D_MODEL - ATT_WIDTH
SC_GROUPS = 8
SC_KERNEL = 3
CONF_WIDTH = D_MODEL
CONF_KERNEL = 31
ROT_FRACTION = 4

HYB_SPLIT_SIZES = (ATT_WIDTH, KV_DIM, KV_DIM, IDX_HEADS * IDX_DIM, IDX_DIM, IDX_HEADS,
                   SC_WIDTH, SC_WIDTH, SC_WIDTH)
HYB_COLS = ATT_WIDTH + 2 * KV_DIM + IDX_HEADS * IDX_DIM + IDX_DIM + IDX_HEADS + 3 * SC_WIDTH


def rms_norm_3(x, g):
    xf = x.astype(jnp.float32)
    y = xf * lax.rsqrt(jnp.mean(xf * xf, axis=-1, keepdims=True) + NORM_EPS)
    return (y * g.astype(jnp.float32)).astype(x.dtype)

def layer_norm_3(x, g, b):
    xf = x.astype(jnp.float32)
    mu = jnp.mean(xf, axis=-1, keepdims=True)
    xc = xf - mu
    var = jnp.mean(xc * xc, axis=-1, keepdims=True)
    y = xc * lax.rsqrt(var + NORM_EPS) * g.astype(jnp.float32) + b.astype(jnp.float32)
    return y.astype(x.dtype)

def half_step_swiglu(h, g, w_gate, w_up, w_down):
    hn = rms_norm_3(h, g)
    return h + FFN_RES_WEIGHT * ((jax.nn.silu(hn @ w_gate) * (hn @ w_up)) @ w_down)

def rope_tables(seq, rot_dim):
    half = rot_dim // 2
    inv_freq = ROPE_THETA ** (-jnp.arange(half, dtype=jnp.float32) / half)
    ang = jnp.arange(seq, dtype=jnp.float32)[:, None] * inv_freq[None, :]
    return jnp.cos(ang), jnp.sin(ang)

def partial_rope(x, cos, sin):
    half = cos.shape[-1]
    shape = (1, cos.shape[0]) + (1,) * (x.ndim - 3) + (half,)
    c = cos.reshape(shape).astype(x.dtype)
    s = sin.reshape(shape).astype(x.dtype)
    x1 = x[..., :half]
    x2 = x[..., half:2 * half]
    return jnp.concatenate([x1 * c - x2 * s, x2 * c + x1 * s, x[..., 2 * half:]], axis=-1)

def causal_depthwise_conv(x, w):
    k, c = w.shape
    return lax.conv_general_dilated(
        x, w[:, None, :].astype(x.dtype), window_strides=(1,), padding=[(k - 1, 0)],
        dimension_numbers=('NWC', 'WIO', 'NWC'), feature_group_count=c)

def dsa_sparse_attention(q, k, v, q_idx, k_idx, w_idx):
    b, s, n_heads, dh = q.shape
    topk = min(TOPK_MAX, s // 4)
    n_blk = s // Q_BLOCK
    key_pos = jnp.arange(s)
    k_idx_f = k_idx.astype(jnp.float32)

    def to_blocks(a):
        return a.reshape((b, n_blk, Q_BLOCK) + a.shape[2:]).swapaxes(0, 1)

    def block(args):
        start, qb, qib, wib = args
        q_pos = start + jnp.arange(Q_BLOCK)
        dots = jnp.einsum('bqhd,bkd->bqhk', qib.astype(jnp.float32), k_idx_f) * (IDX_DIM ** -0.5)
        score = jnp.einsum('bqh,bqhk->bqk', wib.astype(jnp.float32), jax.nn.relu(dots))
        causal = key_pos[None, :] <= q_pos[:, None]
        score = jnp.where(causal[None], score, -jnp.inf)
        _, sel = lax.top_k(score, topk)
        valid = sel <= q_pos[None, :, None]
        k_sel = jax.vmap(lambda kk, ii: kk[ii])(k, sel)
        v_sel = jax.vmap(lambda vv, ii: vv[ii])(v, sel)
        logits = jnp.einsum('bqhd,bqkd->bqhk', qb, k_sel).astype(jnp.float32) * (dh ** -0.5)
        logits = jnp.where(valid[:, :, None, :], logits, -jnp.inf)
        p = jax.nn.softmax(logits, axis=-1).astype(v.dtype)
        return jnp.einsum('bqhk,bqkd->bqhd', p, v_sel)

    starts = jnp.arange(n_blk) * Q_BLOCK
    out = lax.map(block, (starts, to_blocks(q), to_blocks(q_idx), to_blocks(w_idx)))
    return out.swapaxes(0, 1).reshape(b, s, n_heads, dh)

def hybrid_dsa_shortconv_mixer(hn, w_in, conv_w, w_out, cos_a, sin_a, cos_i, sin_i):
    b, s, _ = hn.shape
    z = hn @ w_in
    offsets = []
    acc = 0
    for size in HYB_SPLIT_SIZES[:-1]:
        acc += size
        offsets.append(acc)
    q, k, v, qi, ki, wi, gate_b, gate_c, u = jnp.split(z, offsets, axis=-1)
    q = partial_rope(q.reshape(b, s, ATT_HEADS, ATT_HEAD_DIM), cos_a, sin_a)
    k = partial_rope(k, cos_a, sin_a)
    qi = partial_rope(qi.reshape(b, s, IDX_HEADS, IDX_DIM), cos_i, sin_i)
    ki = partial_rope(ki, cos_i, sin_i)
    wi = wi * (IDX_HEADS ** -0.5)
    y_attn = dsa_sparse_attention(q, k, v, qi, ki, wi).reshape(b, s, ATT_WIDTH)
    y_conv = gate_b * causal_depthwise_conv(gate_c * u, conv_w)
    return jnp.concatenate([y_attn, y_conv], axis=-1) @ w_out

def conformer_conv_module(hn, w_pw1, b_pw1, conv_w, conv_b, ln_g, ln_b, w_pw2, b_pw2):
    a, gate = jnp.split(hn @ w_pw1 + b_pw1, 2, axis=-1)
    u = a * jax.nn.sigmoid(gate)
    u = causal_depthwise_conv(u, conv_w) + conv_b
    u = jax.nn.silu(layer_norm_3(u, ln_g, ln_b))
    return u @ w_pw2 + b_pw2

def third_inputs(seed: int = 0) -> dict:
    key = jax.random.key(seed)
    ks = jax.random.split(key, 20)
    n_even = (DEPTH + 1) // 2
    n_odd = DEPTH // 2
    f32 = jnp.float32

    def nrm(k, shape, scale):
        return jax.random.normal(k, shape, f32) * scale

    return {
        "x": nrm(ks[0], (BATCH, SEQ, D_MODEL), 1.0),
        "ffn_norm": 1.0 + nrm(ks[1], (DEPTH, 2, D_MODEL), 0.02),
        "ffn_w_gate": nrm(ks[2], (DEPTH, 2, D_MODEL, D_FF_3), D_MODEL ** -0.5),
        "ffn_w_up": nrm(ks[3], (DEPTH, 2, D_MODEL, D_FF_3), D_MODEL ** -0.5),
        "ffn_w_down": nrm(ks[4], (DEPTH, 2, D_FF_3, D_MODEL), D_FF_3 ** -0.5),
        "mix_norm": 1.0 + nrm(ks[5], (DEPTH, D_MODEL), 0.02),
        "hyb_w_in": nrm(ks[6], (n_even, D_MODEL, HYB_COLS), D_MODEL ** -0.5),
        "hyb_conv_w": nrm(ks[7], (n_even, SC_KERNEL, SC_WIDTH), SC_KERNEL ** -0.5),
        "hyb_w_out": nrm(ks[8], (n_even, ATT_WIDTH + SC_WIDTH, D_MODEL), (ATT_WIDTH + SC_WIDTH) ** -0.5),
        "conf_w_pw1": nrm(ks[9], (n_odd, D_MODEL, 2 * CONF_WIDTH), D_MODEL ** -0.5),
        "conf_b_pw1": nrm(ks[10], (n_odd, 2 * CONF_WIDTH), 0.02),
        "conf_conv_w": nrm(ks[11], (n_odd, CONF_KERNEL, CONF_WIDTH), CONF_KERNEL ** -0.5),
        "conf_conv_b": nrm(ks[12], (n_odd, CONF_WIDTH), 0.02),
        "conf_ln_g": 1.0 + nrm(ks[13], (n_odd, CONF_WIDTH), 0.02),
        "conf_ln_b": nrm(ks[14], (n_odd, CONF_WIDTH), 0.02),
        "conf_w_pw2": nrm(ks[15], (n_odd, CONF_WIDTH, D_MODEL), CONF_WIDTH ** -0.5),
        "conf_b_pw2": nrm(ks[16], (n_odd, D_MODEL), 0.02),
        "final_norm": 1.0 + nrm(ks[17], (D_MODEL,), 0.02),
    }

def third_block(x, ffn_norm, ffn_w_gate, ffn_w_up, ffn_w_down, mix_norm, hyb_w_in, hyb_conv_w,
              hyb_w_out, conf_w_pw1, conf_b_pw1, conf_conv_w, conf_conv_b, conf_ln_g, conf_ln_b,
              conf_w_pw2, conf_b_pw2, final_norm):
    s = x.shape[1]
    cos_a, sin_a = rope_tables(s, ATT_HEAD_DIM // ROT_FRACTION)
    cos_i, sin_i = rope_tables(s, IDX_DIM // ROT_FRACTION)
    h = x
    for layer in range(DEPTH):
        h = half_step_swiglu(h, ffn_norm[layer, 0], ffn_w_gate[layer, 0], ffn_w_up[layer, 0],
                             ffn_w_down[layer, 0])
        hn = rms_norm_3(h, mix_norm[layer])
        if layer % 2 == 0:
            e = layer // 2
            h = h + hybrid_dsa_shortconv_mixer(hn, hyb_w_in[e], hyb_conv_w[e], hyb_w_out[e],
                                               cos_a, sin_a, cos_i, sin_i)
        else:
            o = layer // 2
            h = h + conformer_conv_module(hn, conf_w_pw1[o], conf_b_pw1[o], conf_conv_w[o],
                                          conf_conv_b[o], conf_ln_g[o], conf_ln_b[o],
                                          conf_w_pw2[o], conf_b_pw2[o])
        h = half_step_swiglu(h, ffn_norm[layer, 1], ffn_w_gate[layer, 1], ffn_w_up[layer, 1],
                             ffn_w_down[layer, 1])
    return rms_norm_3(h, final_norm)


_first_inputs = third_inputs


def third_inputs(seed=0):
    import zlib

    import numpy as np

    out = dict(_first_inputs(seed))
    spreads = {}
    factors = {'ffn_norm': 2.83,
     'conf_b_pw1': 6.225,
     'conf_conv_b': 3.206,
     'conf_ln_g': 5.42,
     'conf_ln_b': 6.749,
     'conf_b_pw2': 4.094,
     'final_norm': 2.873}
    for name, (base, spread) in spreads.items():
        noise = np.random.default_rng([zlib.crc32(name.encode()), seed]).standard_normal(out[name].shape)
        drawn = base * np.exp(spread * noise) if base else spread * noise
        out[name] = __import__('jax').numpy.asarray(drawn.astype(out[name].dtype))
    for name, factor in factors.items():
        out[name] = (out[name] * factor).astype(out[name].dtype)
    return out


_narrow_inputs = third_inputs


def third_inputs(seed=0):

    out = dict(_narrow_inputs(seed))
    wider = {'conf_ln_g': 4.51, 'conf_ln_b': 3.86, 'conf_b_pw2': 4.49, 'final_norm': 3.23}
    for name, times in wider.items():
        mean = out[name].mean()
        out[name] = (mean + times * (out[name] - mean)).astype(out[name].dtype)
    return out


def setup_inputs(seed=0):
    out = dict(first_inputs(seed))
    for name, value in second_inputs(seed + 1).items():
        if name != "x":
            out[name + "_2"] = value
    for name, value in third_inputs(seed + 2).items():
        if name != "x":
            out[name + "_3"] = value
    return out


def reference(
    x, ret_w_in, ret_w_out, kv_w, diff_w_q, diff_lambda, diff_subln_g, diff_w_out, peer_w_q,
    peer_subkeys, peer_u, peer_v, ln_g, ln_b, p_2, positions_2, ffn_norm_2, ffn_w_in_2,
    ffn_w_out_2, mix_norm_2, mla_w_down_2, mla_q_norm_2, mla_w_uq_2, mla_kv_norm_2, mla_w_ukv_2,
    mla_w_o_2, fox_w_in_2, fox_b_f_2, fox_w_o_2, ple_norm_2, ple_w_gate_2, ple_w_proj_2,
    final_norm_2, ffn_norm_3, ffn_w_gate_3, ffn_w_up_3, ffn_w_down_3, mix_norm_3, hyb_w_in_3,
    hyb_conv_w_3, hyb_w_out_3, conf_w_pw1_3, conf_b_pw1_3, conf_conv_w_3, conf_conv_b_3,
    conf_ln_g_3, conf_ln_b_3, conf_w_pw2_3, conf_b_pw2_3, final_norm_3,
):
    x = first_block(
        x, ret_w_in, ret_w_out, kv_w, diff_w_q, diff_lambda, diff_subln_g, diff_w_out, peer_w_q,
        peer_subkeys, peer_u, peer_v, ln_g, ln_b,
    )
    x = second_block(
        x, p_2, positions_2, ffn_norm_2, ffn_w_in_2, ffn_w_out_2, mix_norm_2, mla_w_down_2,
        mla_q_norm_2, mla_w_uq_2, mla_kv_norm_2, mla_w_ukv_2, mla_w_o_2, fox_w_in_2, fox_b_f_2,
        fox_w_o_2, ple_norm_2, ple_w_gate_2, ple_w_proj_2, final_norm_2,
    )
    return third_block(
        x, ffn_norm_3, ffn_w_gate_3, ffn_w_up_3, ffn_w_down_3, mix_norm_3, hyb_w_in_3,
        hyb_conv_w_3, hyb_w_out_3, conf_w_pw1_3, conf_b_pw1_3, conf_conv_w_3, conf_conv_b_3,
        conf_ln_g_3, conf_ln_b_3, conf_w_pw2_3, conf_b_pw2_3, final_norm_3,
    )


_drawn_inputs = setup_inputs


def setup_inputs(seed=0):
    import zlib

    import numpy as np

    out = dict(_drawn_inputs(seed))
    spreads = {}
    factors = {'diff_subln_g': 3.03,
     'mla_q_norm_2': 3.38,
     'mix_norm_3': 2.704,
     'conf_b_pw1_3': 3.858,
     'conf_conv_b_3': 4.665}
    for name, (base, spread) in spreads.items():
        noise = np.random.default_rng([zlib.crc32(name.encode()), seed]).standard_normal(out[name].shape)
        drawn = base * np.exp(spread * noise) if base else spread * noise
        out[name] = __import__('jax').numpy.asarray(drawn.astype(out[name].dtype))
    for name, factor in factors.items():
        out[name] = (out[name] * factor).astype(out[name].dtype)
    return out
```

```python
import math
from contextlib import ExitStack

import numpy as np

import concourse.bass as bass
from concourse import mybir

P = 128
SEQ = 256
TT = SEQ // P
D = 1024
KD = D // P
RING = 4
HIGHS = 3
LOWS = 2
PERIOD = 12
UNIT = 1024
PIECE = 512
D_FF = 2816
N_KEYS = 128
TOPK = 16
PEER_HEADS = 8
DSA_TOPK = 64
NEG = -1.0e30
MARK = -3.0e38
DN_ALPHA = 4.0 ** 0.25
LAM_INIT = 0.8 - 0.6 * math.exp(-0.3)
F32 = mybir.dt.float32
F32R = mybir.dt.float32r
U32 = mybir.dt.uint32
I32 = mybir.dt.int32
ACT = mybir.ActivationFunctionType
ALU = mybir.AluOpType
AX = mybir.AxisListType.X



def constant_tables():
    f32 = np.float32
    t = {}
    ar = np.arange(P)
    t["ident"] = np.eye(P)
    t["iota"] = np.broadcast_to(ar, (P, P))
    causal = np.where(ar[None, :] <= ar[:, None], 0.0, NEG)
    chunked = np.where(ar[None, :] // 64 <= ar[:, None] // 64, 0.0, NEG)
    zero = np.zeros((P, P))
    t["causal"] = np.concatenate([causal, zero, causal], 1)
    t["chunked"] = np.concatenate([chunked, zero, chunked], 1)
    log_g = np.log(f32(1.0) - np.exp2(f32(-5.0) - np.arange(4, dtype=f32))).astype(f32)
    rel = (ar[None, :] - ar[:, None]).astype(f32)
    same = [np.where(rel >= 0, np.exp(np.maximum(rel, 0) * g), 0.0) for g in log_g]
    past = [np.exp((rel + P) * g) for g in log_g]
    t["decay"] = np.concatenate([np.concatenate([s, q, s], 1) for s, q in zip(same, past)], 1) / 16.0
    t["upper"] = np.where(ar[:, None] <= ar[None, :], 1.0, 0.0)
    t["ones"] = np.ones((P, P))

    def rotation(name, freqs):
        pos = np.arange(SEQ, dtype=f32)
        ang = (pos[:, None] * freqs[None, :].astype(f32)).astype(f32).astype(np.float64)
        for kind, fn in (("cos", np.cos), ("sin", np.sin)):
            t[kind + name] = fn(ang).reshape(TT, P, -1).transpose(1, 0, 2).reshape(P, -1)

    rotation("_ret", f32(1.0) / (f32(10000.0) ** np.linspace(0.0, 1.0, 128, dtype=f32)))
    rotation("_att", f32(500000.0) ** (-np.arange(8, dtype=f32) / f32(8)))
    rotation("_idx", f32(500000.0) ** (-np.arange(4, dtype=f32) / f32(4)))
    t["inv_freq"] = np.broadcast_to(f32(10000.0) ** (-np.arange(0, 64, 2, dtype=f32) / f32(64)), (P, 32))
    return {k: np.ascontiguousarray(v, dtype=f32) for k, v in t.items()}


RESIDENT = ("ident", "iota", "causal", "upper", "ones", "cos_att", "sin_att", "cos_idx", "sin_idx", "inv_freq")
FETCHED = ("cos_ret", "sin_ret", "decay", "chunked")


COLUMNS = {"subln": 1, "ffn_norm_2": 32, "mix_norm_2": 16, "mla_norms": 3, "ple_norm": 16, "ffn_norm_3": 32,
           "mix_norm_3": 16, "hyb_conv": 12, "b_pw1": 16, "conf_conv": 248, "conf_conv_b": 8,
           "conf_ln_g": 8, "conf_ln_b": 8}
ROWS = {"ln_g": 0, "ln_b": 4, "final_2": 8, "final_3": 9, "b_pw2": 10, "lambda": 11, "b_f": 12}
N_ROWS = 13


class Counter:

    def __init__(self, sem):
        self.sem = sem
        self.planned = 0

    def reserve(self, n):
        base = self.planned
        self.planned += n
        return base


class Own:

    def __init__(self, eng, sem):
        self.eng, self.sem, self.n = eng, sem, 0

    def step(self, ins):
        ins.then_inc(self.sem, 1)
        self.n += 1
        return self.n

    def settle(self, n=None):
        self.eng.wait_ge(self.sem, self.n if n is None else n)


class Core:

    def __init__(self, nc, ctx, dram):
        self.nc, self.ctx, self.dram = nc, ctx, dram
        self.units = 0
        self.stages = []
        self.counters = {}

        def sb(name, shape, dt=F32):
            return ctx.enter_context(nc.sbuf_tensor(name, shape, dt))

        self.x = sb("x", [P, TT, D])
        self.xT = (sb("xT_high", [P, KD, SEQ], F32R), sb("xT_low", [P, KD, SEQ], F32R))
        self.ring = sb("ring", [P, RING, UNIT])
        self.high = sb("high", [P, HIGHS, UNIT], F32R)
        self.low = sb("low", [P, LOWS, UNIT], F32R)
        self.arena = sb("arena", [P, 32768])
        self.scratch = sb("scratch", [P, 3 * SEQ + 512])
        self.tables = {}
        tables = constant_tables()
        tables = {name: tables[name] for name in RESIDENT}
        self.n_const = sum(v.shape[1] for v in tables.values())
        self.const = sb("const", [P, self.n_const])
        at = 0
        for name, v in tables.items():
            self.tables[name] = self.const[:, at:at + v.shape[1]]
            at += v.shape[1]
        self.n_cols = sum(COLUMNS.values())
        self.cols = sb("cols", [P, self.n_cols])
        at = 0
        self.col = {}
        for name, n in COLUMNS.items():
            self.col[name] = self.cols[:, at:at + n]
            at += n
        self.activated = sb("activated", [P, 2, SEQ])
        self.hidden = (sb("hidden_high", [P, 2, SEQ], F32R), sb("hidden_low", [P, 2, SEQ], F32R))
        self.small = sb("small", [P, 256])
        self.stats = sb("stats", [P, 16, 2, 6])
        self.moments = sb("moments", [P, 16, 2])
        self.square = sb("square", [P, 16])
        self.power = sb("power", [P, 16])
        self.root = sb("root", [P, 16])
        self.rstd = sb("rstd", [P, 16])
        self.acc = ctx.enter_context(nc.psum_tensor("acc", [P, TT, 1024], F32))
        self.bank = ctx.enter_context(nc.psum_tensor("bank", [P, 4, 512], F32))
        self.unit_landed = [self.sem(f"unit_landed{s}") for s in range(RING)]
        self.units_rounded = self.sem("units_rounded")
        self.unit_ready = [self.sem(f"unit_ready{s}") for s in range(LOWS)]
        self.units_multiplied = self.sem("units_multiplied")
        self.stage_done = self.sem("stage_done")

    def sem(self, name):
        return self.ctx.enter_context(self.nc.semaphore(name))

    def counter(self, name):
        if name not in self.counters:
            self.counters[name] = Counter(self.sem(name))
        return self.counters[name]

    def at(self, off, *dims):
        n = int(np.prod(dims))
        v = self.arena[:, off:off + n]
        return shaped(v, *dims)

    def rows_at(self, n):
        return self.arena[:, 30720 + n * D:30720 + (n + 1) * D]

    def round_unit(self, act, unit, i=0):
        act.wait_ge(self.unit_landed[unit % RING], i * (16 * PERIOD // RING) + 16 * (unit // RING + 1))
        if unit >= HIGHS:
            act.wait_ge(self.units_multiplied, i * PERIOD + unit - HIGHS + 1)
        act.activation(self.high[:, unit % HIGHS, :], self.ring[:, unit % RING, :], ACT.Copy).then_inc(
            self.units_rounded, 1)

    def take_remainder(self, eng, unit, i=0):
        eng.wait_ge(self.units_rounded, i * PERIOD + unit + 1)
        if unit >= LOWS:
            eng.wait_ge(self.units_multiplied, i * PERIOD + unit - LOWS + 1)
        eng.tensor_tensor(self.low[:, unit % LOWS, :], self.ring[:, unit % RING, :],
                          self.high[:, unit % HIGHS, :].bitcast(F32), ALU.subtract).then_inc(
                              self.unit_ready[unit % LOWS], 1)

    def unit_parts(self, unit, lo, hi):
        return self.high[:, unit % HIGHS, lo:hi], self.low[:, unit % LOWS, lo:hi]

    def take_units(self, n):
        u = self.units
        self.units += n
        return u


def shaped(v, *dims):
    names = "abcdef"[:len(dims)]
    if len(dims) == 1:
        return v
    return v.rearrange(f"p ({' '.join(names)}) -> p {' '.join(names)}",
                       **{c: d for c, d in zip(names[1:], dims[1:])})


def spread(v, axis, n):
    names = list("abcdef"[:len(v.shape) - 1])
    before, after = names[:axis - 1], names[axis - 1:]
    if after:
        old = before + [f"(z {after[0]})"] + after[1:]
    else:
        old = before[:-1] + [f"({before[-1]} z)"]
    grown = v.rearrange(f"p {' '.join(old)} -> p {' '.join(before + ['z'] + after)}", z=1)
    shape = list(grown.shape)
    shape[axis] = n
    return grown.to_broadcast(shape)


def parts(pair, *cut):
    return tuple(v[cut] for v in pair)


def product(pe, out, lhsT, rhs, start, stop):
    pe.matmul(out, lhsT[0], rhs[0], start=start, stop=False)
    pe.matmul(out, lhsT[0], rhs[1], start=False, stop=False)
    return pe.matmul(out, lhsT[1], rhs[0], start=False, stop=stop)




class Stage:

    def __init__(self, core):
        self.core = core
        self.index = len(core.stages)
        core.stages.append(self)
        self.plan()

    def plan(self):
        pass

    def enter(self, eng):
        if self.index:
            eng.wait_ge(self.core.stage_done, self.index)

    def tensor(self, pe):
        pass

    def vector(self, dve, own):
        pass

    def scalar(self, act, own):
        pass

    def gpsimd(self, pool, own):
        pass


    def ready(self, pe, unit, i=0):
        pe.wait_ge(self.core.unit_ready[unit % LOWS], i * (PERIOD // LOWS) + unit // LOWS + 1)


    def round_next(self, act, n, i=0):
        self.core.round_unit(act, n + HIGHS, i)

    def remainder_next(self, dve, n, i=0):
        self.core.take_remainder(dve, n + LOWS, i)

    def weights_end(self):
        return self.unit0 + self.unit_count

    def last_remainders(self, pool, first):
        for unit in range(first, self.weights_end() + LOWS):
            self.core.take_remainder(pool, unit)


class Load(Stage):

    def scalar(self, act, own):
        c = self.core
        loaded = c.sem("inputs_loaded")
        act.dma_start(c.x[:, :, :], c.dram["x"].rearrange("(t p) d -> p t d", p=P)).then_inc(loaded, 16)
        act.dma_start(c.const[:, :], c.dram["const"]).then_inc(loaded, 16)
        act.dma_start(c.cols[:, :], c.dram["cols"]).then_inc(loaded, 16)
        act.wait_ge(loaded, 48)
        act.activation(c.small[:, 1:2], c.const[:, 0:1], ACT.Copy).then_inc(c.stage_done, 1)
        for unit in range(HIGHS):
            c.round_unit(act, unit)

    def gpsimd(self, pool, own):
        for unit in range(LOWS):
            self.core.take_remainder(pool, unit)


class Fetch(Stage):

    def __init__(self, core, dst, src):
        self.dst, self.src = dst, src
        super().__init__(core)

    def plan(self):
        self.loaded = self.core.counter("fetched")
        self.loaded0 = self.loaded.reserve(16)

    def gpsimd(self, pool, own):
        self.enter(pool)
        pool.dma_start(self.dst, self.src).then_inc(self.loaded.sem, 16)

    def vector(self, dve, own):
        self.enter(dve)
        dve.wait_ge(self.loaded.sem, self.loaded0 + 16)
        dve.tensor_copy(self.core.small[:, 0:1], self.core.const[:, 0:1]).then_inc(self.core.stage_done, 1)


class Transpose(Stage):

    def __init__(self, core, src, dst, chunks, gain=None):
        self.src, self.dst, self.chunks, self.gain = src, dst, chunks, gain
        super().__init__(core)

    def plan(self):
        self.groups = [(t, c0, min(4, self.chunks - c0)) for t in range(TT) for c0 in range(0, self.chunks, 4)]
        self.turned = self.core.counter("tile_transposed")
        self.turned0 = self.turned.reserve(len(self.groups))
        self.plan_copies()

    def plan_copies(self):
        self.copied = self.core.counter("transpose_copied")
        self.copied0 = self.copied.reserve(len(self.groups) - 1)

    def tensor(self, pe):
        c = self.core
        self.enter(pe)
        for g, (t, c0, n) in enumerate(self.groups):
            if g >= 4:
                pe.wait_ge(self.copied.sem, self.copied0 + g - 3)
            for k in range(n):
                last = pe.transpose(c.bank[:, g % 4, k * P:(k + 1) * P],
                                    self.src[:, t, (c0 + k) * P:(c0 + k + 1) * P], c.tables["ident"])
            last.then_inc(self.turned.sem, 1)

    def vector(self, dve, own):
        c = self.core
        self.enter(dve)
        for g, (t, c0, n) in enumerate(self.groups):
            dve.wait_ge(self.turned.sem, self.turned0 + g + 1)
            out = self.dst[:, c0:c0 + n, t * P:(t + 1) * P]
            got = shaped(c.bank[:, g % 4, 0:n * P], n, P)
            if self.gain is None:
                last = dve.tensor_copy(out, got)
            else:
                last = dve.tensor_tensor(out, got, spread(self.gain[:, c0:c0 + n], 2, P), ALU.mult)
            final = g == len(self.groups) - 1
            last.then_inc(c.stage_done if final else self.copied.sem, 1)


class TransposeSplit(Transpose):

    def __init__(self, core, src, chunks=KD, gain=None, at=0, held=28672):
        self.held = core.at(held, 4, 512)
        super().__init__(core, src, parts(core.xT, slice(None), slice(at, at + chunks)), chunks, gain)

    def plan(self):
        super().plan()
        n = len(self.groups)
        self.gained = self.core.counter("transpose_gained")
        self.gained0 = self.gained.reserve(n if self.gain is not None else 0)
        self.rounded = self.core.counter("transpose_rounded")
        self.rounded0 = self.rounded.reserve(n)

    def value(self, g):
        n = self.groups[g][2]
        if self.gain is None:
            return shaped(self.core.bank[:, g % 4, 0:n * P], n, P)
        return shaped(self.held[:, g % 4, 0:n * P], n, P)

    def out(self, g, part):
        t, c0, n = self.groups[g]
        return self.dst[part][:, c0:c0 + n, t * P:(t + 1) * P]

    def scalar(self, act, own):
        self.enter(act)
        for g in range(len(self.groups)):
            if self.gain is None:
                act.wait_ge(self.turned.sem, self.turned0 + g + 1)
            else:
                act.wait_ge(self.gained.sem, self.gained0 + g + 1)
            act.activation(self.out(g, 0), self.value(g), ACT.Copy).then_inc(self.rounded.sem, 1)

    def vector(self, dve, own):
        c, count = self.core, len(self.groups)
        self.enter(dve)

        def apply_gain(g):
            _, c0, n = self.groups[g]
            dve.wait_ge(self.turned.sem, self.turned0 + g + 1)
            dve.tensor_tensor(self.value(g), shaped(c.bank[:, g % 4, 0:n * P], n, P),
                              spread(self.gain[:, c0:c0 + n], 2, P), ALU.mult).then_inc(self.gained.sem, 1)

        if self.gain is not None:
            apply_gain(0)
        for g in range(count):
            if self.gain is not None and g + 1 < count:
                apply_gain(g + 1)
            dve.wait_ge(self.rounded.sem, self.rounded0 + g + 1)
            dve.tensor_tensor(self.out(g, 1), self.value(g), self.out(g, 0).bitcast(F32), ALU.subtract).then_inc(
                c.stage_done if g == count - 1 else self.copied.sem, 1)


class SplitOperand(Stage):

    def __init__(self, core, src, at):
        self.src, self.dst = src, parts(core.xT, slice(None), slice(at, at + src.shape[1]))
        super().__init__(core)

    def plan(self):
        self.rounded = self.core.counter("operand_rounded")
        self.rounded0 = self.rounded.reserve(1)

    def scalar(self, act, own):
        self.enter(act)
        act.activation(self.dst[0], self.src, ACT.Copy).then_inc(self.rounded.sem, 1)

    def vector(self, dve, own):
        self.enter(dve)
        dve.wait_ge(self.rounded.sem, self.rounded0 + 1)
        dve.tensor_tensor(self.dst[1], self.src, self.dst[0].bitcast(F32), ALU.subtract).then_inc(
            self.core.stage_done, 1)


class Norm(Stage):

    def __init__(self, core, entries, kind, eps, rows=()):
        self.entries, self.kind, self.eps, self.rows = entries, kind, eps, rows
        super().__init__(core)

    def plan(self):
        c = self.core
        self.measured = c.counter("moments_ready")
        self.measured0 = self.measured.reserve(1)
        self.rooted = c.counter("root_ready")
        self.rooted0 = self.rooted.reserve(1)
        if self.rows:
            self.rows_in = c.counter("rows_loaded")
            self.rows_in0 = self.rows_in.reserve(16 * len(self.rows))

    def gpsimd(self, pool, own):
        if self.rows:
            self.enter(pool)
            for n, row in enumerate(self.rows):
                src = self.core.dram["rows"][row:row + 1, :].to_broadcast([P, D])
                pool.dma_start(self.core.rows_at(n), src).then_inc(self.rows_in.sem, 16)

    def scalar(self, act, own):
        c, n = self.core, len(self.entries)
        self.enter(act)
        act.wait_ge(self.measured.sem, self.measured0 + 1)
        act.activation(c.root[:, 0:n], c.power[:, 0:n], ACT.Sqrt).then_inc(self.rooted.sem, 1)

    def vector(self, dve, own):
        c, n = self.core, len(self.entries)
        self.enter(dve)
        width = self.entries[0][0].shape[-1]
        for e, (src, _) in enumerate(self.entries):
            width = src.shape[-1]
            for k in range(0, width, 512):
                own.step(dve.bn_stats(c.stats[:, e, k // 512, :], src[:, k:min(k + 512, width)]))
        own.settle()
        for e, (src, _) in enumerate(self.entries):
            parts = -(-src.shape[-1] // 512)
            own.step(dve.bn_aggr(c.moments[:, e, :], shaped(c.stats[:, e, 0:parts, :].rearrange("p a b -> p (a b)"), 6 * parts)))
        own.settle()
        mean, var = c.moments[:, 0:n, 0], c.moments[:, 0:n, 1]
        if self.kind == "rms":
            own.step(dve.tensor_tensor(c.square[:, 0:n], mean, mean, ALU.mult))
            own.settle()
            dve.scalar_tensor_tensor(c.power[:, 0:n], c.square[:, 0:n], self.eps, var,
                                     ALU.add, ALU.add).then_inc(self.measured.sem, 1)
        else:
            dve.tensor_scalar(c.power[:, 0:n], var, self.eps, None, ALU.add).then_inc(self.measured.sem, 1)
        dve.wait_ge(self.rooted.sem, self.rooted0 + 1)
        own.step(dve.reciprocal(c.rstd[:, 0:n], c.root[:, 0:n]))
        own.settle()
        outs = []
        for e, (src, dst) in enumerate(self.entries):
            if self.kind == "rms":
                outs.append((dve.tensor_scalar, (dst, src, c.rstd[:, e:e + 1], None, ALU.mult)))
            else:
                outs.append((dve.tensor_scalar, (dst, src, c.moments[:, e, 0:1], c.rstd[:, e:e + 1],
                                                 ALU.subtract, ALU.mult)))
        if self.rows:
            for fn, args in outs:
                own.step(fn(*args))
            own.settle()
            dve.wait_ge(self.rows_in.sem, self.rows_in0 + 16 * len(self.rows))
            for k in range(len(self.rows)):
                row = c.rows_at(k)
                for e, (_, dst) in enumerate(self.entries):
                    last = dve.tensor_tensor(dst, dst, row, ALU.add if k else ALU.mult)
                    if k < len(self.rows) - 1 or e < n - 1:
                        own.step(last)
                if k < len(self.rows) - 1:
                    own.settle()
            last.then_inc(c.stage_done, 1)
        else:
            for fn, args in outs[:-1]:
                own.step(fn(*args))
            fn, args = outs[-1]
            fn(*args).then_inc(c.stage_done, 1)


class TokenMajor(Stage):

    engine = "scalar"

    def __init__(self, core, lhs, kc, widths):
        self.lhs, self.kc, self.widths = lhs, kc, widths
        super().__init__(core)

    def plan(self):
        c = self.core
        self.blocks = len(self.widths)
        self.unit_count = -(-self.kc * self.blocks // 2)
        self.unit0 = c.take_units(self.unit_count)
        self.freed = c.counter("block_freed")
        self.freed0 = self.freed.reserve(self.blocks - 1)

    def ending(self, unit):
        return [b for b in range(self.blocks) if self.unit0 + (b * self.kc + self.kc - 1) // 2 == unit]

    def tensor(self, pe):
        c = self.core
        self.enter(pe)
        pieces = self.kc * self.blocks
        for b, width in enumerate(self.widths):
            if b >= 2:
                pe.wait_ge(self.freed.sem, self.freed0 + b - 1)
            for k in range(self.kc):
                f = b * self.kc + k
                unit = self.unit0 + f // 2
                if f % 2 == 0:
                    self.ready(pe, unit)
                w = c.unit_parts(unit, (f % 2) * PIECE, (f % 2) * PIECE + width)
                for t in range(TT):
                    mm = product(pe, c.acc[:, t, (b % 2) * PIECE:(b % 2) * PIECE + width],
                                 parts(self.lhs, slice(None), k, slice(t * P, (t + 1) * P)), w,
                                 start=(k == 0), stop=(k == self.kc - 1))
                if f % 2 == 1 or f == pieces - 1:
                    mm.then_inc(c.units_multiplied, 1)

    def evacuate(self, eng, own, b):
        c, width = self.core, self.widths[b]
        for t in range(TT):
            got = c.acc[:, t, (b % 2) * PIECE:(b % 2) * PIECE + width]
            last = self.keep(eng, own, b, t, got)
            if t < TT - 1:
                own.step(last)
        last.then_inc(c.stage_done if b == self.blocks - 1 else self.freed.sem, 1)

    def scalar(self, act, own):
        self.enter(act)
        for unit in range(self.unit0, self.weights_end()):
            if unit < self.weights_end() - 1:
                self.round_next(act, unit)
            if self.engine == "scalar":
                for b in self.ending(unit):
                    act.wait_ge(self.core.units_multiplied, unit + 1)
                    self.evacuate(act, own, b)
        self.round_next(act, self.weights_end() - 1)

    def vector(self, dve, own):
        self.enter(dve)
        for unit in range(self.unit0, self.weights_end()):
            if unit + LOWS < self.weights_end():
                self.remainder_next(dve, unit)
            if self.engine == "vector":
                for b in self.ending(unit):
                    dve.wait_ge(self.core.units_multiplied, unit + 1)
                    self.evacuate(dve, own, b)

    def gpsimd(self, pool, own):
        self.last_remainders(pool, max(self.weights_end(), self.unit0 + LOWS))


class Project(TokenMajor):

    def __init__(self, core, lhs, kc, widths, dst, funcs=None):
        self.dst = dst
        self.funcs = funcs or [ACT.Copy] * len(widths)
        super().__init__(core, lhs, kc, widths)

    def keep(self, act, own, b, t, got):
        return act.activation(self.dst[:, t, b * PIECE:b * PIECE + got.shape[-1]], got, self.funcs[b])


class AddTo(TokenMajor):

    engine = "vector"

    def __init__(self, core, lhs, kc, x_scale=1.0):
        self.x_scale = x_scale
        super().__init__(core, lhs, kc, [PIECE] * (D // PIECE))

    def keep(self, dve, own, b, t, got):
        x = self.core.x[:, t, b * PIECE:(b + 1) * PIECE]
        return dve.scalar_tensor_tensor(x, x, self.x_scale, got, ALU.mult, ALU.add)


class GatedAdd(TokenMajor):

    engine = "vector"

    def __init__(self, core, lhs, kc, gate, product):
        self.gate, self.product = gate, product
        super().__init__(core, lhs, kc, [PIECE] * (D // PIECE))

    def keep(self, dve, own, b, t, got):
        cut = slice(b * PIECE, (b + 1) * PIECE)
        own.step(dve.tensor_tensor(self.product[:, t, cut], got, self.gate[:, t, cut], ALU.mult))
        own.settle()
        x = self.core.x[:, t, cut]
        return dve.tensor_tensor(x, x, self.product[:, t, cut], ALU.add)


class FeatureMajor(Stage):

    def __init__(self, core, rhs, kc, chunks, dst, scales=None):
        self.rhs, self.kc, self.chunks, self.dst = rhs, kc, chunks, dst
        self.scales = scales or [1.0] * chunks
        super().__init__(core)

    def plan(self):
        c = self.core
        self.unit_count = -(-self.kc * self.chunks // 8)
        self.unit0 = c.take_units(self.unit_count)
        self.slots = 4 if self.kc == KD else 8
        assert self.kc == KD or self.chunks <= self.slots
        self.freed = c.counter("chunk_freed")
        self.freed0 = self.freed.reserve(self.chunks - 1)

    def tensor(self, pe):
        c = self.core
        self.enter(pe)
        pieces = self.kc * self.chunks
        for j in range(self.chunks):
            if j >= self.slots:
                pe.wait_ge(self.freed.sem, self.freed0 + j - self.slots + 1)
            for k in range(self.kc):
                f = j * self.kc + k
                unit = self.unit0 + f // 8
                if f % 8 == 0:
                    self.ready(pe, unit)
                mm = product(pe, self.slot(j), c.unit_parts(unit, (f % 8) * P, (f % 8 + 1) * P),
                             parts(self.rhs, slice(None), k), start=(k == 0), stop=(k == self.kc - 1))
                if f % 8 == 7 or f == pieces - 1:
                    mm.then_inc(c.units_multiplied, 1)

    def slot(self, j):
        if self.kc == KD:
            return self.core.bank[:, j % 4, 0:SEQ]
        return self.core.bank[:, j // 2, (j % 2) * SEQ:(j % 2 + 1) * SEQ]

    def last_unit(self, j):
        return self.unit0 + (j * self.kc + self.kc - 1) // 8

    def scalar(self, act, own):
        c = self.core
        self.enter(act)
        for unit in range(self.unit0, self.weights_end()):
            if unit < self.weights_end() - 1:
                self.round_next(act, unit)
            for j in range(self.chunks):
                if self.last_unit(j) == unit:
                    act.wait_ge(c.units_multiplied, unit + 1)
                    act.activation(self.dst[:, j, :], self.slot(j), ACT.Copy, scale=self.scales[j]).then_inc(
                        c.stage_done if j == self.chunks - 1 else self.freed.sem, 1)
        self.round_next(act, self.weights_end() - 1)

    def vector(self, dve, own):
        self.enter(dve)
        for unit in range(self.unit0, self.weights_end() - LOWS):
            self.remainder_next(dve, unit)

    def gpsimd(self, pool, own):
        self.last_remainders(pool, max(self.weights_end(), self.unit0 + LOWS))


class ExpertLoop(Stage):

    def __init__(self, core, chunks, firsts, func, x_scale, out_scale, gates=None):
        self.chunks, self.firsts, self.func = chunks, firsts, func
        self.x_scale, self.out_scale, self.gates = x_scale, out_scale, gates
        super().__init__(core)

    def plan(self):
        c = self.core
        self.per = self.firsts + 1
        self.unit_count = self.per * self.chunks
        self.unit0 = c.take_units(self.unit_count)
        self.body = PERIOD // self.per
        assert (self.chunks - 2) % self.body == 0 and self.body % 2 == 0
        self.activated = c.counter("chunk_activated")
        self.activated0 = self.activated.reserve(self.chunks)
        self.multiplied = c.counter("hidden_multiplied")
        self.multiplied0 = self.multiplied.reserve(self.chunks)
        self.rounded = c.counter("hidden_rounded")
        self.rounded0 = self.rounded.reserve(self.chunks)
        self.hidden = c.counter("hidden_ready")
        self.hidden0 = self.hidden.reserve(self.chunks)

    def first_unit(self, c):
        return self.unit0 + (self.per * c - 1 if c else 0)

    def last_unit(self, c):
        return self.unit0 + self.per * (c + 1) + self.firsts - 1 - (self.firsts if c == self.chunks - 1 else 0)

    def first_bank(self, c, a):
        return self.core.bank[:, (c % 2) * self.firsts + a, 0:SEQ]

    def tensor(self, pe):
        core = self.core
        self.enter(pe)

        def first_products(c, i=0):
            for a in range(self.firsts):
                unit = self.first_unit(c) + a
                self.ready(pe, unit, i)
                for k in range(KD):
                    mm = product(pe, self.first_bank(c, a), core.unit_parts(unit, k * P, (k + 1) * P),
                                 parts(core.xT, slice(None), k), start=(k == 0), stop=(k == KD - 1))
                mm.then_inc(core.units_multiplied, 1)

        def last_product(c, i=0):
            pe.wait_ge(self.hidden.sem, i * self.body + self.hidden0 + c + 1)
            unit = self.last_unit(c)
            self.ready(pe, unit, i)
            for t in range(TT):
                for h in range(2):
                    mm = product(pe, core.acc[:, t, h * PIECE:(h + 1) * PIECE],
                                 parts(core.hidden, slice(None), c % 2, slice(t * P, (t + 1) * P)),
                                 core.unit_parts(unit, h * PIECE, (h + 1) * PIECE),
                                 start=(c == 0), stop=(c == self.chunks - 1))
            mm.then_inc(core.units_multiplied, 1)

        first_products(0)
        first_products(1)
        last_product(0)
        with pe.Fori(0, (self.chunks - 2) // self.body) as i:
            for c in range(1, 1 + self.body):
                first_products(c + 1, i)
                last_product(c, i)
        last_product(self.chunks - 1)

    def scalar(self, act, own):
        core = self.core
        self.enter(act)

        def firsts(c, i=0, steady=True):
            unit = self.first_unit(c)
            self.round_next(act, unit, i)
            act.wait_ge(core.units_multiplied, i * PERIOD + unit + 1)
            if steady:
                act.wait_ge(self.hidden.sem, i * self.body + self.hidden0 + c - 1)
            act.activation(core.activated[:, c % 2, :], self.first_bank(c, 0), self.func).then_inc(self.activated.sem, 1)
            for a in range(1, self.firsts):
                self.round_next(act, unit + a, i)

        firsts(0, steady=False)
        firsts(1, steady=False)
        self.round_next(act, self.last_unit(0))
        with act.Fori(0, (self.chunks - 2) // self.body) as i:
            for c in range(1, 1 + self.body):
                firsts(c + 1, i)
                self.round_next(act, self.last_unit(c), i)
        self.round_next(act, self.last_unit(self.chunks - 1))

    def vector(self, dve, own):
        core = self.core
        self.enter(dve)

        def hide(c, i=0, steady=True):
            unit = self.first_unit(c)
            dve.wait_ge(self.activated.sem, i * self.body + self.activated0 + c + 1)
            if self.gates is None:
                dve.wait_ge(core.units_multiplied, i * PERIOD + unit + 2)
                other = self.first_bank(c, 1)
            else:
                other = self.gates[:, :, bass.ds(i * self.body + c, 1)].rearrange("p t one -> p (t one)")
            value = core.activated[:, c % 2, :]
            dve.tensor_tensor(value, value, other, ALU.mult).then_inc(self.multiplied.sem, 1)
            dve.wait_ge(self.multiplied.sem, i * self.body + self.multiplied0 + c + 1)
            if steady:
                dve.wait_ge(core.units_multiplied, i * PERIOD + self.last_unit(c - 2) + 1)
            high, low = parts(core.hidden, slice(None), c % 2)
            dve.tensor_copy(high, value).then_inc(self.rounded.sem, 1)
            dve.wait_ge(self.rounded.sem, i * self.body + self.rounded0 + c + 1)
            dve.tensor_tensor(low, value, high.bitcast(F32), ALU.subtract).then_inc(self.hidden.sem, 1)

        def firsts(c, i=0, steady=True):
            for a in range(self.firsts):
                self.remainder_next(dve, self.first_unit(c) + a, i)
            hide(c, i, steady)

        firsts(0, steady=False)
        firsts(1, steady=False)
        self.remainder_next(dve, self.last_unit(0))
        with dve.Fori(0, (self.chunks - 2) // self.body) as i:
            for c in range(1, 1 + self.body):
                firsts(c + 1, i)
                self.remainder_next(dve, self.last_unit(c), i)
        dve.wait_ge(core.units_multiplied, self.last_unit(self.chunks - 1) + 1)
        for t in range(TT):
            x = core.x[:, t, :]
            if self.out_scale != 1.0:
                last = dve.scalar_tensor_tensor(x, core.acc[:, t, :], self.out_scale, x, ALU.mult, ALU.add)
            else:
                last = dve.scalar_tensor_tensor(x, x, self.x_scale, core.acc[:, t, :], ALU.mult, ALU.add)
            if t < TT - 1:
                own.step(last)
        last.then_inc(core.stage_done, 1)

    def gpsimd(self, pool, own):
        self.last_remainders(pool, self.weights_end() + 1)


class KeyScores(Stage):

    def __init__(self, core, queries, subkeys, src, scores):
        self.queries, self.subkeys, self.src, self.scores = queries, subkeys, src, scores
        super().__init__(core)

    def plan(self):
        c = self.core
        self.loaded = c.counter("subkeys_loaded")
        self.loaded0 = self.loaded.reserve(16)
        self.scored = c.counter("key_scores_ready")
        self.scored0 = self.scored.reserve(8)
        self.kept = c.counter("key_scores_kept")
        self.kept0 = self.kept.reserve(7)

    def gpsimd(self, pool, own):
        pool.wait_ge(self.core.stage_done, self.index - 1)
        pool.dma_start(self.subkeys, self.src).then_inc(self.loaded.sem, 16)

    def tensor(self, pe):
        c = self.core
        self.enter(pe)
        pe.wait_ge(self.loaded.sem, self.loaded0 + 16)
        for g in range(8):
            t, q = g // 4, g % 4
            if g >= 4:
                pe.wait_ge(self.kept.sem, self.kept0 + g - 3)
            for j in range(4):
                mm = pe.matmul(c.bank[:, q, j * P:(j + 1) * P], self.queries[:, 4 * q + j, t * P:(t + 1) * P],
                               self.subkeys[:, 4 * q + j, :], start=True, stop=True)
            mm.then_inc(self.scored.sem, 1)

    def scalar(self, act, own):
        c = self.core
        self.enter(act)
        for g in range(8):
            t, q = g // 4, g % 4
            act.wait_ge(self.scored.sem, self.scored0 + g + 1)
            act.activation(self.scores[:, t, 4 * q:4 * q + 4, :], shaped(c.bank[:, q, :], 4, P), ACT.Copy).then_inc(
                c.stage_done if g == 7 else self.kept.sem, 1)


class Route(Stage):

    def __init__(self, core, scores, routes, scratch):
        self.scores, self.routes, self.scratch = scores, routes, scratch
        super().__init__(core)

    def plan(self):
        c = self.core
        self.shifted = c.counter("gates_shifted")
        self.shifted0 = self.shifted.reserve(1)
        self.exped = c.counter("gates_exponentiated")
        self.exped0 = self.exped.reserve(1)
        at = self.scratch
        rows, n = 2 * 16, TOPK

        def take(*dims):
            nonlocal at
            v = c.at(at, *dims)
            at += int(np.prod(dims))
            return v

        self.rest = take(rows, P)
        self.best = take(rows, n)
        self.best_at = take(rows, n).bitcast(U32)
        self.keys = take(TT, PEER_HEADS, 2, n)
        self.sums = take(rows // 2, n * n)
        self.sums_rest = take(rows // 2, n * n)
        self.top = take(rows // 2, n)
        self.top_at = take(rows // 2, n).bitcast(U32)
        self.part_at = take(2, rows // 2 * n).bitcast(U32)
        self.part = take(2, rows // 2, n)
        self.shift = take(rows // 2, n)
        self.gate = take(rows // 2, n)
        self.total = take(1, rows // 2)
        self.inverse = take(1, rows // 2)

    def top16(self, dve, own, values, rest, best, best_at, rows):
        for r in range(rows):
            own.step(dve.max(best[:, r, 0:8], values[:, r, :]))
        own.settle()
        for r in range(rows):
            own.step(dve.max_index(best_at[:, r, 0:8], best[:, r, 0:8], values[:, r, :]))
            own.step(dve.match_replace(rest[:, r, :], best[:, r, 0:8], values[:, r, :], MARK))
        own.settle()
        for r in range(rows):
            own.step(dve.max(best[:, r, 8:16], rest[:, r, :]))
        own.settle()
        for r in range(rows):
            own.step(dve.max_index(best_at[:, r, 8:16], best[:, r, 8:16], rest[:, r, :]))
        own.settle()

    def vector(self, dve, own):
        c, n, groups = self.core, TOPK, TT * PEER_HEADS
        self.enter(dve)
        values = self.scores.rearrange("p t h k -> p (t h) k")
        self.top16(dve, own, values, self.rest, self.best, self.best_at, 2 * groups)
        keys = self.keys.rearrange("p t h s n -> p (t h) s n")
        own.step(dve.tensor_copy(keys.rearrange("p g s n -> p (g s n)"), self.best_at.rearrange("p r n -> p (r n)")))
        pair = self.best.rearrange("p (g s) n -> p g s n", s=2)
        sums = self.sums.rearrange("p g (a b) -> p g a b", a=n)
        own.step(dve.tensor_tensor(sums, spread(pair[:, :, 0, :], 3, n), spread(pair[:, :, 1, :], 2, n), ALU.add))
        own.settle()
        self.top16(dve, own, self.sums, self.sums_rest, self.top, self.top_at, groups)
        dve.tensor_tensor(self.shift, self.top, self.top[:, :, 0:1].to_broadcast([P, groups, n]),
                          ALU.subtract).then_inc(self.shifted.sem, 1)
        flat = self.top_at.rearrange("p g n -> p (g n)")
        own.step(dve.tensor_single_scalar(self.part_at[:, 0, :], flat, 4, ALU.logical_shift_right))
        own.step(dve.tensor_single_scalar(self.part_at[:, 1, :], flat, n - 1, ALU.bitwise_and))
        own.settle()
        own.step(dve.tensor_copy(self.part.rearrange("p s g n -> p (s g n)"),
                                 self.part_at.rearrange("p s m -> p (s m)")))
        own.settle()
        hit = self.sums.rearrange("p g (r a) -> p g r a", r=n)
        iota = c.tables["iota"][:, 0:n]
        for s in range(2):
            own.step(dve.tensor_tensor(hit, spread(self.part[:, s, :, :], 3, n),
                                       spread(spread(iota, 1, n), 1, groups), ALU.is_equal))
            own.settle()
            own.step(dve.tensor_tensor(hit, hit, spread(keys[:, :, s, :], 2, n), ALU.mult))
            own.settle()
            for t in range(TT):
                g = slice(t * PEER_HEADS, (t + 1) * PEER_HEADS)
                own.step(dve.tensor_reduce(self.routes[:, t, 1 + s, :].rearrange("p (g r) -> p g r", r=n),
                                           hit[:, g, :, :], AX, ALU.add))
            own.settle()
        dve.wait_ge(self.exped.sem, self.exped0 + 1)
        own.step(dve.tensor_reduce(self.total[:, 0, :], self.gate, AX, ALU.add))
        own.settle()
        own.step(dve.reciprocal(self.inverse[:, 0, :], self.total[:, 0, :]))
        own.settle()
        for t in range(TT):
            g = slice(t * PEER_HEADS, (t + 1) * PEER_HEADS)
            last = dve.tensor_tensor(self.routes[:, t, 0, :].rearrange("p (g r) -> p g r", r=n), self.gate[:, g, :],
                                     spread(self.inverse[:, 0, g], 2, n), ALU.mult)
            if t < TT - 1:
                own.step(last)
        last.then_inc(c.stage_done, 1)

    def scalar(self, act, own):
        self.enter(act)
        act.wait_ge(self.shifted.sem, self.shifted0 + 1)
        act.activation(self.gate, self.shift, ACT.Exp).then_inc(self.exped.sem, 1)


class SpreadGates(Stage):

    def __init__(self, core, routesT, onehots, gates):
        self.routesT, self.onehots, self.gates = routesT, onehots, gates
        super().__init__(core)

    def plan(self):
        c = self.core
        self.ready = c.counter("onehots_ready")
        self.ready0 = self.ready.reserve(SEQ)
        self.placed = c.counter("tokens_placed")
        self.placed0 = self.placed.reserve(SEQ)
        self.kept = c.counter("gates_kept")
        self.kept0 = self.kept.reserve(SEQ // 4 - 1)

    def vector(self, dve, own):
        c = self.core
        self.enter(dve)
        iota = c.tables["iota"]

        def token(t, i=0, steady=True):
            at = i * 8 + t
            if steady:
                dve.wait_ge(self.placed.sem, i * 8 + self.placed0 + t - 3)
            first, second = self.onehots[t % 4]
            dve.tensor_scalar(first, iota, self.routesT[:, 1, bass.ds(at, 1)], self.routesT[:, 0, bass.ds(at, 1)],
                              ALU.is_equal, ALU.mult)
            dve.tensor_scalar(second, iota, self.routesT[:, 2, bass.ds(at, 1)], None,
                              ALU.is_equal).then_inc(self.ready.sem, 1)

        for t in range(8):
            token(t, steady=t >= 4)
        with dve.Fori(0, SEQ // 8 - 1) as i:
            for t in range(8, 16):
                token(t, i)

    def tensor(self, pe):
        c = self.core
        self.enter(pe)

        def token(t, i=0, steady=True):
            if steady and t % 4 == 0:
                pe.wait_ge(self.kept.sem, i * 2 + self.kept0 + t // 4 - 1)
            pe.wait_ge(self.ready.sem, i * 8 + self.ready0 + t + 1)
            first, second = self.onehots[t % 4]
            pe.matmul(c.bank[:, t // 4 % 2, t % 4 * P:(t % 4 + 1) * P], first, second,
                      start=True, stop=True).then_inc(self.placed.sem, 1)

        for t in range(8):
            token(t, steady=False)
        with pe.Fori(0, SEQ // 8 - 1) as i:
            for t in range(8, 16):
                token(t, i)

    def scalar(self, act, own):
        c = self.core
        self.enter(act)

        def keep(g, i, at, sem):
            act.wait_ge(self.placed.sem, i * 8 + self.placed0 + 4 * g + 4)
            act.activation(self.gates[:, bass.ds(at, 4), :], shaped(c.bank[:, g % 2, :], 4, P), ACT.Copy).then_inc(sem, 1)

        with act.Fori(0, SEQ // 8 - 1) as i:
            keep(0, i, i * 8, self.kept.sem)
            keep(1, i, i * 8 + 4, self.kept.sem)
        keep(SEQ // 4 - 2, 0, SEQ - 8, self.kept.sem)
        keep(SEQ // 4 - 1, 0, SEQ - 4, c.stage_done)


class Rotate(Stage):

    def __init__(self, core, views, r, cos, sin, products, split=None):
        self.views, self.r, self.cos, self.sin, self.products = views, r, cos, sin, products
        super().__init__(core)

    def plan(self):
        self.turned = self.core.counter("second_tile_rotated")
        self.turned0 = self.turned.reserve(1)

    def part(self, eng, own, t, at):
        r = self.r
        done = []
        for view in self.views:
            heads = view.shape[2]
            one, two = view[:, t, :, 0:r], view[:, t, :, r:2 * r]
            cos, sin = spread(self.cos[:, t, :], 1, heads), spread(self.sin[:, t, :], 1, heads)
            held = []
            for a, b in ((one, cos), (two, sin), (one, sin), (two, cos)):
                held.append(self.core.at(at, heads, r))
                at += heads * r
                own.step(eng.tensor_tensor(held[-1], a, b, ALU.mult))
            done += [(one, held[0], held[1], ALU.subtract), (two, held[2], held[3], ALU.add)]
        own.settle()
        for args in done[:-1]:
            own.step(eng.tensor_tensor(*args))
        return eng.tensor_tensor(*done[-1])

    def gpsimd(self, pool, own):
        self.enter(pool)
        size = sum(4 * v.shape[2] * self.r for v in self.views)
        self.part(pool, own, 1, self.products + size).then_inc(self.turned.sem, 1)

    def vector(self, dve, own):
        self.enter(dve)
        own.step(self.part(dve, own, 0, self.products))
        dve.wait_ge(self.turned.sem, self.turned0 + 1)
        dve.tensor_copy(self.core.small[:, 0:1], self.core.const[:, 0:1]).then_inc(self.core.stage_done, 1)


class RetentionScores(Stage):

    HEADS, VD = 4, 512

    def __init__(self, core, qT, kT, v, decay, y, held):
        self.qT, self.kT, self.v, self.decay, self.y, self.held = qT, kT, v, decay, y, held
        super().__init__(core)

    def plan(self):
        c = self.core
        self.scored = c.counter("head_scored")
        self.scored0 = self.scored.reserve(self.HEADS)
        self.decayed = c.counter("head_decayed")
        self.decayed0 = self.decayed.reserve(self.HEADS)
        self.mixed = c.counter("head_mixed")
        self.mixed0 = self.mixed.reserve(self.HEADS)
        self.kept = c.counter("head_kept")
        self.kept0 = self.kept.reserve(self.HEADS - 1)

    BLOCKS = ((0, 0), (0, 1), (1, 1))

    def tensor(self, pe):
        c = self.core
        self.enter(pe)

        def score(h):
            if h >= 2:
                pe.wait_ge(self.decayed.sem, self.decayed0 + h - 1)
            for n, (j, i) in enumerate(self.BLOCKS):
                for k in range(2):
                    mm = pe.matmul(c.bank[:, h % 2, n * P:(n + 1) * P], self.kT[:, 2 * h + k, j * P:(j + 1) * P],
                                   self.qT[:, 2 * h + k, i * P:(i + 1) * P], start=(k == 0), stop=(k == 1))
            mm.then_inc(self.scored.sem, 1)

        def mix(h):
            pe.wait_ge(self.decayed.sem, self.decayed0 + h + 1)
            if h >= 1:
                pe.wait_ge(self.kept.sem, self.kept0 + h)
            for n, (j, i) in enumerate(self.BLOCKS):
                mm = pe.matmul(c.bank[:, 2 + i, :], self.held[:, h % 2, n * P:(n + 1) * P],
                               self.v[:, j, h * self.VD:(h + 1) * self.VD], start=(j == 0), stop=(j == i))
            mm.then_inc(self.mixed.sem, 1)

        score(0)
        for h in range(self.HEADS):
            if h + 1 < self.HEADS:
                score(h + 1)
            mix(h)

    def vector(self, dve, own):
        c = self.core
        self.enter(dve)
        for h in range(self.HEADS):
            dve.wait_ge(self.scored.sem, self.scored0 + h + 1)
            if h >= 2:
                dve.wait_ge(self.mixed.sem, self.mixed0 + h - 1)
            dve.tensor_tensor(self.held[:, h % 2, :], c.bank[:, h % 2, 0:3 * P],
                              self.decay[:, h * 3 * P:(h + 1) * 3 * P], ALU.mult).then_inc(self.decayed.sem, 1)

    def scalar(self, act, own):
        c = self.core
        self.enter(act)
        for h in range(self.HEADS):
            act.wait_ge(self.mixed.sem, self.mixed0 + h + 1)
            cut = slice(h * self.VD, (h + 1) * self.VD)
            own.step(act.activation(self.y[:, 0, cut], c.bank[:, 2, :], ACT.Copy))
            act.activation(self.y[:, 1, cut], c.bank[:, 3, :], ACT.Copy).then_inc(
                c.stage_done if h == self.HEADS - 1 else self.kept.sem, 1)


class Multiply(Stage):

    def __init__(self, core, out, a, b):
        self.out, self.a, self.b = out, a, b
        super().__init__(core)

    def plan(self):
        self.second = self.core.counter("second_tile_multiplied")
        self.second0 = self.second.reserve(1)

    def gpsimd(self, pool, own):
        self.enter(pool)
        pool.tensor_tensor(self.out[:, 1], self.a[:, 1], self.b[:, 1], ALU.mult).then_inc(self.second.sem, 1)

    def vector(self, dve, own):
        self.enter(dve)
        own.step(dve.tensor_tensor(self.out[:, 0], self.a[:, 0], self.b[:, 0], ALU.mult))
        dve.wait_ge(self.second.sem, self.second0 + 1)
        dve.tensor_copy(self.core.small[:, 0:1], self.core.const[:, 0:1]).then_inc(self.core.stage_done, 1)


class Attention(Stage):

    HEADS = 8
    SPANS = ((0, P), (P, 3 * P))

    def __init__(self, core, terms, mask, scale, value, out, dv, scratch, maps=1, lam=None, row_add=None):
        self.terms, self.mask, self.scale, self.value, self.out, self.dv = terms, mask, scale, value, out, dv
        self.scratch, self.maps, self.lam, self.row_add = scratch, maps, lam, row_add
        super().__init__(core)

    def plan(self):
        c, n = self.core, self.HEADS
        self.marks = {}
        for name in ("scored", "maxed", "exped", "turned", "turned_kept", "mixed"):
            counter = c.counter("attention_" + name)
            self.marks[name] = (counter.sem, counter.reserve(n))
        self.combined = c.counter("maps_combined")
        self.combined0 = self.combined.reserve(n if self.maps == 2 else 0)
        self.divided = c.counter("head_divided")
        self.divided0 = self.divided.reserve(n - 1)
        at = self.scratch
        self.masked = c.at(at, 2, self.maps, 3 * P)
        at += 2 * self.maps * 3 * P
        self.probs = c.at(at, 2, self.maps, 3 * P)
        at += 2 * self.maps * 3 * P
        self.mixedp = c.at(at, 2, 3 * P)
        at += 2 * 3 * P
        self.probsT = c.at(at, 2, 3 * P)
        self.neg_max = shaped(c.small[:, 64:64 + 2 * self.maps * 2], 2, self.maps, 2)
        self.sums = shaped(c.small[:, 96:96 + 2 * self.maps * 2], 2, self.maps, 2)
        self.inverse = shaped(c.small[:, 128:128 + 2 * self.maps * 2], 2, self.maps, 2)
        self.weight = shaped(c.small[:, 160:164], 2, 2)

    def wait(self, eng, name, h):
        if h >= 0:
            sem, base = self.marks[name]
            eng.wait_ge(sem, base + h + 1)

    def tensor(self, pe):
        c = self.core
        self.enter(pe)

        def score(h):
            self.wait(pe, "maxed", h - 1 if self.maps == 2 else h - 2)
            for m in range(self.maps):
                b = m if self.maps == 2 else h % 2
                terms = self.terms(h, m)
                for i, (lo, hi) in enumerate(self.SPANS):
                    for n, (q, k) in enumerate(terms):
                        mm = pe.matmul(c.bank[:, b, lo:hi], q(i), k[:, 0:hi - lo],
                                       start=(n == 0), stop=(n == len(terms) - 1))
            mm.then_inc(self.marks["scored"][0], 1)

        def turn(h):
            if self.maps == 2:
                pe.wait_ge(self.combined.sem, self.combined0 + h + 1)
            else:
                self.wait(pe, "exped", h)
            probs = self.mixedp[:, h % 2, :] if self.maps == 2 else self.probs[:, h % 2, 0, :]
            for n in range(3):
                last = pe.transpose(c.bank[:, 2, n * P:(n + 1) * P], probs[:, n * P:(n + 1) * P], c.tables["ident"])
            last.then_inc(self.marks["turned"][0], 1)

        def mix(h):
            self.wait(pe, "turned_kept", h)
            if h:
                pe.wait_ge(self.divided.sem, self.divided0 + h)
            for n, (i, k) in enumerate(((0, 0), (1, 0), (1, 1))):
                mm = pe.matmul(c.bank[:, 3, i * P:i * P + self.dv], self.probsT[:, h % 2, n * P:(n + 1) * P],
                               self.value(h, k), start=(k == 0), stop=(k == i))
            mm.then_inc(self.marks["mixed"][0], 1)

        score(0)
        for h in range(self.HEADS):
            if h + 1 < self.HEADS:
                score(h + 1)
            turn(h)
            mix(h)

    def scalar(self, act, own):
        c = self.core
        self.enter(act)
        for h in range(self.HEADS):
            self.wait(act, "maxed", h)
            self.wait(act, "turned", h - 2)
            if h >= 2:
                act.wait_ge(self.divided.sem, self.divided0 + h - 1)
            for m in range(self.maps):
                for i, (lo, hi) in enumerate(self.SPANS):
                    last = act.activation(self.probs[:, h % 2, m, lo:hi], self.masked[:, h % 2, m, lo:hi], ACT.Exp,
                                          bias=self.neg_max[:, h % 2, m, i:i + 1],
                                          accum_out=self.sums[:, h % 2, m, i:i + 1])
                    if (m, i) != (self.maps - 1, 1):
                        own.step(last)
            last.then_inc(self.marks["exped"][0], 1)
            self.wait(act, "turned", h)
            self.wait(act, "mixed", h - 2)
            act.activation(self.probsT[:, h % 2, :], c.bank[:, 2, 0:3 * P], ACT.Copy).then_inc(
                self.marks["turned_kept"][0], 1)

    def vector(self, dve, own):
        c = self.core
        self.enter(dve)

        def mask(h):
            self.wait(dve, "scored", h)
            self.wait(dve, "exped", h - 2)
            for m in range(self.maps):
                got = c.bank[:, m if self.maps == 2 else h % 2, 0:3 * P]
                held = self.masked[:, h % 2, m, :]
                if self.row_add is None:
                    own.step(dve.scalar_tensor_tensor(held, got, self.scale, self.mask, ALU.mult, ALU.add))
                else:
                    for i, (lo, hi) in enumerate(self.SPANS):
                        own.step(dve.scalar_tensor_tensor(held[:, lo:hi], got[:, lo:hi], self.row_add(h, i),
                                                          self.mask[:, lo:hi], ALU.add, ALU.add))
            own.settle()
            for m in range(self.maps):
                for i, (lo, hi) in enumerate(self.SPANS):
                    own.step(dve.tensor_reduce(self.neg_max[:, h % 2, m, i:i + 1], self.masked[:, h % 2, m, lo:hi],
                                               AX, ALU.max))
            own.settle()
            flat = self.neg_max[:, h % 2].rearrange("p m i -> p (m i)")
            dve.tensor_scalar(flat, flat, -1.0, None, ALU.mult).then_inc(self.marks["maxed"][0], 1)

        def combine(h):
            self.wait(dve, "exped", h)
            self.wait(dve, "turned", h - 2)
            own.step(dve.reciprocal(self.inverse[:, h % 2].rearrange("p m i -> p (m i)"),
                                    self.sums[:, h % 2].rearrange("p m i -> p (m i)")))
            own.settle()
            own.step(dve.tensor_scalar(self.weight[:, h % 2, :], self.inverse[:, h % 2, 1, :], self.lam, None, ALU.mult))
            for i, (lo, hi) in enumerate(self.SPANS):
                own.step(dve.tensor_scalar(self.mixedp[:, h % 2, lo:hi], self.probs[:, h % 2, 0, lo:hi],
                                           self.inverse[:, h % 2, 0, i:i + 1], None, ALU.mult))
            own.settle()
            for i, (lo, hi) in enumerate(self.SPANS):
                held = self.mixedp[:, h % 2, lo:hi]
                last = dve.scalar_tensor_tensor(held, self.probs[:, h % 2, 1, lo:hi], self.weight[:, h % 2, i:i + 1],
                                                held, ALU.mult, ALU.add)
                if i == 0:
                    own.step(last)
            last.then_inc(self.combined.sem, 1)

        def finish(h):
            self.wait(dve, "mixed", h)
            if self.maps == 1:
                own.step(dve.reciprocal(self.inverse[:, h % 2, 0, :], self.sums[:, h % 2, 0, :]))
                own.settle()
            for i in range(TT):
                out = self.out[:, i, h * self.dv:(h + 1) * self.dv]
                got = c.bank[:, 3, i * P:i * P + self.dv]
                if self.maps == 1:
                    last = dve.tensor_scalar(out, got, self.inverse[:, h % 2, 0, i:i + 1], None, ALU.mult)
                else:
                    last = dve.tensor_copy(out, got)
                if i == 0:
                    own.step(last)
            last.then_inc(c.stage_done if h == self.HEADS - 1 else self.divided.sem, 1)

        mask(0)
        for h in range(self.HEADS):
            if h + 1 < self.HEADS:
                mask(h + 1)
            if self.maps == 2:
                combine(h)
            if h:
                finish(h - 1)
        finish(self.HEADS - 1)


class ZeroPadded(Stage):

    def __init__(self, core, dst, copies):
        self.dst, self.copies = dst, copies
        super().__init__(core)

    def vector(self, dve, own):
        self.enter(dve)
        own.step(dve.memset(self.dst, 0.0))
        own.settle()
        for out, src in self.copies[:-1]:
            own.step(dve.tensor_copy(out, src))
        out, src = self.copies[-1]
        dve.tensor_copy(out, src).then_inc(self.core.stage_done, 1)


class Lambda(Stage):

    def __init__(self, core, neg_lam, gain, products):
        self.neg_lam, self.gain, self.products = neg_lam, gain, products
        super().__init__(core)

    def plan(self):
        c = self.core
        self.row = c.at(28928, 256)
        self.loaded, self.dotted, self.exped = (c.sem(n) for n in ("lambda_loaded", "lambda_dotted", "lambda_exped"))

    def gpsimd(self, pool, own):
        c, row = self.core, ROWS["lambda"]
        self.enter(pool)
        pool.dma_start(self.row, c.dram["rows"][row:row + 1, 0:256].to_broadcast([P, 256])).then_inc(
            self.loaded, 16)

    def vector(self, dve, own):
        c = self.core
        self.enter(dve)
        dve.wait_ge(self.loaded, 16)
        pairs = shaped(self.row, 2, 2, 64)
        own.step(dve.tensor_tensor(self.products, pairs[:, :, 0, :], pairs[:, :, 1, :], ALU.mult))
        own.settle()
        dve.tensor_reduce(c.small[:, 8:10], self.products, AX, ALU.add).then_inc(self.dotted, 1)
        own.step(dve.tensor_scalar(self.gain, c.col["subln"].to_broadcast([P, 8]), 1.0 - LAM_INIT, None, ALU.mult))
        dve.wait_ge(self.exped, 1)
        own.step(dve.tensor_tensor(c.small[:, 12:13], c.small[:, 11:12], c.small[:, 10:11], ALU.subtract))
        own.settle()
        dve.tensor_scalar(self.neg_lam, c.small[:, 12:13], -LAM_INIT, None, ALU.add).then_inc(c.stage_done, 1)

    def scalar(self, act, own):
        c = self.core
        self.enter(act)
        act.wait_ge(self.dotted, 1)
        act.activation(c.small[:, 10:12], c.small[:, 8:10], ACT.Exp).then_inc(self.exped, 1)


class PositionAngles(Stage):

    MAGIC = 1.5 * 2.0 ** 23
    PARTS = (6.28125, 0.00193500518798828125, 3.0199159819e-07)

    def __init__(self, core, cos, sin, held):
        self.cos, self.sin, self.held = cos, sin, held
        super().__init__(core)

    def plan(self):
        c = self.core
        self.loaded, self.reduced = c.sem("positions_loaded"), c.sem("angles_reduced")

    def gpsimd(self, pool, own):
        c = self.core
        self.enter(pool)
        pool.dma_start(c.small[:, 8:10].bitcast(I32), c.dram["positions"].rearrange("one (t p) -> p (one t)", p=P),
                       allow_slow_non_contiguous=True).then_inc(self.loaded, 16)

    def vector(self, dve, own):
        c = self.core
        self.enter(dve)
        dve.wait_ge(self.loaded, 16)
        step = own.step
        step(dve.tensor_copy(c.small[:, 10:12], c.small[:, 8:10].bitcast(I32)))
        own.settle()
        ang, turns, low, arg = (self.held[:, n, :] for n in range(4))
        for t in range(TT):
            step(dve.tensor_scalar(ang[:, t * 32:(t + 1) * 32], c.tables["inv_freq"], c.small[:, 10 + t:11 + t], None,
                                   ALU.mult))
        own.settle()
        step(dve.tensor_scalar(turns, ang, 1.0 / (2.0 * math.pi), self.MAGIC, ALU.mult, ALU.add))
        own.settle()
        step(dve.tensor_scalar(turns, turns, -self.MAGIC, None, ALU.add))
        own.settle()
        for part in self.PARTS:
            step(dve.scalar_tensor_tensor(ang, turns, -part, ang, ALU.mult, ALU.add))
            own.settle()
        step(dve.tensor_scalar(ang, ang, 3.1415925, -3.1415925, ALU.min, ALU.max))
        own.settle()
        step(dve.tensor_scalar(low, ang, -1.0, None, ALU.mult))
        own.settle()
        step(dve.tensor_tensor(low, low, ang, ALU.max))
        own.settle()
        dve.tensor_scalar(arg, low, -1.0, math.pi / 2, ALU.mult, ALU.add).then_inc(self.reduced, 1)

    def scalar(self, act, own):
        c = self.core
        self.enter(act)
        act.wait_ge(self.reduced, 1)
        own.step(act.activation(self.sin.rearrange("p t f -> p (t f)"), self.held[:, 0, :], ACT.Sin))
        act.activation(self.cos.rearrange("p t f -> p (t f)"), self.held[:, 3, :], ACT.Sin).then_inc(c.stage_done, 1)


class ForgetGates(Stage):

    H = 8

    def __init__(self, core, cum, neg, pick, held):
        self.cum, self.neg, self.pick, self.held = cum, neg, pick, held
        super().__init__(core)

    def plan(self):
        c = self.core
        self.unit_count = 1
        self.unit0 = c.take_units(self.unit_count)
        self.loaded = c.sem("forget_bias_loaded")
        self.logits = c.sem("forget_logits_ready")
        self.ln_ready = c.sem("forget_logarithm_ready")
        self.logs = c.sem("forget_logs_ready")
        self.summed = c.sem("forget_logs_summed")

    def gpsimd(self, pool, own):
        c, row = self.core, ROWS["b_f"]
        self.enter(pool)
        pool.dma_start(c.small[:, 16:24], c.dram["rows"][row:row + 1, 0:8].to_broadcast([P, 8])).then_inc(self.loaded, 16)
        self.last_remainders(pool, self.unit0 + LOWS)

    def tensor(self, pe):
        c = self.core
        self.enter(pe)
        self.ready(pe, self.unit0)
        for t in range(TT):
            for k in range(KD):
                mm = product(pe, c.bank[:, t, 0:self.H], parts(c.xT, slice(None), k, slice(t * P, (t + 1) * P)),
                             c.unit_parts(self.unit0, k * P, k * P + self.H), start=(k == 0), stop=(k == KD - 1))
        mm.then_inc(c.units_multiplied, 1)
        pe.wait_ge(self.logs, 1)
        logs = self.held[:, 3]
        pe.matmul(c.bank[:, 2, 0:self.H], c.tables["upper"], logs[:, 0, :], start=True, stop=True)
        pe.matmul(c.bank[:, 3, 0:self.H], c.tables["ones"], logs[:, 0, :], start=True, stop=False)
        pe.matmul(c.bank[:, 3, 0:self.H], c.tables["upper"], logs[:, 1, :], start=False, stop=True).then_inc(
            self.summed, 1)

    def vector(self, dve, own):
        c, h = self.core, self.H
        self.enter(dve)
        own.step(dve.memset(self.neg, 0.0))
        own.step(dve.tensor_copy(self.pick, spread(c.tables["ident"][:, 0:h], 2, P)))
        dve.wait_ge(self.loaded, 16)
        dve.wait_ge(c.units_multiplied, self.unit0 + 1)
        z, low, ln, logs = (self.held[:, n] for n in range(4))
        for t in range(TT):
            own.step(dve.tensor_tensor(z[:, t, :], c.bank[:, t, 0:h], c.small[:, 16:24], ALU.add))
        own.settle()
        own.step(dve.tensor_scalar(low, z, 0.0, None, ALU.min))
        own.settle()
        dve.scalar_tensor_tensor(ln, low, 2.0, z, ALU.mult, ALU.subtract).then_inc(self.logits, 1)
        dve.wait_ge(self.ln_ready, 1)
        dve.tensor_tensor(logs, low, ln, ALU.subtract).then_inc(self.logs, 1)
        dve.wait_ge(self.summed, 1)
        for t in range(TT):
            own.step(dve.tensor_copy(self.cum[:, t, :], c.bank[:, 2 + t, 0:h]))
        for t in range(TT):
            last = dve.tensor_scalar(self.neg[:, t, 0:h], c.bank[:, 2 + t, 0:h], -1.0, None, ALU.mult)
            if t < TT - 1:
                own.step(last)
        last.then_inc(c.stage_done, 1)

    def scalar(self, act, own):
        self.enter(act)
        act.wait_ge(self.logits, 1)
        ln = self.held[:, 2]
        own.step(act.activation(ln, ln, ACT.Exp))
        own.settle()
        act.activation(ln, ln, ACT.Ln, bias=1.0).then_inc(self.ln_ready, 1)
        self.round_next(act, self.unit0)


class SelectKeys(Stage):

    H = 8

    def __init__(self, core, qT, kT, w, mask, scratch):
        self.qT, self.kT, self.w, self.mask, self.scratch = qT, kT, w, mask, scratch
        super().__init__(core)

    def plan(self):
        c = self.core
        self.scored, self.rectified, self.added = (c.sem(n) for n in ("index_scored", "index_rectified", "index_added"))
        self.relu = c.at(self.scratch, 2, 3 * P)
        self.score = c.at(self.scratch + 768, 3 * P)
        self.weights = c.at(self.scratch + 1152, TT, self.H)
        self.best = c.at(self.scratch + 1168, 2, 8)

    def tensor(self, pe):
        c = self.core
        self.enter(pe)
        for h in range(self.H):
            if h >= 2:
                pe.wait_ge(self.rectified, h - 1)
            for i, (lo, hi) in enumerate(Attention.SPANS):
                mm = pe.matmul(c.bank[:, h % 2, lo:hi], self.qT[:, h // 4, i * P:(i + 1) * P],
                               self.kT[:, h % 4, 0:hi - lo], start=True, stop=True)
            mm.then_inc(self.scored, 1)

    def scalar(self, act, own):
        c = self.core
        self.enter(act)
        for h in range(self.H):
            act.wait_ge(self.scored, h + 1)
            if h >= 2:
                act.wait_ge(self.added, h - 1)
            act.activation(self.relu[:, h % 2, :], c.bank[:, h % 2, 0:3 * P], ACT.Relu, scale=32.0 ** -0.5).then_inc(
                self.rectified, 1)

    def vector(self, dve, own):
        c = self.core
        self.enter(dve)
        own.step(dve.tensor_scalar(self.weights, self.w, self.H ** -0.5, None, ALU.mult))
        own.settle()
        for h in range(self.H):
            dve.wait_ge(self.rectified, h + 1)
            if h:
                dve.wait_ge(self.added, h)
            for i, (lo, hi) in enumerate(Attention.SPANS):
                w, score = self.weights[:, i, h:h + 1], self.score[:, lo:hi]
                if h == 0:
                    last = dve.tensor_scalar(score, self.relu[:, 0, lo:hi], w, None, ALU.mult)
                else:
                    last = dve.scalar_tensor_tensor(score, self.relu[:, h % 2, lo:hi], w, score, ALU.mult, ALU.add)
                if i == 0:
                    own.step(last)
            last.then_inc(self.added, 1)
        dve.wait_ge(self.added, self.H)
        own.step(dve.tensor_tensor(self.score, self.score, c.tables["causal"], ALU.add))
        own.settle()
        for _ in range(DSA_TOPK // 8):
            for i, (lo, hi) in enumerate(Attention.SPANS):
                own.step(dve.max(self.best[:, i, :], self.score[:, lo:hi]))
            own.settle()
            for i, (lo, hi) in enumerate(Attention.SPANS):
                own.step(dve.match_replace(self.score[:, lo:hi], self.best[:, i, :], self.score[:, lo:hi], MARK))
            own.settle()
        own.step(dve.tensor_scalar(self.mask, self.score, MARK, None, ALU.is_equal))
        own.settle()
        own.step(dve.tensor_scalar(self.mask, self.mask, -NEG, NEG, ALU.mult, ALU.add))
        own.settle()
        dve.tensor_tensor(self.mask, self.mask, c.tables["causal"], ALU.add).then_inc(c.stage_done, 1)


class ShortConv(Stage):

    CH, TAPS = 4, 3

    def __init__(self, core, bcu, padded, held, out):
        self.bcu, self.padded, self.held, self.out = bcu, padded, held, out
        super().__init__(core)

    def vector(self, dve, own):
        c, n = self.core, self.CH
        self.enter(dve)
        own.step(dve.memset(self.padded[:, :, 0:self.TAPS - 1], 0.0))
        own.step(dve.tensor_tensor(self.padded[:, :, self.TAPS - 1:self.TAPS - 1 + SEQ], self.bcu[:, n:2 * n, :],
                                   self.bcu[:, 2 * n:3 * n, :], ALU.mult))
        own.settle()
        for j in range(self.TAPS):
            for ch in range(n):
                w = c.col["hyb_conv"][:, ch * self.TAPS + j:ch * self.TAPS + j + 1]
                src, acc = self.padded[:, ch, j:j + SEQ], self.held[:, ch, :]
                if j == 0:
                    own.step(dve.tensor_scalar(acc, src, w, None, ALU.mult))
                else:
                    own.step(dve.scalar_tensor_tensor(acc, src, w, acc, ALU.mult, ALU.add))
            own.settle()
        dve.tensor_tensor(self.out, self.held, self.bcu[:, 0:n, :], ALU.mult).then_inc(c.stage_done, 1)


class GluConv(Stage):

    TAPS, MINE = 31, 5

    def __init__(self, core, ag, sig, padded, products, out):
        self.ag, self.sig, self.padded, self.products, self.out = ag, sig, padded, products, out
        super().__init__(core)

    def plan(self):
        c = self.core
        self.sigmoids, self.glued = c.sem("glu_sigmoids"), c.sem("glu_ready")
        self.taps_done = c.sem("taps_added")
        self.product_ready, self.product_added = c.sem("product_ready"), c.sem("product_added")

    def scalar(self, act, own):
        c, theirs = self.core, KD - self.MINE
        self.enter(act)
        for ch in reversed(range(KD)):
            act.activation(self.sig[:, ch, :], self.ag[:, KD + ch, :], ACT.Sigmoid,
                           bias=c.col["b_pw1"][:, KD + ch:KD + ch + 1]).then_inc(self.sigmoids, 1)
        act.wait_ge(self.glued, theirs)
        for ch in range(self.MINE, KD):
            act.activation(self.out[:, ch, :], self.padded[:, ch, 0:SEQ], ACT.Identity,
                           bias=c.col["conf_conv_b"][:, ch:ch + 1],
                           scale=c.col["conf_conv"][:, ch * self.TAPS:ch * self.TAPS + 1]).then_inc(self.product_ready, 1)

        def multiply(n, i=0, steady=True):
            ch, slot = n % theirs, n // theirs % 2
            if steady:
                act.wait_ge(self.product_added, i * (2 * theirs) + n - 2 * theirs + 1)
            tap = i * 2 + n // theirs + 1
            act.activation(self.products[:, slot, ch, :], self.padded[:, self.MINE + ch, bass.ds(tap, SEQ)], ACT.Copy,
                           scale=c.col["conf_conv"][:, bass.ds(tap + (self.MINE + ch) * self.TAPS, 1)]).then_inc(
                               self.product_ready, 1)

        for n in range(2 * theirs):
            multiply(n, steady=False)
        with act.Fori(0, (self.TAPS - 3) // 2) as i:
            for n in range(2 * theirs, 4 * theirs):
                multiply(n, i)

    def vector(self, dve, own):
        c, pad = self.core, self.TAPS - 1
        self.enter(dve)
        own.step(dve.memset(self.padded[:, :, 0:pad], 0.0))
        own.settle()
        for n, ch in enumerate(reversed(range(KD))):
            dve.wait_ge(self.sigmoids, n + 1)
            dve.scalar_tensor_tensor(self.padded[:, ch, pad:pad + SEQ], self.ag[:, ch, :],
                                     c.col["b_pw1"][:, ch:ch + 1], self.sig[:, ch, :], ALU.add,
                                     ALU.mult).then_inc(self.glued, 1)
        dve.wait_ge(self.glued, KD)
        for ch in range(self.MINE):
            w = c.col["conf_conv"][:, ch * self.TAPS:ch * self.TAPS + 1]
            dve.tensor_scalar(self.out[:, ch, :], self.padded[:, ch, 0:SEQ], w, c.col["conf_conv_b"][:, ch:ch + 1],
                              ALU.mult, ALU.add).then_inc(self.taps_done, 1)
        with dve.Fori(0, self.TAPS - 1) as i:
            for ch in range(self.MINE):
                w = c.col["conf_conv"][:, bass.ds(i + ch * self.TAPS + 1, 1)]
                src = self.padded[:, ch, bass.ds(i + 1, SEQ)]
                dve.wait_ge(self.taps_done, i * self.MINE + ch + 1)
                dve.scalar_tensor_tensor(self.out[:, ch, :], src, w, self.out[:, ch, :], ALU.mult,
                                         ALU.add).then_inc(self.taps_done, 1)
        dve.wait_ge(self.product_added, (KD - self.MINE) * (self.TAPS - 1))
        dve.tensor_copy(c.small[:, 0:1], c.const[:, 0:1]).then_inc(c.stage_done, 1)

    def gpsimd(self, pool, own):
        c, theirs = self.core, KD - self.MINE
        self.enter(pool)

        def add(n, i=0, first=False):
            ch, slot = n % theirs, n // theirs % 2
            pool.wait_ge(self.product_ready, i * (2 * theirs) + n + theirs + 1)
            if not first:
                pool.wait_ge(self.product_added, i * (2 * theirs) + n - theirs + 1)
            acc = self.out[:, self.MINE + ch, :]
            pool.tensor_tensor(acc, acc, self.products[:, slot, ch, :], ALU.add).then_inc(self.product_added, 1)

        for n in range(2 * theirs):
            add(n, first=n < theirs)
        with pool.Fori(0, (self.TAPS - 3) // 2) as i:
            for n in range(2 * theirs, 4 * theirs):
                add(n, i)


class TransposeSwish(Transpose):

    def __init__(self, core, src, held, gain, bias):
        self.bias = bias
        super().__init__(core, src, held, KD, gain)

    def plan_copies(self):
        assert len(self.groups) <= 4
        self.swished, self.rounded = self.core.sem("swish_ready"), self.core.sem("swish_rounded")

    def scalar(self, act, own):
        c = self.core
        self.enter(act)
        for g, (t, c0, n) in enumerate(self.groups):
            act.wait_ge(self.turned.sem, self.turned0 + g + 1)
            for k in range(n):
                ch = c0 + k
                last = act.activation(self.dst[:, ch, t * P:(t + 1) * P], c.bank[:, g % 4, k * P:(k + 1) * P], ACT.Silu,
                                      bias=self.bias[:, ch:ch + 1], scale=self.gain[:, ch:ch + 1])
                if k < n - 1:
                    own.step(last)
            last.then_inc(self.swished, 1)

    def vector(self, dve, own):
        self.enter(dve)
        high, low = self.core.xT
        for g, (t, c0, n) in enumerate(self.groups):
            cut = (slice(None), slice(c0, c0 + n), slice(t * P, (t + 1) * P))
            dve.wait_ge(self.swished, g + 1)
            dve.tensor_copy(high[cut], self.dst[cut]).then_inc(self.rounded, 1)
            dve.wait_ge(self.rounded, g + 1)
            last = dve.tensor_tensor(low[cut], self.dst[cut], high[cut].bitcast(F32), ALU.subtract)
            if g < len(self.groups) - 1:
                own.step(last)
        last.then_inc(self.core.stage_done, 1)


class BackTranspose(Stage):

    def __init__(self, core, src, dst):
        self.src, self.dst = src, dst
        super().__init__(core)

    def plan(self):
        self.turned = self.core.counter("tile_transposed")
        self.turned0 = self.turned.reserve(4)

    def tensor(self, pe):
        c = self.core
        self.enter(pe)
        for g in range(4):
            t, q = g // 2, g % 2
            for k in range(4):
                last = pe.transpose(c.bank[:, g, k * P:(k + 1) * P], self.src[:, 4 * q + k, t * P:(t + 1) * P],
                                    c.tables["ident"])
            last.then_inc(self.turned.sem, 1)

    def vector(self, dve, own):
        c = self.core
        self.enter(dve)
        for g in range(4):
            t, q = g // 2, g % 2
            dve.wait_ge(self.turned.sem, self.turned0 + g + 1)
            last = dve.tensor_copy(self.dst[:, t, q * 512:(q + 1) * 512], c.bank[:, g, :])
            if g < 3:
                own.step(last)
        last.then_inc(c.stage_done, 1)


class AddRow(Stage):

    def __init__(self, core, row):
        self.row = row
        super().__init__(core)

    def plan(self):
        self.loaded = self.core.counter("rows_loaded")
        self.loaded0 = self.loaded.reserve(16)

    def gpsimd(self, pool, own):
        c = self.core
        self.enter(pool)
        pool.dma_start(c.rows_at(0), c.dram["rows"][self.row:self.row + 1, :].to_broadcast([P, D])).then_inc(
            self.loaded.sem, 16)

    def vector(self, dve, own):
        c = self.core
        self.enter(dve)
        dve.wait_ge(self.loaded.sem, self.loaded0 + 16)
        own.step(dve.tensor_tensor(c.x[:, 0, :], c.x[:, 0, :], c.rows_at(0), ALU.add))
        dve.tensor_tensor(c.x[:, 1, :], c.x[:, 1, :], c.rows_at(0), ALU.add).then_inc(c.stage_done, 1)


class Store(Stage):

    def scalar(self, act, own):
        c = self.core
        self.enter(act)
        stored = c.sem("output_stored")
        act.dma_start(c.dram["out"].rearrange("(t p) d -> p t d", p=P), c.x[:, :, :]).then_inc(stored, 16)
        act.wait_ge(stored, 16)




def rows_of(c):
    return [(c.x[:, t, :], c.x[:, t, :]) for t in range(TT)]


def post_norm(c, layer, which):
    n = 2 * layer + which
    Norm(c, rows_of(c), "ln", 1e-5, rows=(ROWS["ln_g"] + n, ROWS["ln_b"] + n))
    TransposeSplit(c, c.x)


def pre_norm(c, gain):
    y = c.at(26624, TT, D)
    Norm(c, [(c.x[:, t, :], y[:, t, :]) for t in range(TT)], "rms", 1e-6)
    TransposeSplit(c, y, gain=gain)


def peer(c, layer):
    queries, scores = c.at(0, 16, SEQ), c.at(4096, TT, 16, P)
    routes = c.at(8192, TT, 3, P)
    FeatureMajor(c, c.xT, KD, 16, queries)
    KeyScores(c, queries, c.at(30720, 16, P), c.dram["subkeysT"][layer], scores)
    Route(c, scores, routes, 9216)
    routesT = shaped(c.scratch[:, 0:3 * SEQ], 3, SEQ)
    Transpose(c, routes.rearrange("p t s n -> p t (s n)"), routesT, 3)
    gates = c.at(0, SEQ, N_KEYS)
    spare = [c.activated[:, n, :] for n in range(2)] + [c.scratch[:, 768 + n * SEQ:768 + (n + 1) * SEQ] for n in range(2)]
    SpreadGates(c, routesT, [(v[:, 0:P], v[:, P:2 * P]) for v in spare], gates)
    ExpertLoop(c, N_KEYS, 1, ACT.Gelu_apprx_tanh, DN_ALPHA, 1.0, gates)


def swiglu(c, gain):
    pre_norm(c, gain)
    ExpertLoop(c, D_FF // P, 2, ACT.Silu, 1.0, 0.5)


def heads(v, n):
    return v.rearrange("p t (h d) -> p t h d", h=n)


def at_tile(ap):
    return lambda i: ap[:, i * P:(i + 1) * P]


def first_block(c):
    TransposeSplit(c, c.x)
    retention(c)
    post_norm(c, 0, 0)
    peer(c, 0)
    post_norm(c, 0, 1)
    differential(c)
    post_norm(c, 1, 0)
    peer(c, 1)
    Norm(c, rows_of(c), "ln", 1e-5, rows=(ROWS["ln_g"] + 3, ROWS["ln_b"] + 3))


def retention(c):
    proj = c.at(0, TT, 6144)
    tables = c.at(30720, 2048)
    Fetch(c, tables, c.dram["fetched"][:, 0:2048])
    Project(c, c.xT, KD, [PIECE] * 12, proj, [ACT.Copy] * 8 + [ACT.Silu] * 4)
    qk = [heads(proj[:, :, 0:1024], 4), heads(proj[:, :, 1024:2048], 4)]
    Rotate(c, qk, 128, shaped(tables[:, 0:256], TT, 128), shaped(tables[:, 256:512], TT, 128), 12288)
    qkT = c.at(21504, 16, SEQ)
    Transpose(c, proj[:, :, 0:2048], qkT, 16)
    y = c.at(12288, TT, 2048)
    RetentionScores(c, qkT[:, 0:8], qkT[:, 8:16], proj[:, :, 2048:4096], tables[:, 512:2048], y,
                    c.at(16384, 2, 3 * P))
    cuts = [y[:, t, h * 512:(h + 1) * 512] for t in range(TT) for h in range(4)]
    Norm(c, [(v, v) for v in cuts], "ln", 1e-5)
    Multiply(c, y, y, proj[:, :, 4096:6144])
    for half in range(2):
        TransposeSplit(c, y[:, :, half * D:(half + 1) * D])
        AddTo(c, c.xT, KD, DN_ALPHA if half == 0 else 1.0)


def differential(c):
    tab = c.tables
    qkv = c.at(0, TT, 3072)
    Project(c, c.xT, KD, [PIECE] * 6, qkv)
    q, k = qkv[:, :, 0:1024], qkv[:, :, 1024:2048]
    Rotate(c, [heads(q, 16), heads(k, 16)], 8, shaped(tab["cos_att"], TT, 8), shaped(tab["sin_att"], TT, 8), 24576)
    padded = c.at(12288, TT, 2, 8, P)
    kh = k.rearrange("p t (h m d) -> p t h m d", h=8, m=2)
    ZeroPadded(c, padded.rearrange("p t m h d -> p (t m h d)"),
               [(padded[:, t, m, :, 64 * m:64 * m + 64], kh[:, t, :, m, :]) for t in range(TT) for m in range(2)])
    qT, kT = c.at(6144, 8, SEQ), c.at(8192, 16, SEQ)
    Transpose(c, q, qT, 8)
    Transpose(c, padded.rearrange("p t m h d -> p t (m h d)"), kT, 16)
    neg_lam, sub_gain = c.small[:, 200:201], c.small[:, 208:216]
    Lambda(c, neg_lam, sub_gain, c.at(28672, 2, 64))
    o = c.at(22528, TT, D)
    Attention(c, lambda h, m: [(at_tile(qT[:, h, :]), kT[:, 8 * m + h, :])], tab["causal"], 64.0 ** -0.5,
              lambda h, t: qkv[:, t, 2048 + h * P:2048 + (h + 1) * P], o, P, 16384, maps=2, lam=neg_lam)
    cuts = [o[:, t, h * P:(h + 1) * P] for t in range(TT) for h in range(8)]
    Norm(c, [(v, v) for v in cuts], "rms", 1e-5)
    TransposeSplit(c, o, gain=sub_gain)
    AddTo(c, c.xT, KD, DN_ALPHA)


def second_block(c):
    for layer in range(2):
        swiglu(c, c.col["ffn_norm_2"][:, 16 * layer:16 * layer + 8])
        pre_norm(c, c.col["mix_norm_2"][:, 8 * layer:8 * layer + 8])
        (mla, fox)[layer](c)
        swiglu(c, c.col["ffn_norm_2"][:, 16 * layer + 8:16 * layer + 16])
        pre_norm(c, c.col["ple_norm"][:, 8 * layer:8 * layer + 8])
        gate, gated, pT = c.at(0, TT, D), c.at(2048, TT, D), c.at(4096, 2, SEQ)
        Project(c, c.xT, KD, [PIECE] * 2, gate, [ACT.Sigmoid] * 2)
        Fetch(c, pT, c.dram["pT"][layer])
        SplitOperand(c, pT, 0)
        GatedAdd(c, parts(c.xT, slice(None), slice(0, 2)), 2, gate, gated)
    Norm(c, rows_of(c), "rms", 1e-6, rows=(ROWS["final_2"],))


def mla(c):
    low = c.at(0, TT, 512)
    Project(c, c.xT, KD, [448], low)
    Norm(c, [(low[:, t, a:b], low[:, t, a:b]) for t in range(TT) for a, b in ((0, 256), (256, 384))], "rms", 1e-6)
    cos, sin = c.at(12288, TT, 32), c.at(12352, TT, 32)
    PositionAngles(c, cos, sin, c.at(12416, 4, 64))
    chunked = c.at(12800, 3 * P)
    Fetch(c, chunked, c.dram["fetched"][:, 2048:2432])
    TransposeSplit(c, low[:, :, 0:384], 3, c.col["mla_norms"])
    c_q, c_kv = parts(c.xT, slice(None), slice(0, 2)), parts(c.xT, slice(None), slice(2, 3))
    qT = c.at(4096, 8, SEQ)
    FeatureMajor(c, c_q, 2, 8, qT)
    q_rope = c.at(6144, TT, 512)
    Project(c, c_q, 2, [PIECE], q_rope)
    kT = c.at(8192, 8, SEQ)
    FeatureMajor(c, c_kv, 1, 8, kT)
    v = c.at(10240, TT, D)
    Project(c, c_kv, 1, [PIECE] * 2, v)
    Rotate(c, [heads(q_rope, 8), heads(low[:, :, 384:448], 1)], 32, cos, sin, 24576)
    padded = c.at(1024, TT, 2, P)
    ZeroPadded(c, padded.rearrange("p t m d -> p (t m d)"),
               [(padded[:, :, m, 64 * m:64 * m + 64], low[:, :, 384:448]) for m in range(2)])
    q_ropeT, k_ropeT = c.at(7168, 4, SEQ), c.at(3072, 2, SEQ)
    Transpose(c, q_rope, q_ropeT, 4)
    Transpose(c, padded.rearrange("p t m d -> p t (m d)"), k_ropeT, 2)
    o = c.at(22528, TT, D)
    Attention(c, lambda h, m: [(at_tile(qT[:, h, :]), kT[:, h, :]),
                               (at_tile(q_ropeT[:, h // 2, :]), k_ropeT[:, h % 2, :])],
              chunked, 192.0 ** -0.5, lambda h, t: v[:, t, h * P:(h + 1) * P], o, P, 16384)
    TransposeSplit(c, o)
    AddTo(c, c.xT, KD)


def fox(c):
    qkT, v = c.at(0, 16, SEQ), c.at(4096, TT, D)
    FeatureMajor(c, c.xT, KD, 16, qkT, [128.0 ** -0.5] * 8 + [1.0] * 8)
    Project(c, c.xT, KD, [PIECE] * 2, v)
    cum, neg, pick = c.at(6144, TT, 8), c.at(6400, TT, P), c.at(7168, 8, P)
    ForgetGates(c, cum, neg, pick, c.at(8192, 4, TT, 8))
    negT = c.at(8448, 1, SEQ)
    Transpose(c, neg, negT, 1)
    o = c.at(22528, TT, D)
    Attention(c, lambda h, m: [(at_tile(qkT[:, h, :]), qkT[:, 8 + h, :]), (lambda i: pick[:, h, :], negT[:, 0, :])],
              c.tables["causal"], 1.0, lambda h, t: v[:, t, h * P:(h + 1) * P], o, P, 16384,
              row_add=lambda h, i: cum[:, i, h:h + 1])
    TransposeSplit(c, o)
    AddTo(c, c.xT, KD)


def third_block(c):
    for layer in range(2):
        swiglu(c, c.col["ffn_norm_3"][:, 16 * layer:16 * layer + 8])
        pre_norm(c, c.col["mix_norm_3"][:, 8 * layer:8 * layer + 8])
        (sparse_and_conv, conformer)[layer](c)
        swiglu(c, c.col["ffn_norm_3"][:, 16 * layer + 8:16 * layer + 16])
    Norm(c, rows_of(c), "rms", 1e-6, rows=(ROWS["final_3"],))


def sparse_and_conv(c):
    tab = c.tables
    z, bcu = c.at(0, TT, 1024), c.at(2048, 12, SEQ)
    Project(c, c.xT, KD, [512, 424], z)
    FeatureMajor(c, c.xT, KD, 12, bcu)
    Rotate(c, [heads(z[:, :, 0:576], 9)], 8, shaped(tab["cos_att"], TT, 8), shaped(tab["sin_att"], TT, 8), 28672)
    Rotate(c, [heads(z[:, :, 640:928], 9)], 4, shaped(tab["cos_idx"], TT, 4), shaped(tab["sin_idx"], TT, 4), 28672)
    padded = c.at(8192, TT, 6, P)
    ZeroPadded(c, padded.rearrange("p t m d -> p (t m d)"),
               [(padded[:, :, m, 64 * m:64 * m + 64], z[:, :, 512:576]) for m in range(2)]
               + [(padded[:, :, 2 + m, 32 * m:32 * m + 32], z[:, :, 896:928]) for m in range(4)])
    qT, qiT, kT = c.at(10240, 4, SEQ), c.at(11264, 2, SEQ), c.at(12288, 6, SEQ)
    Transpose(c, z[:, :, 0:512], qT, 4)
    Transpose(c, z[:, :, 640:896], qiT, 2)
    Transpose(c, padded.rearrange("p t m d -> p t (m d)"), kT, 6)
    mask = c.at(14336, 3 * P)
    SelectKeys(c, qiT, kT[:, 2:6], z[:, :, 928:936], mask, 15360)
    o, convolved = c.at(22528, TT, 512), c.at(24576, 4, SEQ)
    Attention(c, lambda h, m: [(at_tile(qT[:, h // 2, :]), kT[:, h % 2, :])], mask, 64.0 ** -0.5,
              lambda h, t: z[:, t, 576:640], o, 64, 16896)
    ShortConv(c, bcu, shaped(c.arena[:, 5120:5120 + 4 * 258], 4, 258), c.at(6400, 4, SEQ), convolved)
    SplitOperand(c, convolved, 4)
    TransposeSplit(c, o, 4)
    AddTo(c, c.xT, KD)


def conformer(c):
    ag, sig = c.at(0, 16, SEQ), c.at(4096, KD, SEQ)
    FeatureMajor(c, c.xT, KD, 16, ag)
    convolved = c.at(9216, KD, SEQ)
    GluConv(c, ag, sig, c.at(6144, KD, SEQ + 30), c.at(16384, 2, 3, SEQ), convolved)
    turned = c.at(12288, TT, D)
    BackTranspose(c, convolved, turned)
    Norm(c, [(turned[:, t, :], turned[:, t, :]) for t in range(TT)], "ln", 1e-6)
    TransposeSwish(c, turned, c.at(14336, KD, SEQ), c.col["conf_ln_g"], c.col["conf_ln_b"])
    AddTo(c, c.xT, KD)
    AddRow(c, ROWS["b_pw2"])




def build(nc, dram, plan=None):
    with ExitStack() as ctx:
        c = Core(nc, ctx, dram)
        Load(c)
        if plan:
            plan(c)
        else:
            first_block(c)
            second_block(c)
            third_block(c)
        Store(c)
        units = c.units + HIGHS
        vector_own, scalar_own, pool_own = c.sem("vector_own"), c.sem("scalar_own"), c.sem("pool_own")
        block = ctx.enter_context(nc.Block())

        @block.sync
        def _(sp):
            def load(unit, i=0):
                if unit >= RING:
                    sp.wait_ge(c.unit_ready[unit % LOWS], i * (RING // LOWS) + (unit - RING) // LOWS + 1)
                src = dram["stream"][bass.ds(i * RING + unit, 1), :, :].rearrange("one p n -> (one p) n")
                sp.dma_start(c.ring[:, unit % RING, :], src).then_inc(c.unit_landed[unit % RING], 16)

            for unit in range(min(RING, units)):
                load(unit)
            if units >= 2 * RING:
                with sp.Fori(0, units // RING - 1) as i:
                    for slot in range(RING):
                        load(RING + slot, i)
            for unit in range(max(units // RING, 1) * RING, units):
                load(unit)

        @block.gpsimd
        def _(pool):
            own = Own(pool, pool_own)
            for stage in c.stages:
                stage.gpsimd(pool, own)

        @block.scalar
        def _(act):
            own = Own(act, scalar_own)
            for stage in c.stages:
                stage.scalar(act, own)

        @block.vector
        def _(dve):
            own = Own(dve, vector_own)
            for stage in c.stages:
                stage.vector(dve, own)

        @block.tensor
        def _(pe):
            for stage in c.stages:
                stage.tensor(pe)

        return units




def moving_units(w):
    k, n = w.shape
    blocks = -(-n // PIECE)
    if n < blocks * PIECE:
        w = np.concatenate([w, np.zeros((k, blocks * PIECE - n), w.dtype)], 1)
    pieces = w.reshape(k // P, P, blocks, PIECE).transpose(2, 0, 1, 3).reshape(-1, P, PIECE)
    return pieces.reshape(-1, 2, P, PIECE).transpose(0, 2, 1, 3).reshape(-1, P, UNIT)


def standing_units(w):
    k, n = w.shape
    chunks = -(-n // P)
    if n < chunks * P:
        w = np.concatenate([w, np.zeros((k, chunks * P - n), w.dtype)], 1)
    pieces = w.reshape(k // P, P, chunks, P).transpose(2, 0, 1, 3).reshape(-1, P, P)
    if len(pieces) % 8:
        pieces = np.concatenate([pieces, np.zeros((-len(pieces) % 8, P, P), w.dtype)])
    return pieces.reshape(-1, 8, P, P).transpose(0, 2, 1, 3).reshape(-1, P, UNIT)


def loop_units(firsts, last):
    n = len(last)
    out = [f[0] for f in firsts]
    for c in range(n):
        if c + 1 < n:
            out += [f[c + 1] for f in firsts]
        out.append(last[c])
    return np.stack(out)


def peer_units(w_q, u, v):
    yield standing_units(w_q)
    first = u.reshape(N_KEYS, N_KEYS, KD, P).transpose(1, 3, 2, 0).reshape(N_KEYS, P, UNIT)
    yield loop_units([first], v.reshape(N_KEYS, N_KEYS, D).transpose(1, 0, 2))


def swiglu_units(gate, up, down):
    return loop_units([standing_units(gate), standing_units(up)], down.reshape(-1, P, D))


def stream_of(i):
    yield moving_units(i["ret_w_in"][0])
    yield moving_units(i["ret_w_out"][0][:D])
    yield moving_units(i["ret_w_out"][0][D:])
    yield from peer_units(i["peer_w_q"][0], i["peer_u"][0], i["peer_v"][0])
    yield moving_units(i["diff_w_q"][0])
    yield moving_units(i["kv_w"])
    yield moving_units(i["diff_w_out"][0])
    yield from peer_units(i["peer_w_q"][1], i["peer_u"][1], i["peer_v"][1])
    for layer in range(2):
        w_in, w_out = i["ffn_w_in_2"][layer], i["ffn_w_out_2"][layer]
        yield swiglu_units(w_in[0, :, :D_FF], w_in[0, :, D_FF:], w_out[0])
        if layer == 0:
            yield moving_units(i["mla_w_down_2"][0])
            w_uq = i["mla_w_uq_2"][0].reshape(256, 8, 192)
            yield standing_units(w_uq[:, :, :128].reshape(256, 1024))
            yield moving_units(w_uq[:, :, 128:].reshape(256, 512))
            w_ukv = i["mla_w_ukv_2"][0].reshape(128, 8, 256)
            yield standing_units(w_ukv[:, :, :128].reshape(128, 1024))
            yield moving_units(w_ukv[:, :, 128:].reshape(128, 1024))
            yield moving_units(i["mla_w_o_2"][0])
        else:
            w = i["fox_w_in_2"][0]
            yield standing_units(w[:, :2048])
            yield moving_units(w[:, 2048:3072])
            yield standing_units(w[:, 3072:])
            yield moving_units(i["fox_w_o_2"][0])
        yield swiglu_units(w_in[1, :, :D_FF], w_in[1, :, D_FF:], w_out[1])
        yield moving_units(i["ple_w_gate_2"][layer])
        yield moving_units(i["ple_w_proj_2"][layer])
    for layer in range(2):
        gate, up, down = (i[f"ffn_w_{n}_3"][layer] for n in ("gate", "up", "down"))
        yield swiglu_units(gate[0], up[0], down[0])
        if layer == 0:
            w = i["hyb_w_in_3"][0]
            yield moving_units(w[:, :936])
            yield standing_units(w[:, 936:])
            yield moving_units(i["hyb_w_out_3"][0])
        else:
            yield standing_units(i["conf_w_pw1_3"][0])
            yield moving_units(i["conf_w_pw2_3"][0])
        yield swiglu_units(gate[1], up[1], down[1])
    yield np.zeros((HIGHS, P, UNIT), i["x"].dtype)


def columns_of(i):
    def col(a):
        return a.reshape(-1, P).T

    conv = i["hyb_conv_w_3"][0].reshape(3, 4, P).transpose(2, 1, 0).reshape(P, 12)
    conf = i["conf_conv_w_3"][0].reshape(31, KD, P).transpose(2, 1, 0).reshape(P, 248)
    return np.ascontiguousarray(np.concatenate([
        col(i["diff_subln_g"][0]), col(i["ffn_norm_2"]), col(i["mix_norm_2"]), col(i["mla_q_norm_2"][0]),
        col(i["mla_kv_norm_2"][0]), col(i["ple_norm_2"]), col(i["ffn_norm_3"]), col(i["mix_norm_3"]), conv,
        col(i["conf_b_pw1_3"][0]), conf, col(i["conf_conv_b_3"][0]), col(i["conf_ln_g_3"][0]),
        col(i["conf_ln_b_3"][0])], 1))


def rows_from(i):
    def padded(a):
        a = a.reshape(1, -1)
        return np.concatenate([a, np.zeros((1, D - a.shape[1]), a.dtype)], 1)

    return np.concatenate([i["ln_g"].reshape(4, D), i["ln_b"].reshape(4, D), i["final_norm_2"][None],
                           i["final_norm_3"][None], i["conf_b_pw2_3"], padded(i["diff_lambda"]),
                           padded(i["fox_b_f_2"])], 0)


def arrays_of(i):
    tables = constant_tables()
    return {
        "x_dram": i["x"].reshape(SEQ, D),
        "stream_dram": np.concatenate(list(stream_of(i)), 0),
        "const_dram": np.concatenate([tables[name] for name in RESIDENT], 1),
        "fetched_dram": np.concatenate([tables[name] for name in FETCHED], 1),
        "subkeysT_dram": np.ascontiguousarray(i["peer_subkeys"].reshape(2, 16, N_KEYS, P).transpose(0, 3, 1, 2)),
        "cols_dram": columns_of(i),
        "rows_dram": rows_from(i),
        "positions_dram": i["positions_2"],
        "pT_dram": np.ascontiguousarray(i["p_2"][:, 0].reshape(2, SEQ, 2, P).transpose(0, 3, 2, 1)),
    }


def kernel(**inputs):
    import concourse.bacc as bacc
    from concourse.bass_utils import run_bass_kernel_spmd

    arrays = arrays_of({k: np.asarray(v) for k, v in inputs.items()})
    nc = bacc.Bacc("TRN2", target_bir_lowering=False, num_devices=1)
    dram = {n.removesuffix("_dram"): nc.dram_tensor(n, a.shape, mybir.dt.from_np(a.dtype), kind="ExternalInput").ap()
            for n, a in arrays.items()}
    dram["out"] = nc.dram_tensor("out_dram", (SEQ, D), F32, kind="ExternalOutput").ap()
    units = build(nc, dram)
    assert units == len(arrays["stream_dram"]), (units, len(arrays["stream_dram"]))
    r = run_bass_kernel_spmd(nc, [arrays], core_ids=[0])
    return r.results[0]["out_dram"].reshape(1, SEQ, D)
```

```python
import math
from contextlib import ExitStack

import numpy as np

import concourse.bass as bass
from concourse import mybir

P = 128
SEQ = 256
TT = SEQ // P
D = 1024
KD = D // P
RING = 4
HIGHS = 3
LOWS = 2
PERIOD = 12
UNIT = 1024
PIECE = 512
D_FF = 2816
N_KEYS = 128
TOPK = 16
PEER_HEADS = 8
DSA_TOPK = 64
AHEAD = 3 * PERIOD
NEG = -1.0e30
MARK = -3.0e38
DN_ALPHA = 4.0 ** 0.25
LAM_INIT = 0.8 - 0.6 * math.exp(-0.3)
F32 = mybir.dt.float32
F32R = mybir.dt.float32r
U32 = mybir.dt.uint32
I32 = mybir.dt.int32
ACT = mybir.ActivationFunctionType
ALU = mybir.AluOpType
AX = mybir.AxisListType.X



def constant_tables():
    f32 = np.float32
    t = {}
    ar = np.arange(P)
    t["ident"] = np.eye(P)
    t["iota"] = np.broadcast_to(ar, (P, P))
    causal = np.where(ar[None, :] <= ar[:, None], 0.0, NEG)
    chunked = np.where(ar[None, :] // 64 <= ar[:, None] // 64, 0.0, NEG)
    zero = np.zeros((P, P))
    t["causal"] = np.concatenate([causal, zero, causal], 1)
    t["chunked"] = np.concatenate([chunked, zero, chunked], 1)
    log_g = np.log(f32(1.0) - np.exp2(f32(-5.0) - np.arange(4, dtype=f32))).astype(f32)
    rel = (ar[None, :] - ar[:, None]).astype(f32)
    same = [np.where(rel >= 0, np.exp(np.maximum(rel, 0) * g), 0.0) for g in log_g]
    past = [np.exp((rel + P) * g) for g in log_g]
    t["decay"] = np.concatenate([np.concatenate([s, q, s], 1) for s, q in zip(same, past)], 1) / 16.0
    t["upper"] = np.where(ar[:, None] <= ar[None, :], 1.0, 0.0)
    t["ones"] = np.ones((P, P))

    def rotation(name, freqs):
        pos = np.arange(SEQ, dtype=f32)
        ang = (pos[:, None] * freqs[None, :].astype(f32)).astype(f32).astype(np.float64)
        for kind, fn in (("cos", np.cos), ("sin", np.sin)):
            t[kind + name] = fn(ang).reshape(TT, P, -1).transpose(1, 0, 2).reshape(P, -1)

    rotation("_ret", f32(1.0) / (f32(10000.0) ** np.linspace(0.0, 1.0, 128, dtype=f32)))
    rotation("_att", f32(500000.0) ** (-np.arange(8, dtype=f32) / f32(8)))
    rotation("_idx", f32(500000.0) ** (-np.arange(4, dtype=f32) / f32(4)))
    t["inv_freq"] = np.broadcast_to(f32(10000.0) ** (-np.arange(0, 64, 2, dtype=f32) / f32(64)), (P, 32))
    return {k: np.ascontiguousarray(v, dtype=f32) for k, v in t.items()}


RESIDENT = ("ident", "iota", "causal", "upper", "ones", "cos_att", "sin_att", "cos_idx", "sin_idx", "inv_freq")
FETCHED = ("cos_ret", "sin_ret", "decay", "chunked")


COLUMNS = {"subln": 1, "mla_norms": 3, "hyb_conv": 12, "b_pw1": 16, "conf_conv": 248, "conf_conv_b": 8,
           "conf_ln_g": 8, "conf_ln_b": 8}
ROWS = {"ln_g": 0, "ln_b": 4, "final_2": 8, "final_3": 9, "b_pw2": 10, "lambda": 11, "b_f": 12,
        "ffn_norm_2": 13, "mix_norm_2": 17, "ple_norm": 19, "ffn_norm_3": 21, "mix_norm_3": 25}
N_ROWS = 27


class Counter:

    def __init__(self, sem):
        self.sem = sem
        self.planned = 0

    def reserve(self, n):
        base = self.planned
        self.planned += n
        return base


class Own:

    def __init__(self, eng, sem):
        self.eng, self.sem, self.n = eng, sem, 0

    def step(self, ins):
        ins.then_inc(self.sem, 1)
        self.n += 1
        return self.n

    def settle(self, n=None):
        self.eng.wait_ge(self.sem, self.n if n is None else n)


class Core:

    def __init__(self, nc, ctx, dram):
        self.nc, self.ctx, self.dram = nc, ctx, dram
        self.units = 0
        self.stages = []
        self.counted = 0
        self.counters = {}

        def sb(name, shape, dt=F32):
            return ctx.enter_context(nc.sbuf_tensor(name, shape, dt))

        self.x = sb("x", [P, TT, D])
        self.xT = (sb("xT_high", [P, KD, SEQ], F32R), sb("xT_low", [P, KD, SEQ], F32R))
        self.ring = sb("ring", [P, RING, UNIT])
        self.high = sb("high", [P, HIGHS, UNIT], F32R)
        self.low = sb("low", [P, LOWS, UNIT], F32R)
        self.arena = sb("arena", [P, 32768])
        self.scratch = sb("scratch", [P, 3 * SEQ + 512])
        self.tables = {}
        tables = constant_tables()
        tables = {name: tables[name] for name in RESIDENT}
        self.n_const = sum(v.shape[1] for v in tables.values())
        self.const = sb("const", [P, self.n_const])
        at = 0
        for name, v in tables.items():
            self.tables[name] = self.const[:, at:at + v.shape[1]]
            at += v.shape[1]
        self.n_cols = sum(COLUMNS.values())
        self.cols = sb("cols", [P, self.n_cols])
        at = 0
        self.col = {}
        for name, n in COLUMNS.items():
            self.col[name] = self.cols[:, at:at + n]
            at += n
        self.activated = sb("activated", [P, 2, SEQ])
        self.hidden = (sb("hidden_high", [P, 2, SEQ], F32R), sb("hidden_low", [P, 2, SEQ], F32R))
        self.small = sb("small", [P, 256])
        self.stats = sb("stats", [P, 16, 2, 6])
        self.moments = sb("moments", [P, 16, 2])
        self.square = sb("square", [P, 16])
        self.power = sb("power", [P, 16])
        self.root = sb("root", [P, 16])
        self.rstd = sb("rstd", [P, 16])
        self.acc = ctx.enter_context(nc.psum_tensor("acc", [P, TT, 1024], F32))
        self.bank = ctx.enter_context(nc.psum_tensor("bank", [P, 4, 512], F32))
        self.unit_landed = [self.sem(f"unit_landed{s}") for s in range(RING)]
        self.units_rounded = self.sem("units_rounded")
        self.unit_ready = [self.sem(f"unit_ready{s}") for s in range(LOWS)]
        self.units_multiplied = self.sem("units_multiplied")
        self.stage_done = self.sem("stage_done")
        self.inputs_loaded = self.sem("inputs_loaded")

    def sem(self, name):
        return self.ctx.enter_context(self.nc.semaphore(name))

    def counter(self, name):
        if name not in self.counters:
            self.counters[name] = Counter(self.sem(name))
        return self.counters[name]

    def at(self, off, *dims):
        n = int(np.prod(dims))
        v = self.arena[:, off:off + n]
        return shaped(v, *dims)

    def rows_at(self, n):
        return self.arena[:, 30720 + n * D:30720 + (n + 1) * D]

    def round_unit(self, act, unit, i=0):
        act.wait_ge(self.unit_landed[unit % RING], i * (16 * PERIOD // RING) + 16 * (unit // RING + 1))
        if unit >= HIGHS:
            act.wait_ge(self.units_multiplied, i * PERIOD + unit - HIGHS + 1)
        act.activation(self.high[:, unit % HIGHS, :], self.ring[:, unit % RING, :], ACT.Copy).then_inc(
            self.units_rounded, 1)

    def take_remainder(self, eng, unit, i=0):
        eng.wait_ge(self.units_rounded, i * PERIOD + unit + 1)
        if unit >= LOWS:
            eng.wait_ge(self.units_multiplied, i * PERIOD + unit - LOWS + 1)
        eng.tensor_tensor(self.low[:, unit % LOWS, :], self.ring[:, unit % RING, :],
                          self.high[:, unit % HIGHS, :].bitcast(F32), ALU.subtract).then_inc(
                              self.unit_ready[unit % LOWS], 1)

    def unit_parts(self, unit, lo, hi):
        return self.high[:, unit % HIGHS, lo:hi], self.low[:, unit % LOWS, lo:hi]

    def take_units(self, n):
        u = self.units
        self.units += n
        return u


def shaped(v, *dims):
    names = "abcdef"[:len(dims)]
    if len(dims) == 1:
        return v
    return v.rearrange(f"p ({' '.join(names)}) -> p {' '.join(names)}",
                       **{c: d for c, d in zip(names[1:], dims[1:])})


def spread(v, axis, n):
    names = list("abcdef"[:len(v.shape) - 1])
    before, after = names[:axis - 1], names[axis - 1:]
    if after:
        old = before + [f"(z {after[0]})"] + after[1:]
    else:
        old = before[:-1] + [f"({before[-1]} z)"]
    grown = v.rearrange(f"p {' '.join(old)} -> p {' '.join(before + ['z'] + after)}", z=1)
    shape = list(grown.shape)
    shape[axis] = n
    return grown.to_broadcast(shape)


def parts(pair, *cut):
    return tuple(v[cut] for v in pair)


def product(pe, out, lhsT, rhs, start, stop):
    pe.matmul(out, lhsT[0], rhs[0], start=start, stop=False)
    pe.matmul(out, lhsT[0], rhs[1], start=False, stop=False)
    return pe.matmul(out, lhsT[1], rhs[0], start=False, stop=stop)




class Stage:

    def __init__(self, core):
        self.core = core
        self.index = core.counted
        core.counted += 1
        core.stages.append(self)
        self.needs = []
        self.chained = False
        self.plan()

    def plan(self):
        pass

    def enter(self, eng):
        if self.index:
            eng.wait_ge(self.core.stage_done, self.index)
        for job in self.needs:
            job.needed(eng)

    def enter_products(self, pe):
        before = next(s for s in self.core.stages if isinstance(s, Stage) and s.index == self.index - 1)
        self.halved = isinstance(before, (NormSplit, TransposeSplit)) and before.split and not self.needs
        if self.halved:
            pe.wait_ge(before.half_ready.sem, before.half_ready0 + 1)
        else:
            self.enter(pe)

    def second_half(self, pe):
        if self.halved:
            self.enter(pe)

    def after(self, *jobs):
        self.needs += jobs
        return self

    def tensor(self, pe):
        pass

    def vector(self, dve, own):
        pass

    def scalar(self, act, own):
        pass

    def gpsimd(self, pool, own):
        pass


    def ready(self, pe, unit, i=0):
        pe.wait_ge(self.core.unit_ready[unit % LOWS], i * (PERIOD // LOWS) + unit // LOWS + 1)


    def round_next(self, act, n, i=0):
        self.core.round_unit(act, n + HIGHS, i)

    def remainder_next(self, dve, n, i=0):
        self.core.take_remainder(dve, n + LOWS, i)

    def weights_end(self):
        return self.unit0 + self.unit_count

    def feeding(self):
        self.chained = True
        return self

    def last_remainders(self, pool, first):
        for unit in range(first, self.weights_end() + LOWS):
            self.core.take_remainder(pool, unit)


def take_in(c, act, own, func):
    own.settle()
    own.step(act.activation(c.small[:, 3:4], c.const[:, 0:1], func))


class Load(Stage):

    def scalar(self, act, own):
        c = self.core
        loaded = c.inputs_loaded
        act.dma_start(c.x[:, :, :], c.dram["x"].rearrange("(t p) d -> p t d", p=P)).then_inc(loaded, 16)
        act.dma_start(c.const[:, :], c.dram["const"]).then_inc(loaded, 16)
        act.dma_start(c.cols[:, :], c.dram["cols"]).then_inc(loaded, 16)
        act.wait_ge(loaded, 48)
        act.activation(c.small[:, 1:2], c.const[:, 0:1], ACT.Copy).then_inc(c.stage_done, 1)


class FirstUnits:

    def __init__(self, core):
        self.core = core

    def vector(self, dve, own):
        for unit in range(LOWS):
            self.core.take_remainder(dve, unit)

    def scalar(self, act, own):
        for unit in range(HIGHS):
            self.core.round_unit(act, unit)

    def gpsimd(self, pool, own):
        pass

    def tensor(self, pe):
        pass


class Prefetch:

    def __init__(self, core, name, dst, src, ahead=0, slow=False):
        self.core, self.dst, self.src, self.slow = core, dst, src, slow
        at = max(len(core.stages) - ahead, 0)
        self.index = core.stages[at].index if at < len(core.stages) else core.counted
        core.stages.insert(at, self)
        self.loaded = core.counter(name + "_loaded")
        self.loaded0 = self.loaded.reserve(16)

    def gpsimd(self, pool, own):
        if self.index:
            pool.wait_ge(self.core.stage_done, self.index)
        pool.dma_start(self.dst, self.src, allow_slow_non_contiguous=self.slow).then_inc(self.loaded.sem, 16)

    def needed(self, eng):
        eng.wait_ge(self.loaded.sem, self.loaded0 + 16)

    def scalar(self, act, own):
        pass

    def vector(self, dve, own):
        pass

    def tensor(self, pe):
        pass


def prefetch_row(c, name, place, row, ahead):
    return Prefetch(c, name, c.rows_at(place), c.dram["rows"][row:row + 1, :].to_broadcast([P, D]), ahead)


class Transpose(Stage):

    def __init__(self, core, src, dst, chunks, gain=None):
        self.src, self.dst, self.chunks, self.gain = src, dst, chunks, gain
        super().__init__(core)

    def plan(self):
        self.groups = [(t, c0, min(4, self.chunks - c0)) for c0 in range(0, self.chunks, 4) for t in range(TT)]
        self.turned = self.core.counter("tile_transposed")
        self.turned0 = self.turned.reserve(len(self.groups))
        self.plan_copies()

    def plan_copies(self):
        self.copied = self.core.counter("transpose_copied")
        self.copied0 = self.copied.reserve(len(self.groups) - 1)

    def tensor(self, pe):
        c = self.core
        self.enter(pe)
        for g, (t, c0, n) in enumerate(self.groups):
            if g >= 4:
                pe.wait_ge(self.copied.sem, self.copied0 + g - 3)
            for k in range(n):
                last = pe.transpose(c.bank[:, g % 4, k * P:(k + 1) * P],
                                    self.src[:, t, (c0 + k) * P:(c0 + k + 1) * P], c.tables["ident"])
            last.then_inc(self.turned.sem, 1)

    def vector(self, dve, own):
        c = self.core
        self.enter(dve)
        for g, (t, c0, n) in enumerate(self.groups):
            dve.wait_ge(self.turned.sem, self.turned0 + g + 1)
            out = self.dst[:, c0:c0 + n, t * P:(t + 1) * P]
            got = shaped(c.bank[:, g % 4, 0:n * P], n, P)
            if self.gain is None:
                last = dve.tensor_copy(out, got)
            else:
                last = dve.tensor_tensor(out, got, spread(self.gain[:, c0:c0 + n], 2, P), ALU.mult)
            final = g == len(self.groups) - 1
            last.then_inc(c.stage_done if final else self.copied.sem, 1)


class TransposeSplit(Transpose):

    def __init__(self, core, src, chunks=KD, gain=None, at=0, held=28672):
        self.held = core.at(held, 4, 512)
        super().__init__(core, src, parts(core.xT, slice(None), slice(at, at + chunks)), chunks, gain)

    def plan(self):
        super().plan()
        n = len(self.groups)
        self.gained = self.core.counter("transpose_gained")
        self.gained0 = self.gained.reserve(n if self.gain is not None else 0)
        self.rounded = self.core.counter("transpose_rounded")
        self.rounded0 = self.rounded.reserve(n)
        self.half_ready = self.core.counter("operand_half_ready")
        self.half_ready0 = self.half_ready.reserve(1 if self.split else 0)

    def plan_copies(self):
        self.split = len(self.groups) == 2 * TT
        self.copied = self.core.counter("transpose_copied")
        self.copied0 = self.copied.reserve(len(self.groups) - (2 if self.split else 1))

    def value(self, g):
        n = self.groups[g][2]
        if self.gain is None:
            return shaped(self.core.bank[:, g % 4, 0:n * P], n, P)
        return shaped(self.held[:, g % 4, 0:n * P], n, P)

    def out(self, g, part):
        t, c0, n = self.groups[g]
        return self.dst[part][:, c0:c0 + n, t * P:(t + 1) * P]

    def scalar(self, act, own):
        self.enter(act)
        for g in range(len(self.groups)):
            if self.gain is None:
                act.wait_ge(self.turned.sem, self.turned0 + g + 1)
            else:
                act.wait_ge(self.gained.sem, self.gained0 + g + 1)
            act.activation(self.out(g, 0), self.value(g), ACT.Copy).then_inc(self.rounded.sem, 1)

    def vector(self, dve, own):
        c, count = self.core, len(self.groups)
        self.enter(dve)

        def apply_gain(g):
            _, c0, n = self.groups[g]
            dve.wait_ge(self.turned.sem, self.turned0 + g + 1)
            dve.tensor_tensor(self.value(g), shaped(c.bank[:, g % 4, 0:n * P], n, P),
                              spread(self.gain[:, c0:c0 + n], 2, P), ALU.mult).then_inc(self.gained.sem, 1)

        if self.gain is not None:
            apply_gain(0)
        for g in range(count):
            if self.gain is not None and g + 1 < count:
                apply_gain(g + 1)
            dve.wait_ge(self.rounded.sem, self.rounded0 + g + 1)
            dve.tensor_tensor(self.out(g, 1), self.value(g), self.out(g, 0).bitcast(F32), ALU.subtract).then_inc(
                c.stage_done if g == count - 1 else self.half_ready.sem if self.split and g == TT - 1 else
                self.copied.sem, 1)


class SplitOperand(Stage):

    def __init__(self, core, src, at):
        self.src, self.dst = src, parts(core.xT, slice(None), slice(at, at + src.shape[1]))
        super().__init__(core)

    def plan(self):
        self.rounded = self.core.counter("operand_rounded")
        self.rounded0 = self.rounded.reserve(1)

    def scalar(self, act, own):
        self.enter(act)
        act.activation(self.dst[0], self.src, ACT.Copy).then_inc(self.rounded.sem, 1)

    def vector(self, dve, own):
        self.enter(dve)
        dve.wait_ge(self.rounded.sem, self.rounded0 + 1)
        dve.tensor_tensor(self.dst[1], self.src, self.dst[0].bitcast(F32), ALU.subtract).then_inc(
            self.core.stage_done, 1)


class Norm(Stage):

    def __init__(self, core, entries, kind, eps, measured=False):
        self.entries, self.kind, self.eps, self.given = entries, kind, eps, measured
        super().__init__(core)

    def plan(self):
        c = self.core
        self.measured = c.counter("moments_ready")
        self.measured0 = self.measured.reserve(1)
        self.rooted = c.counter("root_ready")
        self.rooted0 = self.rooted.reserve(1)

    def scalar(self, act, own):
        c, n = self.core, len(self.entries)
        self.enter(act)
        take_in(c, act, own, ACT.Sqrt)
        act.wait_ge(self.measured.sem, self.measured0 + 1)
        act.activation(c.root[:, 0:n], c.power[:, 0:n], ACT.Sqrt).then_inc(self.rooted.sem, 1)

    def vector(self, dve, own):
        c, n = self.core, len(self.entries)
        self.enter(dve)
        for e, (src, _) in enumerate([] if self.given else self.entries):
            width = src.shape[-1]
            for k in range(0, width, 512):
                own.step(dve.bn_stats(c.stats[:, e, k // 512, :], src[:, k:min(k + 512, width)]))
        own.settle()
        for e, (src, _) in enumerate(self.entries):
            parts = -(-src.shape[-1] // 512)
            own.step(dve.bn_aggr(c.moments[:, e, :], shaped(c.stats[:, e, 0:parts, :].rearrange("p a b -> p (a b)"), 6 * parts)))
        own.settle()
        mean, var = c.moments[:, 0:n, 0], c.moments[:, 0:n, 1]
        if self.kind == "rms":
            own.step(dve.tensor_tensor(c.square[:, 0:n], mean, mean, ALU.mult))
            own.settle()
            dve.scalar_tensor_tensor(c.power[:, 0:n], c.square[:, 0:n], self.eps, var,
                                     ALU.add, ALU.add).then_inc(self.measured.sem, 1)
        else:
            dve.tensor_scalar(c.power[:, 0:n], var, self.eps, None, ALU.add).then_inc(self.measured.sem, 1)
        dve.wait_ge(self.rooted.sem, self.rooted0 + 1)
        own.step(dve.reciprocal(c.rstd[:, 0:n], c.root[:, 0:n]))
        own.settle()
        outs = []
        for e, (src, dst) in enumerate(self.entries):
            if self.kind == "rms":
                outs.append((dve.tensor_scalar, (dst, src, c.rstd[:, e:e + 1], None, ALU.mult)))
            else:
                outs.append((dve.tensor_scalar, (dst, src, c.moments[:, e, 0:1], c.rstd[:, e:e + 1],
                                                 ALU.subtract, ALU.mult)))
        for fn, args in outs[:-1]:
            own.step(fn(*args))
        fn, args = outs[-1]
        fn(*args).then_inc(c.stage_done, 1)


class NormSplit(Stage):

    def __init__(self, core, kind, eps, y, gain, bias=None, split=True):
        self.kind, self.eps, self.y, self.gain, self.bias, self.split = kind, eps, y, gain, bias, split
        self.squares = core.at(26624, D)
        super().__init__(core)

    def plan(self):
        c = self.core
        self.quarters = [(t, slice(h * PIECE, (h + 1) * PIECE), h) for h in range(2) for t in range(TT)]
        self.squared = c.counter("tile_squared")
        self.squared0 = self.squared.reserve(1 if self.kind == "rms" else 0)
        self.measured = c.counter("moments_ready")
        self.measured0 = self.measured.reserve(1)
        self.rooted = c.counter("root_ready")
        self.rooted0 = self.rooted.reserve(1)
        if not self.split:
            return
        self.normed = c.counter("quarter_normed")
        self.normed0 = self.normed.reserve(4)
        self.turned = c.counter("tile_transposed")
        self.turned0 = self.turned.reserve(4)
        self.rounded = c.counter("transpose_rounded")
        self.rounded0 = self.rounded.reserve(4)
        self.half_ready = c.counter("operand_half_ready")
        self.half_ready0 = self.half_ready.reserve(1)

    def tensor(self, pe):
        c = self.core
        if not self.split:
            return
        self.enter(pe)
        for q, (t, cut, h) in enumerate(self.quarters):
            pe.wait_ge(self.normed.sem, self.normed0 + q + 1)
            for k in range(4):
                last = pe.transpose(c.bank[:, q, k * P:(k + 1) * P], self.y[:, t, (4 * h + k) * P:(4 * h + k + 1) * P],
                                    c.tables["ident"])
            last.then_inc(self.turned.sem, 1)

    def out(self, q, part):
        t, _, h = self.quarters[q]
        return self.core.xT[part][:, 4 * h:4 * h + 4, t * P:(t + 1) * P]

    def scalar(self, act, own):
        c = self.core
        self.enter(act)
        if self.kind == "rms":
            act.activation(self.squares, c.x[:, 1, :], ACT.Square, scale=D ** -0.5,
                           accum_out=c.power[:, 1:2]).then_inc(self.squared.sem, 1)
        act.wait_ge(self.measured.sem, self.measured0 + 1)
        act.activation(c.root[:, 0:2], c.power[:, 0:2], ACT.Sqrt).then_inc(self.rooted.sem, 1)
        for q in range(4 if self.split else 0):
            act.wait_ge(self.turned.sem, self.turned0 + q + 1)
            act.activation(self.out(q, 0), shaped(c.bank[:, q, :], 4, P), ACT.Copy).then_inc(self.rounded.sem, 1)

    def vector(self, dve, own):
        c, rms = self.core, self.kind == "rms"
        self.enter(dve)
        mine = 1 if rms else TT
        for t in range(mine):
            for h in range(2):
                own.step(dve.bn_stats(c.stats[:, t, h, :], c.x[:, t, h * PIECE:(h + 1) * PIECE]))
        own.settle()
        for t in range(mine):
            own.step(dve.bn_aggr(c.moments[:, t, :], c.stats[:, t, :, :].rearrange("p a b -> p (a b)")))
        own.settle()
        mean, var = c.moments[:, 0:mine, 0], c.moments[:, 0:mine, 1]
        if rms:
            own.step(dve.tensor_tensor(c.square[:, 0:1], mean, mean, ALU.mult))
            own.settle()
            own.step(dve.tensor_tensor(c.power[:, 0:1], c.square[:, 0:1], var, ALU.add))
            own.settle()
            dve.wait_ge(self.squared.sem, self.squared0 + 1)
            dve.tensor_scalar(c.power[:, 0:2], c.power[:, 0:2], self.eps, None, ALU.add).then_inc(self.measured.sem, 1)
        else:
            dve.tensor_scalar(c.power[:, 0:2], var, self.eps, None, ALU.add).then_inc(self.measured.sem, 1)
            for t, cut, _ in self.quarters:
                own.step(dve.scalar_tensor_tensor(self.y[:, t, cut], c.x[:, t, cut], c.moments[:, t, 0:1],
                                                  self.gain[:, cut], ALU.subtract, ALU.mult))
        dve.wait_ge(self.rooted.sem, self.rooted0 + 1)
        own.step(dve.reciprocal(c.rstd[:, 0:2], c.root[:, 0:2]))
        own.settle()
        for t, cut, _ in self.quarters:
            y, rstd = self.y[:, t, cut], c.rstd[:, t:t + 1]
            if rms:
                last = dve.scalar_tensor_tensor(y, c.x[:, t, cut], rstd, self.gain[:, cut], ALU.mult, ALU.mult)
            else:
                last = dve.scalar_tensor_tensor(y, y, rstd, self.bias[:, cut], ALU.mult, ALU.add)
            if self.split:
                last.then_inc(self.normed.sem, 1)
            elif (t, cut, 1) != self.quarters[-1]:
                own.step(last)
        for q in range(4 if self.split else 0):
            dve.wait_ge(self.rounded.sem, self.rounded0 + q + 1)
            last = dve.tensor_tensor(self.out(q, 1), shaped(c.bank[:, q, :], 4, P), self.out(q, 0).bitcast(F32),
                                     ALU.subtract)
            if q == 1:
                last.then_inc(self.half_ready.sem, 1)
            elif q < 3:
                own.step(last)
        last.then_inc(c.stage_done, 1)


class TokenMajor(Stage):

    engine = "scalar"

    def __init__(self, core, lhs, kc, widths):
        self.lhs, self.kc, self.widths = lhs, kc, widths
        super().__init__(core)

    def plan(self):
        c = self.core
        self.blocks = len(self.widths)
        self.unit_count = -(-self.kc * self.blocks // 2)
        self.unit0 = c.take_units(self.unit_count)
        self.freed = c.counter("block_freed")
        self.freed0 = self.freed.reserve(self.blocks - 1)

    def ending(self, unit):
        return [b for b in range(self.blocks) if self.unit0 + (b * self.kc + self.kc - 1) // 2 == unit]

    def tensor(self, pe):
        c = self.core
        self.enter_products(pe)
        pieces = self.kc * self.blocks
        for b, width in enumerate(self.widths):
            if b >= 2:
                pe.wait_ge(self.freed.sem, self.freed0 + b - 1)
            for k in range(self.kc):
                f = b * self.kc + k
                unit = self.unit0 + f // 2
                if f % 2 == 0:
                    self.ready(pe, unit)
                if f == KD // 2:
                    self.second_half(pe)
                w = c.unit_parts(unit, (f % 2) * PIECE, (f % 2) * PIECE + width)
                for t in range(TT):
                    mm = product(pe, c.acc[:, t, (b % 2) * PIECE:(b % 2) * PIECE + width],
                                 parts(self.lhs, slice(None), k, slice(t * P, (t + 1) * P)), w,
                                 start=(k == 0), stop=(k == self.kc - 1))
                if f % 2 == 1 or f == pieces - 1:
                    mm.then_inc(c.units_multiplied, 1)

    def evacuate(self, eng, own, b):
        c, width = self.core, self.widths[b]
        for t in range(TT):
            got = c.acc[:, t, (b % 2) * PIECE:(b % 2) * PIECE + width]
            last = self.keep(eng, own, b, t, got)
            if t < TT - 1:
                own.step(last)
        last.then_inc(c.stage_done if b == self.blocks - 1 else self.freed.sem, 1)

    def scalar(self, act, own):
        self.enter(act)
        if self.engine == "vector":
            take_in(self.core, act, own, ACT.Sqrt)
        for unit in range(self.unit0, self.weights_end()):
            if unit < self.weights_end() - 1:
                self.round_next(act, unit)
            if self.engine == "scalar":
                for b in self.ending(unit):
                    act.wait_ge(self.core.units_multiplied, unit + 1)
                    self.evacuate(act, own, b)
        self.round_next(act, self.weights_end() - 1)

    def vector(self, dve, own):
        self.enter(dve)
        for unit in range(self.unit0, self.weights_end()):
            if self.chained or unit + LOWS < self.weights_end():
                self.remainder_next(dve, unit)
            if self.engine == "vector":
                for b in self.ending(unit):
                    dve.wait_ge(self.core.units_multiplied, unit + 1)
                    self.evacuate(dve, own, b)

    def gpsimd(self, pool, own):
        if not self.chained:
            self.last_remainders(pool, max(self.weights_end(), self.unit0 + LOWS))


class Project(TokenMajor):

    def __init__(self, core, lhs, kc, widths, dst, funcs=None):
        self.dst = dst
        self.funcs = funcs or [ACT.Copy] * len(widths)
        super().__init__(core, lhs, kc, widths)

    def keep(self, act, own, b, t, got):
        return act.activation(self.dst[:, t, b * PIECE:b * PIECE + got.shape[-1]], got, self.funcs[b])


class AddTo(TokenMajor):

    engine = "vector"

    def __init__(self, core, lhs, kc, x_scale=1.0):
        self.x_scale = x_scale
        super().__init__(core, lhs, kc, [PIECE] * (D // PIECE))

    def keep(self, dve, own, b, t, got):
        x = self.core.x[:, t, b * PIECE:(b + 1) * PIECE]
        return dve.scalar_tensor_tensor(x, x, self.x_scale, got, ALU.mult, ALU.add)


class GatedAdd(TokenMajor):

    engine = "vector"

    def __init__(self, core, lhs, kc, gate, product):
        self.gate, self.product = gate, product
        super().__init__(core, lhs, kc, [PIECE] * (D // PIECE))

    def keep(self, dve, own, b, t, got):
        cut = slice(b * PIECE, (b + 1) * PIECE)
        own.step(dve.tensor_tensor(self.product[:, t, cut], got, self.gate[:, t, cut], ALU.mult))
        own.settle()
        x = self.core.x[:, t, cut]
        return dve.tensor_tensor(x, x, self.product[:, t, cut], ALU.add)


class FeatureMajor(Stage):

    def __init__(self, core, rhs, kc, chunks, dst, scales=None):
        self.rhs, self.kc, self.chunks, self.dst = rhs, kc, chunks, dst
        self.scales = scales or [1.0] * chunks
        super().__init__(core)

    def plan(self):
        c = self.core
        self.unit_count = -(-self.kc * self.chunks // 8)
        self.unit0 = c.take_units(self.unit_count)
        self.slots = 4 if self.kc == KD else 8
        assert self.kc == KD or self.chunks <= self.slots
        self.freed = c.counter("chunk_freed")
        self.freed0 = self.freed.reserve(self.chunks - 1)

    def tensor(self, pe):
        c = self.core
        self.enter_products(pe)
        pieces = self.kc * self.chunks
        for j in range(self.chunks):
            if j >= self.slots:
                pe.wait_ge(self.freed.sem, self.freed0 + j - self.slots + 1)
            for k in range(self.kc):
                f = j * self.kc + k
                unit = self.unit0 + f // 8
                if f % 8 == 0:
                    self.ready(pe, unit)
                if f == KD // 2:
                    self.second_half(pe)
                mm = product(pe, self.slot(j), c.unit_parts(unit, (f % 8) * P, (f % 8 + 1) * P),
                             parts(self.rhs, slice(None), k), start=(k == 0), stop=(k == self.kc - 1))
                if f % 8 == 7 or f == pieces - 1:
                    mm.then_inc(c.units_multiplied, 1)

    def slot(self, j):
        if self.kc == KD:
            return self.core.bank[:, j % 4, 0:SEQ]
        return self.core.bank[:, j // 2, (j % 2) * SEQ:(j % 2 + 1) * SEQ]

    def last_unit(self, j):
        return self.unit0 + (j * self.kc + self.kc - 1) // 8

    def scalar(self, act, own):
        c = self.core
        self.enter(act)
        for unit in range(self.unit0, self.weights_end()):
            if unit < self.weights_end() - 1:
                self.round_next(act, unit)
            for j in range(self.chunks):
                if self.last_unit(j) == unit:
                    act.wait_ge(c.units_multiplied, unit + 1)
                    act.activation(self.dst[:, j, :], self.slot(j), ACT.Copy, scale=self.scales[j]).then_inc(
                        c.stage_done if j == self.chunks - 1 else self.freed.sem, 1)
        self.round_next(act, self.weights_end() - 1)

    def vector(self, dve, own):
        self.enter(dve)
        for unit in range(self.unit0, self.weights_end() - (0 if self.chained else LOWS)):
            self.remainder_next(dve, unit)

    def gpsimd(self, pool, own):
        if not self.chained:
            self.last_remainders(pool, max(self.weights_end(), self.unit0 + LOWS))


class ExpertLoop(Stage):

    def __init__(self, core, chunks, firsts, func, x_scale, out_scale, gates=None, begun=False):
        self.chunks, self.firsts, self.func, self.begun = chunks, firsts, func, begun
        self.x_scale, self.out_scale, self.gates = x_scale, out_scale, gates
        super().__init__(core)

    def plan(self):
        c = self.core
        self.per = self.firsts + 1
        self.unit_count = self.per * self.chunks
        self.unit0 = c.take_units(self.unit_count)
        self.body = PERIOD // self.per
        assert (self.chunks - 2) % self.body == 0 and self.body % 2 == 0
        self.activated = c.counter("chunk_activated")
        self.activated0 = self.activated.reserve(self.chunks)
        self.multiplied = c.counter("hidden_multiplied")
        self.multiplied0 = self.multiplied.reserve(self.chunks)
        self.rounded = c.counter("hidden_rounded")
        self.rounded0 = self.rounded.reserve(self.chunks)
        self.hidden = c.counter("hidden_ready")
        self.hidden0 = self.hidden.reserve(self.chunks)
        self.summed = c.counter("first_tile_summed")
        self.summed0 = self.summed.reserve(1)

    def first_unit(self, c):
        return self.unit0 + (self.per * c - 1 if c else 0)

    def last_unit(self, c):
        return self.unit0 + self.per * (c + 1) + self.firsts - 1 - (self.firsts if c == self.chunks - 1 else 0)

    def first_bank(self, c, a):
        return self.core.bank[:, (c % 2) * self.firsts + a, 0:SEQ]

    def tensor(self, pe):
        core = self.core
        self.enter_products(pe)

        def first_products(c, i=0):
            for a in range(self.firsts):
                unit = self.first_unit(c) + a
                self.ready(pe, unit, i)
                for k in range(KD):
                    if (c, a, k) == (0, 0, KD // 2):
                        self.second_half(pe)
                    mm = product(pe, self.first_bank(c, a), core.unit_parts(unit, k * P, (k + 1) * P),
                                 parts(core.xT, slice(None), k), start=(k == 0), stop=(k == KD - 1))
                mm.then_inc(core.units_multiplied, 1)

        def last_product(c, i=0):
            pe.wait_ge(self.hidden.sem, i * self.body + self.hidden0 + c + 1)
            unit = self.last_unit(c)
            self.ready(pe, unit, i)
            for t in range(TT):
                for h in range(2):
                    mm = product(pe, core.acc[:, t, h * PIECE:(h + 1) * PIECE],
                                 parts(core.hidden, slice(None), c % 2, slice(t * P, (t + 1) * P)),
                                 core.unit_parts(unit, h * PIECE, (h + 1) * PIECE),
                                 start=(c == 0 and not self.begun), stop=(c == self.chunks - 1))
                if c == self.chunks - 1 and t == 0:
                    mm.then_inc(self.summed.sem, 1)
            mm.then_inc(core.units_multiplied, 1)

        first_products(0)
        first_products(1)
        last_product(0)
        with pe.Fori(0, (self.chunks - 2) // self.body) as i:
            for c in range(1, 1 + self.body):
                first_products(c + 1, i)
                last_product(c, i)
        last_product(self.chunks - 1)

    def scalar(self, act, own):
        core = self.core
        self.enter(act)

        def firsts(c, i=0, steady=True):
            unit = self.first_unit(c)
            self.round_next(act, unit, i)
            act.wait_ge(core.units_multiplied, i * PERIOD + unit + 1)
            if steady:
                act.wait_ge(self.hidden.sem, i * self.body + self.hidden0 + c - 1)
            act.activation(core.activated[:, c % 2, :], self.first_bank(c, 0), self.func).then_inc(self.activated.sem, 1)
            for a in range(1, self.firsts):
                self.round_next(act, unit + a, i)

        firsts(0, steady=False)
        firsts(1, steady=False)
        self.round_next(act, self.last_unit(0))
        with act.Fori(0, (self.chunks - 2) // self.body) as i:
            for c in range(1, 1 + self.body):
                firsts(c + 1, i)
                self.round_next(act, self.last_unit(c), i)
        take_in(core, act, own, ACT.Sqrt)
        self.round_next(act, self.last_unit(self.chunks - 1))

    def vector(self, dve, own):
        core = self.core
        self.enter(dve)

        def hide(c, i=0, steady=True):
            unit = self.first_unit(c)
            dve.wait_ge(self.activated.sem, i * self.body + self.activated0 + c + 1)
            if self.gates is None:
                dve.wait_ge(core.units_multiplied, i * PERIOD + unit + 2)
                other = self.first_bank(c, 1)
            else:
                other = self.gates[:, :, bass.ds(i * self.body + c, 1)].rearrange("p t one -> p (t one)")
            value = core.activated[:, c % 2, :]
            dve.tensor_tensor(value, value, other, ALU.mult).then_inc(self.multiplied.sem, 1)
            dve.wait_ge(self.multiplied.sem, i * self.body + self.multiplied0 + c + 1)
            if steady:
                dve.wait_ge(core.units_multiplied, i * PERIOD + self.last_unit(c - 2) + 1)
            high, low = parts(core.hidden, slice(None), c % 2)
            dve.tensor_copy(high, value).then_inc(self.rounded.sem, 1)
            dve.wait_ge(self.rounded.sem, i * self.body + self.rounded0 + c + 1)
            dve.tensor_tensor(low, value, high.bitcast(F32), ALU.subtract).then_inc(self.hidden.sem, 1)

        def firsts(c, i=0, steady=True):
            for a in range(self.firsts):
                self.remainder_next(dve, self.first_unit(c) + a, i)
            hide(c, i, steady)

        firsts(0, steady=False)
        firsts(1, steady=False)
        self.remainder_next(dve, self.last_unit(0))
        with dve.Fori(0, (self.chunks - 2) // self.body) as i:
            for c in range(1, 1 + self.body):
                firsts(c + 1, i)
                self.remainder_next(dve, self.last_unit(c), i)
        dve.wait_ge(self.summed.sem, self.summed0 + 1)
        for t in range(TT):
            if t == 1:
                dve.wait_ge(core.units_multiplied, self.last_unit(self.chunks - 1) + 1)
            x = core.x[:, t, :]
            if self.out_scale != 1.0:
                last = dve.scalar_tensor_tensor(x, core.acc[:, t, :], self.out_scale, x, ALU.mult, ALU.add)
            else:
                last = dve.scalar_tensor_tensor(x, x, self.x_scale, core.acc[:, t, :], ALU.mult, ALU.add)
            if t < TT - 1:
                own.step(last)
        last.then_inc(core.stage_done, 1)

    def gpsimd(self, pool, own):
        self.last_remainders(pool, self.weights_end() + 1)


class KeyScores(Stage):

    def __init__(self, core, queries, subkeys, scores):
        self.queries, self.subkeys, self.scores = queries, subkeys, scores
        super().__init__(core)

    def plan(self):
        c = self.core
        self.scored = c.counter("key_scores_ready")
        self.scored0 = self.scored.reserve(8)
        self.kept = c.counter("key_scores_kept")
        self.kept0 = self.kept.reserve(7)

    def tensor(self, pe):
        c = self.core
        self.enter(pe)
        for g in range(8):
            t, q = g // 4, g % 4
            if g >= 4:
                pe.wait_ge(self.kept.sem, self.kept0 + g - 3)
            for j in range(4):
                mm = pe.matmul(c.bank[:, q, j * P:(j + 1) * P], self.queries[:, 4 * q + j, t * P:(t + 1) * P],
                               self.subkeys[:, 4 * q + j, :], start=True, stop=True)
            mm.then_inc(self.scored.sem, 1)

    def scalar(self, act, own):
        c = self.core
        self.enter(act)
        for g in range(8):
            t, q = g // 4, g % 4
            act.wait_ge(self.scored.sem, self.scored0 + g + 1)
            act.activation(self.scores[:, t, 4 * q:4 * q + 4, :], shaped(c.bank[:, q, :], 4, P), ACT.Copy).then_inc(
                c.stage_done if g == 7 else self.kept.sem, 1)


class Route(Stage):

    def __init__(self, core, scores, routes, scratch, store):
        self.scores, self.routes, self.scratch, self.store = scores, routes, scratch, store
        super().__init__(core)

    def plan(self):
        c = self.core
        self.shifted = c.counter("gates_shifted")
        self.shifted0 = self.shifted.reserve(1)
        self.exped = c.counter("gates_exponentiated")
        self.exped0 = self.exped.reserve(1)
        self.unit_count = self.ahead = self.store.shape[1]
        self.unit0 = c.take_units(self.unit_count)
        self.activated = c.counter("chunk_activated")
        self.activated0 = self.activated.reserve(self.ahead)
        rows, n = 2 * 16, TOPK
        self.rest = c.at(0, rows, P)
        self.sums_rest = c.at(0, rows // 2, n * n)
        at = self.scratch

        def take(*dims):
            nonlocal at
            v = c.at(at, *dims)
            at += int(np.prod(dims))
            return v

        self.best = take(rows, n)
        self.best_at = take(rows, n).bitcast(U32)
        self.keys = take(TT, PEER_HEADS, 2, n)
        self.sums = take(rows // 2, n * n)
        self.top = take(rows // 2, n)
        self.top_at = take(rows // 2, n).bitcast(U32)
        self.part_at = take(2, rows // 2 * n).bitcast(U32)
        self.part = take(2, rows // 2, n)
        self.shift = take(rows // 2, n)
        self.gate = take(rows // 2, n)
        self.total = take(1, rows // 2)
        self.inverse = take(1, rows // 2)

    def top16(self, dve, own, values, rest, best, best_at, rows):
        for r in range(rows):
            own.step(dve.max(best[:, r, 0:8], values[:, r, :]))
        own.settle()
        for r in range(rows):
            own.step(dve.max_index(best_at[:, r, 0:8], best[:, r, 0:8], values[:, r, :]))
            own.step(dve.match_replace(rest[:, r, :], best[:, r, 0:8], values[:, r, :], MARK))
        own.settle()
        for r in range(rows):
            own.step(dve.max(best[:, r, 8:16], rest[:, r, :]))
        own.settle()
        for r in range(rows):
            own.step(dve.max_index(best_at[:, r, 8:16], best[:, r, 8:16], rest[:, r, :]))
        own.settle()

    def vector(self, dve, own):
        c, n, groups = self.core, TOPK, TT * PEER_HEADS
        self.enter(dve)
        values = self.scores.rearrange("p t h k -> p (t h) k")
        self.top16(dve, own, values, self.rest, self.best, self.best_at, 2 * groups)
        keys = self.keys.rearrange("p t h s n -> p (t h) s n")
        own.step(dve.tensor_copy(keys.rearrange("p g s n -> p (g s n)"), self.best_at.rearrange("p r n -> p (r n)")))
        pair = self.best.rearrange("p (g s) n -> p g s n", s=2)
        sums = self.sums.rearrange("p g (a b) -> p g a b", a=n)
        own.step(dve.tensor_tensor(sums, spread(pair[:, :, 0, :], 3, n), spread(pair[:, :, 1, :], 2, n), ALU.add))
        own.settle()
        self.top16(dve, own, self.sums, self.sums_rest, self.top, self.top_at, groups)
        dve.tensor_tensor(self.shift, self.top, self.top[:, :, 0:1].to_broadcast([P, groups, n]),
                          ALU.subtract).then_inc(self.shifted.sem, 1)
        flat = self.top_at.rearrange("p g n -> p (g n)")
        own.step(dve.tensor_single_scalar(self.part_at[:, 0, :], flat, 4, ALU.logical_shift_right))
        own.step(dve.tensor_single_scalar(self.part_at[:, 1, :], flat, n - 1, ALU.bitwise_and))
        own.settle()
        own.step(dve.tensor_copy(self.part.rearrange("p s g n -> p (s g n)"),
                                 self.part_at.rearrange("p s m -> p (s m)")))
        own.settle()
        hit = self.sums.rearrange("p g (r a) -> p g r a", r=n)
        iota = c.tables["iota"][:, 0:n]
        for s in range(2):
            own.step(dve.tensor_tensor(hit, spread(self.part[:, s, :, :], 3, n),
                                       spread(spread(iota, 1, n), 1, groups), ALU.is_equal))
            own.settle()
            own.step(dve.tensor_tensor(hit, hit, spread(keys[:, :, s, :], 2, n), ALU.mult))
            own.settle()
            for t in range(TT):
                g = slice(t * PEER_HEADS, (t + 1) * PEER_HEADS)
                own.step(dve.tensor_reduce(self.routes[:, t, 1 + s, :].rearrange("p (g r) -> p g r", r=n),
                                           hit[:, g, :, :], AX, ALU.add))
            own.settle()
        dve.wait_ge(self.exped.sem, self.exped0 + 1)
        own.step(dve.tensor_reduce(self.total[:, 0, :], self.gate, AX, ALU.add))
        own.settle()
        own.step(dve.reciprocal(self.inverse[:, 0, :], self.total[:, 0, :]))
        own.settle()
        for t in range(TT):
            g = slice(t * PEER_HEADS, (t + 1) * PEER_HEADS)
            last = dve.tensor_tensor(self.routes[:, t, 0, :].rearrange("p (g r) -> p g r", r=n), self.gate[:, g, :],
                                     spread(self.inverse[:, 0, g], 2, n), ALU.mult)
            own.step(last)
        own.settle()
        dve.wait_ge(self.activated.sem, self.activated0 + self.ahead)
        dve.tensor_copy(c.small[:, 0:1], c.const[:, 0:1]).then_inc(c.stage_done, 1)

    def tensor(self, pe):
        c = self.core
        self.enter(pe)

        def first_products(n, i=0, steady=True):
            if steady:
                pe.wait_ge(self.activated.sem, i * PERIOD + self.activated0 + n - 3)
            unit = self.unit0 + n
            self.ready(pe, unit, i)
            for k in range(KD):
                mm = product(pe, c.bank[:, n % 4, 0:SEQ], c.unit_parts(unit, k * P, (k + 1) * P),
                             parts(c.xT, slice(None), k), start=(k == 0), stop=(k == KD - 1))
            mm.then_inc(c.units_multiplied, 1)

        for n in range(PERIOD):
            first_products(n, steady=n >= 4)
        with pe.Fori(0, self.ahead // PERIOD - 1) as i:
            for n in range(PERIOD, 2 * PERIOD):
                first_products(n, i)

    def scalar(self, act, own):
        c = self.core
        self.enter(act)

        def activate(n, i=0):
            unit = self.unit0 + n
            self.round_next(act, unit, i)
            act.wait_ge(c.units_multiplied, i * PERIOD + unit + 1)
            act.activation(self.store[:, bass.ds(i * PERIOD + n, 1), :].rearrange("p one t -> p (one t)"),
                           c.bank[:, n % 4, 0:SEQ], ACT.Gelu_apprx_tanh).then_inc(self.activated.sem, 1)

        with act.Fori(0, self.ahead // PERIOD - 1) as i:
            for n in range(PERIOD):
                activate(n, i)
        act.wait_ge(self.shifted.sem, self.shifted0 + 1)
        act.activation(self.gate, self.shift, ACT.Exp).then_inc(self.exped.sem, 1)
        for n in range(self.ahead - PERIOD, self.ahead):
            activate(n)

    def gpsimd(self, pool, own):
        with pool.Fori(0, self.ahead // PERIOD) as i:
            for n in range(PERIOD):
                self.core.take_remainder(pool, self.unit0 + n + LOWS, i)


class SpreadGates(Stage):

    BATCH, PAIR = 4, 2
    BODY = 4

    def __init__(self, core, routesT, onehots, gates, store):
        self.routesT, self.onehots, self.gates, self.store = routesT, onehots, gates, store
        super().__init__(core)

    def plan(self):
        c = self.core
        self.batches = n = SEQ // self.BATCH
        self.pairs = 2 * n
        self.matched = c.counter("onehots_matched")
        self.matched0 = self.matched.reserve(2 * n)
        self.gated = c.counter("onehots_gated")
        self.gated0 = self.gated.reserve(2 * n)
        self.placed = c.counter("pairs_placed")
        self.placed0 = self.placed.reserve(2 * n)
        self.kept = c.counter("gates_kept")
        self.kept0 = self.kept.reserve(n)
        self.applied = c.counter("gates_applied")
        self.applied0 = self.applied.reserve(n - 1)

    def vector(self, dve, own):
        c, n, pairs = self.core, self.BATCH, 2 * self.BODY
        self.enter(dve)
        iota = spread(c.tables["iota"], 1, self.PAIR)

        def match(p, i=0, steady=True):
            if steady:
                dve.wait_ge(self.placed.sem, i * pairs + self.placed0 + p - 3)
            for key, out in ((1, self.onehots[p % 4][0]), (2, self.onehots[p % 4][1])):
                keys = self.routesT[:, key, bass.ds(i * (self.BODY * n) + p * self.PAIR, self.PAIR)]
                last = dve.tensor_tensor(out, iota, spread(keys, 2, P), ALU.is_equal)
            last.then_inc(self.matched.sem, 1)

        def apply(b, i=0, sem=None):
            dve.wait_ge(self.kept.sem, i * self.BODY + self.kept0 + b + 1)
            value = self.store[:, :, bass.ds(i * (self.BODY * n) + b * n, n)]
            got = c.bank[:, b % 4, :].rearrange("p (t k) -> p k t", t=n)[:, 0:AHEAD, :]
            dve.tensor_tensor(value, value, got, ALU.mult).then_inc(sem or self.applied.sem, 1)

        for p in range(6):
            match(p, steady=p >= 4)
        with dve.Fori(0, (self.batches - self.BODY) // self.BODY) as i:
            for b in range(self.BODY):
                match(2 * b + 6, i)
                match(2 * b + 7, i)
                apply(b, i)
        for b in range(self.batches - self.BODY, self.batches):
            for p in (2 * b + 6, 2 * b + 7):
                if p < self.pairs:
                    match(p)
            apply(b, sem=c.stage_done if b == self.batches - 1 else None)

    def tensor(self, pe):
        c, n = self.core, self.PAIR
        self.enter(pe)

        def place(b, i=0, steady=True):
            if steady:
                pe.wait_ge(self.applied.sem, i * self.BODY + self.applied0 + b - 3)
            for p in (2 * b, 2 * b + 1):
                pe.wait_ge(self.gated.sem, i * (2 * self.BODY) + self.gated0 + p + 1)
                first, second = self.onehots[p % 4]
                for t in range(n):
                    at = (p % 2 * n + t) * P
                    mm = pe.matmul(c.bank[:, b % 4, at:at + P], first[:, t, :], second[:, t, :].bitcast(F32),
                                   start=True, stop=True)
                mm.then_inc(self.placed.sem, 1)

        for b in range(self.BODY):
            place(b, steady=False)
        with pe.Fori(0, self.batches // self.BODY - 1) as i:
            for b in range(self.BODY, 2 * self.BODY):
                place(b, i)

    def scalar(self, act, own):
        c, n, pairs = self.core, self.BATCH, 2 * self.BODY
        self.enter(act)

        def gate(p, i=0):
            act.wait_ge(self.matched.sem, i * pairs + self.matched0 + p + 1)
            first = self.onehots[p % 4][0]
            for t in range(self.PAIR):
                token = i * (self.BODY * n) + p * self.PAIR + t
                last = act.activation(first[:, t, :], first[:, t, :], ACT.Copy,
                                      scale=self.routesT[:, 0, bass.ds(token, 1)])
            last.then_inc(self.gated.sem, 1)

        def keep(b, i=0):
            act.wait_ge(self.placed.sem, i * pairs + self.placed0 + 2 * b + 2)
            act.activation(self.gates[:, bass.ds(i * (self.BODY * n) + b * n, n), :],
                           shaped(c.bank[:, b % 4, :], n, P)[:, :, AHEAD:], ACT.Copy).then_inc(self.kept.sem, 1)

        for p in range(3):
            gate(p)
        with act.Fori(0, self.batches // self.BODY - 1) as i:
            for b in range(self.BODY):
                gate(2 * b + 3, i)
                keep(b, i)
                gate(2 * b + 4, i)
        for b in range(self.batches - self.BODY, self.batches):
            if 2 * b + 3 < self.pairs:
                gate(2 * b + 3)
            keep(b)
            if 2 * b + 4 < self.pairs:
                gate(2 * b + 4)


class StoredChunks(Stage):

    def __init__(self, core, store):
        self.store = store
        super().__init__(core)

    def plan(self):
        c = self.core
        self.unit_count = self.store.shape[1]
        self.unit0 = c.take_units(self.unit_count)
        self.rounded = c.counter("hidden_rounded")
        self.rounded0 = self.rounded.reserve(self.unit_count)
        self.hidden = c.counter("hidden_ready")
        self.hidden0 = self.hidden.reserve(self.unit_count)

    def tensor(self, pe):
        core = self.core
        self.enter(pe)

        def last_product(c, i=0, start=False):
            pe.wait_ge(self.hidden.sem, i * PERIOD + self.hidden0 + c + 1)
            unit = self.unit0 + c
            self.ready(pe, unit, i)
            for t in range(TT):
                for h in range(2):
                    mm = product(pe, core.acc[:, t, h * PIECE:(h + 1) * PIECE],
                                 parts(core.hidden, slice(None), c % 2, slice(t * P, (t + 1) * P)),
                                 core.unit_parts(unit, h * PIECE, (h + 1) * PIECE), start=start, stop=False)
            mm.then_inc(core.units_multiplied, 1)

        for c in range(PERIOD):
            last_product(c, start=(c == 0))
        with pe.Fori(0, self.unit_count // PERIOD - 1) as i:
            for c in range(PERIOD, 2 * PERIOD):
                last_product(c, i)

    def scalar(self, act, own):
        self.enter(act)
        with act.Fori(0, self.unit_count // PERIOD) as i:
            for c in range(PERIOD):
                self.round_next(act, self.unit0 + c, i)

    def vector(self, dve, own):
        core = self.core
        self.enter(dve)

        def hide(c, i=0, steady=True):
            value = self.store[:, bass.ds(i * PERIOD + c, 1), :].rearrange("p one t -> p (one t)")
            if steady:
                dve.wait_ge(core.units_multiplied, i * PERIOD + self.unit0 + c - 1)
            high, low = parts(core.hidden, slice(None), c % 2)
            dve.tensor_copy(high, value).then_inc(self.rounded.sem, 1)
            dve.wait_ge(self.rounded.sem, i * PERIOD + self.rounded0 + c + 1)
            dve.tensor_tensor(low, value, high.bitcast(F32), ALU.subtract).then_inc(self.hidden.sem, 1)

        hide(0, steady=False)
        hide(1, steady=False)
        with dve.Fori(0, self.unit_count // PERIOD - 1) as i:
            for c in range(PERIOD):
                hide(c + 2, i)
                self.remainder_next(dve, self.unit0 + c, i)
        for c in range(self.unit_count - PERIOD, self.unit_count):
            if c + 2 < self.unit_count:
                hide(c + 2)
            self.remainder_next(dve, self.unit0 + c)
        dve.wait_ge(core.units_multiplied, self.weights_end())
        dve.tensor_copy(core.small[:, 0:1], core.const[:, 0:1]).then_inc(core.stage_done, 1)


class Rotate(Stage):

    def __init__(self, core, views, r, cos, sin, products):
        self.views, self.r, self.cos, self.sin, self.products = views, r, cos, sin, products
        even = len({v.shape[2] for v in views}) == 1 and len(views) > 1
        self.theirs = [(views[-1], 1)] if even else [(v, 1) for v in views]
        self.mine = [(v, 0) for v in views] + ([(v, 1) for v in views[:-1]] if even else [])
        super().__init__(core)

    def plan(self):
        self.turned = self.core.counter("second_tile_rotated")
        self.turned0 = self.turned.reserve(1)

    def part(self, eng, own, pieces, at):
        r = self.r
        done = []
        for view, t in pieces:
            heads = view.shape[2]
            one, two = view[:, t, :, 0:r], view[:, t, :, r:2 * r]
            cos, sin = spread(self.cos[:, t, :], 1, heads), spread(self.sin[:, t, :], 1, heads)
            held = []
            for a, b in ((one, cos), (two, sin), (one, sin), (two, cos)):
                held.append(self.core.at(at, heads, r))
                at += heads * r
                own.step(eng.tensor_tensor(held[-1], a, b, ALU.mult))
            done += [(one, held[0], held[1], ALU.subtract), (two, held[2], held[3], ALU.add)]
        own.settle()
        for args in done[:-1]:
            own.step(eng.tensor_tensor(*args))
        return eng.tensor_tensor(*done[-1])

    def gpsimd(self, pool, own):
        self.enter(pool)
        size = sum(4 * v.shape[2] * self.r for v, _ in self.mine)
        self.part(pool, own, self.theirs, self.products + size).then_inc(self.turned.sem, 1)

    def vector(self, dve, own):
        self.enter(dve)
        own.step(self.part(dve, own, self.mine, self.products))
        dve.wait_ge(self.turned.sem, self.turned0 + 1)
        dve.tensor_copy(self.core.small[:, 0:1], self.core.const[:, 0:1]).then_inc(self.core.stage_done, 1)


class RetentionScores(Stage):

    HEADS, VD = 4, 512

    def __init__(self, core, qT, kT, v, decay, y, held):
        self.qT, self.kT, self.v, self.decay, self.y, self.held = qT, kT, v, decay, y, held
        super().__init__(core)

    def plan(self):
        c = self.core
        self.scored = c.counter("head_scored")
        self.scored0 = self.scored.reserve(self.HEADS)
        self.decayed = c.counter("head_decayed")
        self.decayed0 = self.decayed.reserve(self.HEADS)
        self.mixed = c.counter("head_mixed")
        self.mixed0 = self.mixed.reserve(self.HEADS)
        self.kept = c.counter("head_kept")
        self.kept0 = self.kept.reserve(self.HEADS)

    BLOCKS = ((0, 0), (0, 1), (1, 1))

    def tensor(self, pe):
        c = self.core
        self.enter(pe)

        def score(h):
            if h >= 2:
                pe.wait_ge(self.decayed.sem, self.decayed0 + h - 1)
            for n, (j, i) in enumerate(self.BLOCKS):
                for k in range(2):
                    mm = pe.matmul(c.bank[:, h % 2, n * P:(n + 1) * P], self.kT[:, 2 * h + k, j * P:(j + 1) * P],
                                   self.qT[:, 2 * h + k, i * P:(i + 1) * P], start=(k == 0), stop=(k == 1))
            mm.then_inc(self.scored.sem, 1)

        def mix(h):
            pe.wait_ge(self.decayed.sem, self.decayed0 + h + 1)
            if h >= 1:
                pe.wait_ge(self.kept.sem, self.kept0 + h)
            for n, (j, i) in enumerate(self.BLOCKS):
                mm = pe.matmul(c.bank[:, 2 + i, :], self.held[:, h % 2, n * P:(n + 1) * P],
                               self.v[:, j, h * self.VD:(h + 1) * self.VD], start=(j == 0), stop=(j == i))
            mm.then_inc(self.mixed.sem, 1)

        score(0)
        for h in range(self.HEADS):
            if h + 1 < self.HEADS:
                score(h + 1)
            mix(h)

    def vector(self, dve, own):
        c = self.core
        self.enter(dve)
        for h in range(self.HEADS):
            dve.wait_ge(self.scored.sem, self.scored0 + h + 1)
            if h >= 2:
                dve.wait_ge(self.mixed.sem, self.mixed0 + h - 1)
            dve.tensor_tensor(self.held[:, h % 2, :], c.bank[:, h % 2, 0:3 * P],
                              self.decay[:, h * 3 * P:(h + 1) * 3 * P], ALU.mult).then_inc(self.decayed.sem, 1)
            if h:
                self.head_stats(dve, own, h - 1)
        self.head_stats(dve, own, self.HEADS - 1)

    def head_stats(self, dve, own, h):
        dve.wait_ge(self.kept.sem, self.kept0 + h + 1)
        for t in range(TT):
            last = dve.bn_stats(self.core.stats[:, t * self.HEADS + h, 0, :], self.y[:, t, h * self.VD:(h + 1) * self.VD])
            if (h, t) != (self.HEADS - 1, TT - 1):
                own.step(last)
            else:
                last.then_inc(self.core.stage_done, 1)

    def scalar(self, act, own):
        c = self.core
        self.enter(act)
        for h in range(self.HEADS):
            act.wait_ge(self.mixed.sem, self.mixed0 + h + 1)
            cut = slice(h * self.VD, (h + 1) * self.VD)
            own.step(act.activation(self.y[:, 0, cut], c.bank[:, 2, :], ACT.Copy))
            act.activation(self.y[:, 1, cut], c.bank[:, 3, :], ACT.Copy).then_inc(self.kept.sem, 1)


class Multiply(Stage):

    def __init__(self, core, out, a, b):
        self.out, self.a, self.b = out, a, b
        self.theirs = out.shape[2] // 3 * 2
        super().__init__(core)

    def plan(self):
        self.second = self.core.counter("last_columns_multiplied")
        self.second0 = self.second.reserve(1)

    def gpsimd(self, pool, own):
        self.enter(pool)
        cut = slice(self.out.shape[2] - self.theirs, self.out.shape[2])
        pool.tensor_tensor(self.out[:, 1, cut], self.a[:, 1, cut], self.b[:, 1, cut], ALU.mult).then_inc(
            self.second.sem, 1)

    def vector(self, dve, own):
        self.enter(dve)
        own.step(dve.tensor_tensor(self.out[:, 0], self.a[:, 0], self.b[:, 0], ALU.mult))
        cut = slice(0, self.out.shape[2] - self.theirs)
        own.step(dve.tensor_tensor(self.out[:, 1, cut], self.a[:, 1, cut], self.b[:, 1, cut], ALU.mult))
        dve.wait_ge(self.second.sem, self.second0 + 1)
        dve.tensor_copy(self.core.small[:, 0:1], self.core.const[:, 0:1]).then_inc(self.core.stage_done, 1)


class Attention(Stage):

    HEADS = 8
    SPANS = ((0, P), (P, 3 * P))

    def __init__(self, core, terms, mask, scale, value, out, dv, scratch, maps=1, lam=None, row_add=None):
        self.terms, self.mask, self.scale, self.value, self.out, self.dv = terms, mask, scale, value, out, dv
        self.scratch, self.maps, self.lam, self.row_add = scratch, maps, lam, row_add
        super().__init__(core)

    def plan(self):
        c, n = self.core, self.HEADS
        self.marks = {}
        for name in ("scored", "maxed", "exped", "turned", "turned_kept", "mixed"):
            counter = c.counter("attention_" + name)
            self.marks[name] = (counter.sem, counter.reserve(n))
        self.combined = c.counter("maps_combined")
        self.combined0 = self.combined.reserve(n if self.maps == 2 else 0)
        self.divided = c.counter("head_divided")
        self.divided0 = self.divided.reserve(n - 1)
        at = self.scratch
        self.masked = c.at(at, 2, self.maps, 3 * P)
        at += 2 * self.maps * 3 * P
        self.probs = c.at(at, 2, self.maps, 3 * P)
        at += 2 * self.maps * 3 * P
        self.mixedp = c.at(at, 2, 3 * P)
        at += 2 * 3 * P
        self.probsT = c.at(at, 2, 3 * P)
        self.neg_max = shaped(c.small[:, 64:64 + 2 * self.maps * 2], 2, self.maps, 2)
        self.sums = shaped(c.small[:, 96:96 + 4 * self.maps * 2], 4, self.maps, 2)
        self.inverse = shaped(c.small[:, 128:128 + 4 * self.maps * 2], 4, self.maps, 2)
        self.weight = shaped(c.small[:, 160:164], 2, 2)

    def wait(self, eng, name, h):
        if h >= 0:
            sem, base = self.marks[name]
            eng.wait_ge(sem, base + h + 1)

    def wait_divided(self, eng, h):
        if h >= 0:
            eng.wait_ge(self.divided.sem, self.divided0 + h + 1)

    def scores(self, h, m):
        return self.core.bank[:, h % 2 * self.maps + m, 0:3 * P]

    def turned(self, h):
        return self.core.acc[:, 0, h % 2 * PIECE:h % 2 * PIECE + 3 * P]

    def mixed(self, h, i):
        at = h % 2 * PIECE + i * P
        return self.core.acc[:, 1, at:at + self.dv]

    def tensor(self, pe):
        c, heads = self.core, self.HEADS
        self.enter(pe)

        def score(h):
            self.wait(pe, "maxed", h - 2)
            for m in range(self.maps):
                terms = self.terms(h, m)
                for i, (lo, hi) in enumerate(self.SPANS):
                    for n, (q, k) in enumerate(terms):
                        mm = pe.matmul(self.scores(h, m)[:, lo:hi], q(i), k[:, 0:hi - lo],
                                       start=(n == 0), stop=(n == len(terms) - 1))
            mm.then_inc(self.marks["scored"][0], 1)

        def turn(h):
            if self.maps == 2:
                pe.wait_ge(self.combined.sem, self.combined0 + h + 1)
            else:
                self.wait(pe, "exped", h)
            self.wait(pe, "turned_kept", h - 2)
            probs = self.mixedp[:, h % 2, :] if self.maps == 2 else self.probs[:, h % 2, 0, :]
            for n in range(3):
                last = pe.transpose(self.turned(h)[:, n * P:(n + 1) * P], probs[:, n * P:(n + 1) * P],
                                    c.tables["ident"])
            last.then_inc(self.marks["turned"][0], 1)

        def mix(h):
            self.wait(pe, "turned_kept", h)
            self.wait_divided(pe, h - 2)
            for n, (i, k) in enumerate(((0, 0), (1, 0), (1, 1))):
                mm = pe.matmul(self.mixed(h, i), self.probsT[:, h % 2, n * P:(n + 1) * P],
                               self.value(h, k), start=(k == 0), stop=(k == i))
            mm.then_inc(self.marks["mixed"][0], 1)

        score(0)
        score(1)
        for h in range(heads):
            if h + 2 < heads:
                score(h + 2)
            turn(h)
            if h:
                mix(h - 1)
        mix(heads - 1)

    def scalar(self, act, own):
        heads = self.HEADS
        self.enter(act)

        def exponentiate(h):
            self.wait(act, "maxed", h)
            self.wait(act, "turned", h - 2)
            self.wait_divided(act, h - 4)
            for m in range(self.maps):
                for i, (lo, hi) in enumerate(self.SPANS):
                    last = act.activation(self.probs[:, h % 2, m, lo:hi], self.masked[:, h % 2, m, lo:hi], ACT.Exp,
                                          bias=self.neg_max[:, h % 2, m, i:i + 1],
                                          accum_out=self.sums[:, h % 4, m, i:i + 1])
                    if (m, i) != (self.maps - 1, 1):
                        own.step(last)
            last.then_inc(self.marks["exped"][0], 1)

        take_in(self.core, act, own, ACT.Exp)
        exponentiate(0)
        for h in range(heads):
            if h + 1 < heads:
                exponentiate(h + 1)
            self.wait(act, "turned", h)
            self.wait(act, "mixed", h - 2)
            act.activation(self.probsT[:, h % 2, :], self.turned(h), ACT.Copy).then_inc(self.marks["turned_kept"][0], 1)

    def vector(self, dve, own):
        c, heads = self.core, self.HEADS
        self.enter(dve)

        def mask(h):
            self.wait(dve, "scored", h)
            self.wait(dve, "exped", h - 2)
            for m in range(self.maps):
                got = self.scores(h, m)
                held = self.masked[:, h % 2, m, :]
                if self.row_add is None:
                    own.step(dve.scalar_tensor_tensor(held, got, self.scale, self.mask, ALU.mult, ALU.add))
                else:
                    for i, (lo, hi) in enumerate(self.SPANS):
                        own.step(dve.scalar_tensor_tensor(held[:, lo:hi], got[:, lo:hi], self.row_add(h, i),
                                                          self.mask[:, lo:hi], ALU.add, ALU.add))
            own.settle()
            for m in range(self.maps):
                for i, (lo, hi) in enumerate(self.SPANS):
                    own.step(dve.tensor_reduce(self.neg_max[:, h % 2, m, i:i + 1], self.masked[:, h % 2, m, lo:hi],
                                               AX, ALU.max))
            own.settle()
            flat = self.neg_max[:, h % 2].rearrange("p m i -> p (m i)")
            dve.tensor_scalar(flat, flat, -1.0, None, ALU.mult).then_inc(self.marks["maxed"][0], 1)

        def combine(h):
            self.wait(dve, "exped", h)
            self.wait(dve, "turned", h - 2)
            own.step(dve.reciprocal(self.inverse[:, h % 4].rearrange("p m i -> p (m i)"),
                                    self.sums[:, h % 4].rearrange("p m i -> p (m i)")))
            own.settle()
            own.step(dve.tensor_scalar(self.weight[:, h % 2, :], self.inverse[:, h % 4, 1, :], self.lam, None, ALU.mult))
            for i, (lo, hi) in enumerate(self.SPANS):
                own.step(dve.tensor_scalar(self.mixedp[:, h % 2, lo:hi], self.probs[:, h % 2, 0, lo:hi],
                                           self.inverse[:, h % 4, 0, i:i + 1], None, ALU.mult))
            own.settle()
            for i, (lo, hi) in enumerate(self.SPANS):
                held = self.mixedp[:, h % 2, lo:hi]
                last = dve.scalar_tensor_tensor(held, self.probs[:, h % 2, 1, lo:hi], self.weight[:, h % 2, i:i + 1],
                                                held, ALU.mult, ALU.add)
                if i == 0:
                    own.step(last)
            last.then_inc(self.combined.sem, 1)

        def finish(h):
            self.wait(dve, "mixed", h)
            if self.maps == 1:
                own.step(dve.reciprocal(self.inverse[:, h % 4, 0, :], self.sums[:, h % 4, 0, :]))
                own.settle()
            for i in range(TT):
                out = self.out[:, i, h * self.dv:(h + 1) * self.dv]
                if self.maps == 1:
                    last = dve.tensor_scalar(out, self.mixed(h, i), self.inverse[:, h % 4, 0, i:i + 1], None, ALU.mult)
                else:
                    last = dve.tensor_copy(out, self.mixed(h, i))
                if i == 0:
                    own.step(last)
            last.then_inc(c.stage_done if h == heads - 1 else self.divided.sem, 1)

        mask(0)
        for h in range(heads):
            if h + 1 < heads:
                mask(h + 1)
            if self.maps == 2:
                combine(h)
            if h >= 2:
                finish(h - 2)
        finish(heads - 2)
        finish(heads - 1)


class ZeroPadded(Stage):

    def __init__(self, core, dst, copies):
        self.dst, self.copies = dst, copies
        super().__init__(core)

    def vector(self, dve, own):
        self.enter(dve)
        own.step(dve.memset(self.dst, 0.0))
        own.settle()
        for out, src in self.copies[:-1]:
            own.step(dve.tensor_copy(out, src))
        out, src = self.copies[-1]
        dve.tensor_copy(out, src).then_inc(self.core.stage_done, 1)


class Lambda(Stage):

    def __init__(self, core, neg_lam, gain, row, products):
        self.neg_lam, self.gain, self.row, self.products = neg_lam, gain, row, products
        super().__init__(core)

    def plan(self):
        c = self.core
        self.dotted, self.exped = (c.sem(n) for n in ("lambda_dotted", "lambda_exped"))

    def vector(self, dve, own):
        c = self.core
        self.enter(dve)
        pairs = shaped(self.row, 2, 2, 64)
        own.step(dve.tensor_tensor(self.products, pairs[:, :, 0, :], pairs[:, :, 1, :], ALU.mult))
        own.settle()
        dve.tensor_reduce(c.small[:, 8:10], self.products, AX, ALU.add).then_inc(self.dotted, 1)
        own.step(dve.tensor_scalar(self.gain, c.col["subln"].to_broadcast([P, 8]), 1.0 - LAM_INIT, None, ALU.mult))
        dve.wait_ge(self.exped, 1)
        own.step(dve.tensor_tensor(c.small[:, 12:13], c.small[:, 11:12], c.small[:, 10:11], ALU.subtract))
        own.settle()
        dve.tensor_scalar(self.neg_lam, c.small[:, 12:13], -LAM_INIT, None, ALU.add).then_inc(c.stage_done, 1)

    def scalar(self, act, own):
        c = self.core
        self.enter(act)
        act.wait_ge(self.dotted, 1)
        act.activation(c.small[:, 10:12], c.small[:, 8:10], ACT.Exp).then_inc(self.exped, 1)


class PositionAngles(Stage):

    MAGIC = 1.5 * 2.0 ** 23
    PARTS = (6.28125, 0.00193500518798828125, 3.0199159819e-07)

    def __init__(self, core, cos, sin, held):
        self.cos, self.sin, self.held = cos, sin, held
        super().__init__(core)

    def plan(self):
        c = self.core
        self.reduced = c.sem("angles_reduced")

    def vector(self, dve, own):
        c = self.core
        self.enter(dve)
        step = own.step
        step(dve.tensor_copy(c.small[:, 10:12], c.small[:, 8:10].bitcast(I32)))
        own.settle()
        ang, turns, low, arg = (self.held[:, n, :] for n in range(4))
        for t in range(TT):
            step(dve.tensor_scalar(ang[:, t * 32:(t + 1) * 32], c.tables["inv_freq"], c.small[:, 10 + t:11 + t], None,
                                   ALU.mult))
        own.settle()
        step(dve.tensor_scalar(turns, ang, 1.0 / (2.0 * math.pi), self.MAGIC, ALU.mult, ALU.add))
        own.settle()
        step(dve.tensor_scalar(turns, turns, -self.MAGIC, None, ALU.add))
        own.settle()
        for part in self.PARTS:
            step(dve.scalar_tensor_tensor(ang, turns, -part, ang, ALU.mult, ALU.add))
            own.settle()
        step(dve.tensor_scalar(ang, ang, 3.1415925, -3.1415925, ALU.min, ALU.max))
        own.settle()
        step(dve.tensor_scalar(low, ang, -1.0, None, ALU.mult))
        own.settle()
        step(dve.tensor_tensor(low, low, ang, ALU.max))
        own.settle()
        dve.tensor_scalar(arg, low, -1.0, math.pi / 2, ALU.mult, ALU.add).then_inc(self.reduced, 1)

    def scalar(self, act, own):
        c = self.core
        self.enter(act)
        act.wait_ge(self.reduced, 1)
        own.step(act.activation(self.sin.rearrange("p t f -> p (t f)"), self.held[:, 0, :], ACT.Sin))
        act.activation(self.cos.rearrange("p t f -> p (t f)"), self.held[:, 3, :], ACT.Sin).then_inc(c.stage_done, 1)


class ForgetGates(Stage):

    H = 8

    def __init__(self, core, cum, neg, pick, held):
        self.cum, self.neg, self.pick, self.held = cum, neg, pick, held
        super().__init__(core)

    def plan(self):
        c = self.core
        self.unit_count = 1
        self.unit0 = c.take_units(self.unit_count)
        self.logits = c.sem("forget_logits_ready")
        self.ln_ready = c.sem("forget_logarithm_ready")
        self.logs = c.sem("forget_logs_ready")
        self.summed = c.sem("forget_logs_summed")

    def gpsimd(self, pool, own):
        self.last_remainders(pool, self.unit0 + LOWS)

    def tensor(self, pe):
        c = self.core
        self.enter(pe)
        self.ready(pe, self.unit0)
        for t in range(TT):
            for k in range(KD):
                mm = product(pe, c.bank[:, t, 0:self.H], parts(c.xT, slice(None), k, slice(t * P, (t + 1) * P)),
                             c.unit_parts(self.unit0, k * P, k * P + self.H), start=(k == 0), stop=(k == KD - 1))
        mm.then_inc(c.units_multiplied, 1)
        pe.wait_ge(self.logs, 1)
        logs = self.held[:, 3]
        pe.matmul(c.bank[:, 2, 0:self.H], c.tables["upper"], logs[:, 0, :], start=True, stop=True)
        pe.matmul(c.bank[:, 3, 0:self.H], c.tables["ones"], logs[:, 0, :], start=True, stop=False)
        pe.matmul(c.bank[:, 3, 0:self.H], c.tables["upper"], logs[:, 1, :], start=False, stop=True).then_inc(
            self.summed, 1)

    def vector(self, dve, own):
        c, h = self.core, self.H
        self.enter(dve)
        own.step(dve.memset(self.neg, 0.0))
        own.step(dve.tensor_copy(self.pick, spread(c.tables["ident"][:, 0:h], 2, P)))
        dve.wait_ge(c.units_multiplied, self.unit0 + 1)
        z, low, ln, logs = (self.held[:, n] for n in range(4))
        for t in range(TT):
            own.step(dve.tensor_tensor(z[:, t, :], c.bank[:, t, 0:h], c.small[:, 16:24], ALU.add))
        own.settle()
        own.step(dve.tensor_scalar(low, z, 0.0, None, ALU.min))
        own.settle()
        dve.scalar_tensor_tensor(ln, low, 2.0, z, ALU.mult, ALU.subtract).then_inc(self.logits, 1)
        dve.wait_ge(self.ln_ready, 1)
        dve.tensor_tensor(logs, low, ln, ALU.subtract).then_inc(self.logs, 1)
        dve.wait_ge(self.summed, 1)
        for t in range(TT):
            own.step(dve.tensor_copy(self.cum[:, t, :], c.bank[:, 2 + t, 0:h]))
        for t in range(TT):
            last = dve.tensor_scalar(self.neg[:, t, 0:h], c.bank[:, 2 + t, 0:h], -1.0, None, ALU.mult)
            if t < TT - 1:
                own.step(last)
        last.then_inc(c.stage_done, 1)

    def scalar(self, act, own):
        self.enter(act)
        act.wait_ge(self.logits, 1)
        ln = self.held[:, 2]
        own.step(act.activation(ln, ln, ACT.Exp))
        own.settle()
        act.activation(ln, ln, ACT.Ln, bias=1.0).then_inc(self.ln_ready, 1)
        self.round_next(act, self.unit0)


class SelectKeys(Stage):

    H = 8

    def __init__(self, core, qT, kT, w, mask, scratch):
        self.qT, self.kT, self.w, self.mask, self.scratch = qT, kT, w, mask, scratch
        super().__init__(core)

    def plan(self):
        c = self.core
        self.scored, self.rectified, self.added = (c.sem(n) for n in ("index_scored", "index_rectified", "index_added"))
        self.relu = c.at(self.scratch, 2, 3 * P)
        self.score = c.at(self.scratch + 768, 3 * P)
        self.weights = c.at(self.scratch + 1152, TT, self.H)
        self.best = c.at(self.scratch + 1168, 2, 8)

    def tensor(self, pe):
        c = self.core
        self.enter(pe)
        for h in range(self.H):
            if h >= 2:
                pe.wait_ge(self.rectified, h - 1)
            for i, (lo, hi) in enumerate(Attention.SPANS):
                mm = pe.matmul(c.bank[:, h % 2, lo:hi], self.qT[:, h // 4, i * P:(i + 1) * P],
                               self.kT[:, h % 4, 0:hi - lo], start=True, stop=True)
            mm.then_inc(self.scored, 1)

    def scalar(self, act, own):
        c = self.core
        self.enter(act)
        for h in range(self.H):
            act.wait_ge(self.scored, h + 1)
            if h >= 2:
                act.wait_ge(self.added, h - 1)
            act.activation(self.relu[:, h % 2, :], c.bank[:, h % 2, 0:3 * P], ACT.Relu, scale=32.0 ** -0.5).then_inc(
                self.rectified, 1)

    def vector(self, dve, own):
        c = self.core
        self.enter(dve)
        own.step(dve.tensor_scalar(self.weights, self.w, self.H ** -0.5, None, ALU.mult))
        own.settle()
        for h in range(self.H):
            dve.wait_ge(self.rectified, h + 1)
            if h:
                dve.wait_ge(self.added, h)
            for i, (lo, hi) in enumerate(Attention.SPANS):
                w, score = self.weights[:, i, h:h + 1], self.score[:, lo:hi]
                if h == 0:
                    last = dve.tensor_scalar(score, self.relu[:, 0, lo:hi], w, None, ALU.mult)
                else:
                    last = dve.scalar_tensor_tensor(score, self.relu[:, h % 2, lo:hi], w, score, ALU.mult, ALU.add)
                if i == 0:
                    own.step(last)
            last.then_inc(self.added, 1)
        dve.wait_ge(self.added, self.H)
        own.step(dve.tensor_tensor(self.score, self.score, c.tables["causal"], ALU.add))
        own.settle()
        for _ in range(DSA_TOPK // 8):
            for i, (lo, hi) in enumerate(Attention.SPANS):
                own.step(dve.max(self.best[:, i, :], self.score[:, lo:hi]))
            own.settle()
            for i, (lo, hi) in enumerate(Attention.SPANS):
                own.step(dve.match_replace(self.score[:, lo:hi], self.best[:, i, :], self.score[:, lo:hi], MARK))
            own.settle()
        own.step(dve.tensor_scalar(self.mask, self.score, MARK, None, ALU.is_equal))
        own.settle()
        own.step(dve.tensor_scalar(self.mask, self.mask, -NEG, NEG, ALU.mult, ALU.add))
        own.settle()
        dve.tensor_tensor(self.mask, self.mask, c.tables["causal"], ALU.add).then_inc(c.stage_done, 1)


class ShortConv:

    CH, TAPS = 4, 3

    def __init__(self, core, bcu, padded, products, held, out):
        self.core, self.index = core, core.counted
        self.bcu, self.padded, self.products, self.held, self.out = bcu, padded, products, held, out
        core.stages.append(self)
        self.done = core.sem("short_conv_done")

    def gpsimd(self, pool, own):
        c, n = self.core, self.CH
        pool.wait_ge(c.stage_done, self.index)
        own.step(pool.memset(self.padded[:, :, 0:self.TAPS - 1], 0.0))
        own.step(pool.tensor_tensor(self.padded[:, :, self.TAPS - 1:self.TAPS - 1 + SEQ], self.bcu[:, n:2 * n, :],
                                    self.bcu[:, 2 * n:3 * n, :], ALU.mult))
        own.settle()
        for j in range(self.TAPS):
            out = self.products if j else self.held
            for ch in range(n):
                w = c.col["hyb_conv"][:, ch * self.TAPS + j:ch * self.TAPS + j + 1]
                own.step(pool.tensor_scalar(out[:, ch, :], self.padded[:, ch, j:j + SEQ], w, None, ALU.mult))
            own.settle()
            if j:
                own.step(pool.tensor_tensor(self.held, self.held, self.products, ALU.add))
                own.settle()
        pool.tensor_tensor(self.out, self.held, self.bcu[:, 0:n, :], ALU.mult).then_inc(self.done, 1)

    def needed(self, eng):
        eng.wait_ge(self.done, 1)

    def scalar(self, act, own):
        pass

    def vector(self, dve, own):
        pass

    def tensor(self, pe):
        pass


class GluConv(Stage):

    TAPS, MINE = 31, 4

    def __init__(self, core, ag, sig, padded, products, diagonals, out):
        self.ag, self.sig, self.padded, self.products, self.out = ag, sig, padded, products, out
        self.diagonals = diagonals
        super().__init__(core)

    def plan(self):
        c = self.core
        self.sigmoids, self.glued = c.sem("glu_sigmoids"), c.sem("glu_ready")
        self.taps_done = c.sem("taps_added")
        self.product_ready, self.product_added = c.sem("product_ready"), c.sem("product_added")
        self.diagonals_ready, self.taps_multiplied = c.sem("diagonals_ready"), c.sem("taps_multiplied")
        self.banks_kept = c.sem("convolved_banks_kept")
        self.turned = range(self.MINE + 1, KD)

    def tap_of(self, ch, tap):
        if isinstance(tap, int):
            return self.core.col["conf_conv"][:, ch * self.TAPS + tap:ch * self.TAPS + tap + 1]
        return self.core.col["conf_conv"][:, bass.ds(tap + ch * self.TAPS, 1)]

    def by_taps(self, eng, step):
        for j in range(3):
            step(j)
        with eng.Fori(0, (self.TAPS - 5) // 2) as i:
            for j in (3, 4):
                step(j, i)
        for j in (self.TAPS - 2, self.TAPS - 1):
            step(j)

    def tensor(self, pe):
        c = self.core
        self.enter(pe)
        pe.wait_ge(self.glued, len(self.turned))

        def tap(j, i=None):
            past, at = (0, j) if i is None else (i * 2, i * 2 + j)
            pe.wait_ge(self.diagonals_ready, past + j + 1)
            for n, ch in enumerate(self.turned):
                mm = pe.matmul(c.bank[:, n, 0:SEQ], self.diagonals[:, j % 2, n, :], self.padded[:, ch, bass.ds(at, SEQ)],
                               start=(j == 0), stop=(j == self.TAPS - 1))
            mm.then_inc(self.taps_multiplied, 1)

        self.by_taps(pe, tap)

    def scalar(self, act, own):
        c, mine = self.core, self.MINE
        self.enter(act)
        for ch in reversed(range(KD)):
            act.activation(self.sig[:, ch, :], self.ag[:, KD + ch, :], ACT.Sigmoid,
                           bias=c.col["b_pw1"][:, KD + ch:KD + ch + 1]).then_inc(self.sigmoids, 1)

        def tap(j, i=None):
            past, at = (0, j) if i is None else (i * 2, i * 2 + j)
            if j >= 2:
                act.wait_ge(self.taps_multiplied, past + j - 1)
            for n, ch in enumerate(self.turned):
                last = act.activation(self.diagonals[:, j % 2, n, :], c.tables["ident"], ACT.Copy,
                                      scale=self.tap_of(ch, at))
            last.then_inc(self.diagonals_ready, 1)
            if j == 0:
                act.wait_ge(self.glued, KD - mine)
                act.activation(self.out[:, mine, :], self.padded[:, mine, 0:SEQ], ACT.Identity,
                               bias=c.col["conf_conv_b"][:, mine:mine + 1],
                               scale=self.tap_of(mine, 0)).then_inc(self.product_ready, 1)
                return
            if j >= 3:
                act.wait_ge(self.product_added, past + j - 2)
            act.activation(self.products[:, j % 2, :], self.padded[:, mine, bass.ds(at, SEQ)], ACT.Copy,
                           scale=self.tap_of(mine, at)).then_inc(self.product_ready, 1)

        self.by_taps(act, tap)
        act.wait_ge(self.taps_multiplied, self.TAPS)
        for n, ch in enumerate(self.turned):
            act.activation(self.out[:, ch, :], c.bank[:, n, 0:SEQ], ACT.Identity,
                           bias=c.col["conf_conv_b"][:, ch:ch + 1]).then_inc(self.banks_kept, 1)

    def vector(self, dve, own):
        c, pad = self.core, self.TAPS - 1
        self.enter(dve)
        own.step(dve.memset(self.padded[:, :, 0:pad], 0.0))
        own.settle()
        for n, ch in enumerate(reversed(range(KD))):
            dve.wait_ge(self.sigmoids, n + 1)
            dve.scalar_tensor_tensor(self.padded[:, ch, pad:pad + SEQ], self.ag[:, ch, :],
                                     c.col["b_pw1"][:, ch:ch + 1], self.sig[:, ch, :], ALU.add,
                                     ALU.mult).then_inc(self.glued, 1)
        dve.wait_ge(self.glued, KD)
        for ch in range(self.MINE):
            dve.tensor_scalar(self.out[:, ch, :], self.padded[:, ch, 0:SEQ], self.tap_of(ch, 0),
                              c.col["conf_conv_b"][:, ch:ch + 1], ALU.mult, ALU.add).then_inc(self.taps_done, 1)
        with dve.Fori(0, self.TAPS - 1) as i:
            for ch in range(self.MINE):
                src = self.padded[:, ch, bass.ds(i + 1, SEQ)]
                dve.wait_ge(self.taps_done, i * self.MINE + ch + 1)
                dve.scalar_tensor_tensor(self.out[:, ch, :], src, self.tap_of(ch, i + 1), self.out[:, ch, :], ALU.mult,
                                         ALU.add).then_inc(self.taps_done, 1)
        dve.wait_ge(self.product_added, self.TAPS - 1)
        dve.wait_ge(self.banks_kept, len(self.turned))
        dve.tensor_copy(c.small[:, 0:1], c.const[:, 0:1]).then_inc(c.stage_done, 1)

    def gpsimd(self, pool, own):
        self.enter(pool)

        def tap(j, i=None):
            past = 0 if i is None else i * 2
            if j == 0:
                return
            pool.wait_ge(self.product_ready, past + j + 1)
            if j >= 2:
                pool.wait_ge(self.product_added, past + j - 1)
            acc = self.out[:, self.MINE, :]
            pool.tensor_tensor(acc, acc, self.products[:, j % 2, :], ALU.add).then_inc(self.product_added, 1)

        self.by_taps(pool, tap)


class TransposeSwish(Transpose):

    def __init__(self, core, src, held, gain, bias):
        self.bias = bias
        super().__init__(core, src, held, KD, gain)

    def plan_copies(self):
        assert len(self.groups) <= 4
        self.swished, self.rounded = self.core.sem("swish_ready"), self.core.sem("swish_rounded")

    def scalar(self, act, own):
        c = self.core
        self.enter(act)
        for g, (t, c0, n) in enumerate(self.groups):
            act.wait_ge(self.turned.sem, self.turned0 + g + 1)
            for k in range(n):
                ch = c0 + k
                last = act.activation(self.dst[:, ch, t * P:(t + 1) * P], c.bank[:, g % 4, k * P:(k + 1) * P], ACT.Silu,
                                      bias=self.bias[:, ch:ch + 1], scale=self.gain[:, ch:ch + 1])
                if k < n - 1:
                    own.step(last)
            last.then_inc(self.swished, 1)

    def vector(self, dve, own):
        self.enter(dve)
        high, low = self.core.xT
        for g, (t, c0, n) in enumerate(self.groups):
            cut = (slice(None), slice(c0, c0 + n), slice(t * P, (t + 1) * P))
            dve.wait_ge(self.swished, g + 1)
            dve.tensor_copy(high[cut], self.dst[cut]).then_inc(self.rounded, 1)
            dve.wait_ge(self.rounded, g + 1)
            last = dve.tensor_tensor(low[cut], self.dst[cut], high[cut].bitcast(F32), ALU.subtract)
            if g < len(self.groups) - 1:
                own.step(last)
        last.then_inc(self.core.stage_done, 1)


class BackTranspose(Stage):

    def __init__(self, core, src, dst):
        self.src, self.dst = src, dst
        super().__init__(core)

    def plan(self):
        self.turned = self.core.counter("tile_transposed")
        self.turned0 = self.turned.reserve(4)

    def tensor(self, pe):
        c = self.core
        self.enter(pe)
        for g in range(4):
            t, q = g // 2, g % 2
            for k in range(4):
                last = pe.transpose(c.bank[:, g, k * P:(k + 1) * P], self.src[:, 4 * q + k, t * P:(t + 1) * P],
                                    c.tables["ident"])
            last.then_inc(self.turned.sem, 1)

    def vector(self, dve, own):
        c = self.core
        self.enter(dve)
        for g in range(4):
            t, q = g // 2, g % 2
            dve.wait_ge(self.turned.sem, self.turned0 + g + 1)
            last = dve.tensor_copy(self.dst[:, t, q * 512:(q + 1) * 512], c.bank[:, g, :])
            if g < 3:
                own.step(last)
        last.then_inc(c.stage_done, 1)


class AddRow(Stage):

    def __init__(self, core, row):
        load = prefetch_row(core, "norm_row0", 0, row, 1)
        super().__init__(core)
        self.after(load)

    def vector(self, dve, own):
        c = self.core
        self.enter(dve)
        own.step(dve.tensor_tensor(c.x[:, 0, :], c.x[:, 0, :], c.rows_at(0), ALU.add))
        dve.tensor_tensor(c.x[:, 1, :], c.x[:, 1, :], c.rows_at(0), ALU.add).then_inc(c.stage_done, 1)


class Store(Stage):

    def scalar(self, act, own):
        c = self.core
        self.enter(act)
        stored = c.sem("output_stored")
        act.dma_start(c.dram["out"].rearrange("(t p) d -> p t d", p=P), c.x[:, :, :]).then_inc(stored, 16)
        act.wait_ge(stored, 16)




def final_norm(c, row):
    load = prefetch_row(c, "norm_row0", 0, row, 1)
    NormSplit(c, "rms", 1e-6, c.x, c.rows_at(0), split=False).after(load)


def post_norm(c, layer, which, split=True):
    n = 2 * layer + which
    loads = [prefetch_row(c, f"norm_row{k}", k, ROWS[name] + n, 1) for k, name in enumerate(("ln_g", "ln_b"))]
    NormSplit(c, "ln", 1e-5, c.x, c.rows_at(0), c.rows_at(1), split).after(*loads)


def pre_norm(c, name, n, ahead=1):
    load = prefetch_row(c, "gain_row", -1, ROWS[name] + n, ahead)
    NormSplit(c, "rms", 1e-6, c.at(26624, TT, D), c.rows_at(-1)).after(load)


def peer(c, layer):
    queries, scores = c.at(0, 16, SEQ), c.at(4096, TT, 16, P)
    routes = c.at(8192, TT, 3, P)
    subkeys = c.at(20480, 16, P)
    load = Prefetch(c, "subkeys", subkeys, c.dram["subkeysT"][layer])
    FeatureMajor(c, c.xT, KD, 16, queries)
    KeyScores(c, queries, subkeys, scores).after(load)
    later = N_KEYS - AHEAD
    gates, store = c.at(0, SEQ, later), c.at(SEQ * later, AHEAD, SEQ)
    Route(c, scores, routes, 9216, store)
    routesT = shaped(c.scratch[:, 0:3 * SEQ], 3, SEQ)
    Transpose(c, routes.rearrange("p t s n -> p t (s n)"), routesT, 3)
    firsts = [c.activated[:, n, :] for n in range(2)] + [c.scratch[:, (3 + n) * SEQ:(4 + n) * SEQ] for n in range(2)]
    seconds = [c.hidden[part][:, n, :] for part in range(2) for n in range(2)]
    SpreadGates(c, routesT, [(shaped(a, 2, P), shaped(b, 2, P)) for a, b in zip(firsts, seconds)], gates, store)
    StoredChunks(c, store)
    ExpertLoop(c, later, 1, ACT.Gelu_apprx_tanh, DN_ALPHA, 1.0, gates, begun=True)


def swiglu(c, name, n, ahead=1):
    pre_norm(c, name, n, ahead)
    ExpertLoop(c, D_FF // P, 2, ACT.Silu, 1.0, 0.5)


def heads(v, n):
    return v.rearrange("p t (h d) -> p t h d", h=n)


def at_tile(ap):
    return lambda i: ap[:, i * P:(i + 1) * P]


def first_block(c):
    TransposeSplit(c, c.x)
    retention(c)
    post_norm(c, 0, 0)
    peer(c, 0)
    post_norm(c, 0, 1)
    differential(c)
    post_norm(c, 1, 0)
    peer(c, 1)
    post_norm(c, 1, 1, split=False)


def retention(c):
    proj = c.at(0, TT, 6144)
    tables = c.at(30720, 2048)
    load = Prefetch(c, "tables", tables, c.dram["fetched"][:, 0:2048])
    Project(c, c.xT, KD, [PIECE] * 12, proj, [ACT.Copy] * 8 + [ACT.Silu] * 4)
    qk = [heads(proj[:, :, 0:1024], 4), heads(proj[:, :, 1024:2048], 4)]
    Rotate(c, qk, 128, shaped(tables[:, 0:256], TT, 128), shaped(tables[:, 256:512], TT, 128), 12288).after(load)
    qkT = c.at(21504, 16, SEQ)
    Transpose(c, proj[:, :, 0:2048], qkT, 16)
    y = c.at(12288, TT, 2048)
    RetentionScores(c, qkT[:, 0:8], qkT[:, 8:16], proj[:, :, 2048:4096], tables[:, 512:2048], y,
                    c.at(16384, 2, 3 * P))
    cuts = [y[:, t, h * 512:(h + 1) * 512] for t in range(TT) for h in range(4)]
    Norm(c, [(v, v) for v in cuts], "ln", 1e-5, measured=True)
    Multiply(c, y, y, proj[:, :, 4096:6144])
    for half in range(2):
        TransposeSplit(c, y[:, :, half * D:(half + 1) * D])
        AddTo(c, c.xT, KD, DN_ALPHA if half == 0 else 1.0)


def differential(c):
    tab = c.tables
    qkv = c.at(0, TT, 3072)
    row = c.at(28928, 256)
    load = Prefetch(c, "lambda", row, c.dram["rows"][ROWS["lambda"]:ROWS["lambda"] + 1, 0:256].to_broadcast([P, 256]))
    Project(c, c.xT, KD, [PIECE] * 6, qkv)
    q, k = qkv[:, :, 0:1024], qkv[:, :, 1024:2048]
    Rotate(c, [heads(q, 16), heads(k, 16)], 8, shaped(tab["cos_att"], TT, 8), shaped(tab["sin_att"], TT, 8), 24576)
    padded = c.at(12288, TT, 2, 8, P)
    kh = k.rearrange("p t (h m d) -> p t h m d", h=8, m=2)
    ZeroPadded(c, padded.rearrange("p t m h d -> p (t m h d)"),
               [(padded[:, t, m, :, 64 * m:64 * m + 64], kh[:, t, :, m, :]) for t in range(TT) for m in range(2)])
    qT, kT = c.at(6144, 8, SEQ), c.at(8192, 16, SEQ)
    Transpose(c, q, qT, 8)
    Transpose(c, padded.rearrange("p t m h d -> p t (m h d)"), kT, 16)
    neg_lam, sub_gain = c.small[:, 200:201], c.small[:, 208:216]
    Lambda(c, neg_lam, sub_gain, row, c.at(28672, 2, 64)).after(load)
    o = c.at(22528, TT, D)
    Attention(c, lambda h, m: [(at_tile(qT[:, h, :]), kT[:, 8 * m + h, :])], tab["causal"], 64.0 ** -0.5,
              lambda h, t: qkv[:, t, 2048 + h * P:2048 + (h + 1) * P], o, P, 16384, maps=2, lam=neg_lam)
    cuts = [o[:, t, h * P:(h + 1) * P] for t in range(TT) for h in range(8)]
    Norm(c, [(v, v) for v in cuts], "rms", 1e-5)
    TransposeSplit(c, o, gain=sub_gain)
    AddTo(c, c.xT, KD, DN_ALPHA)


def second_block(c):
    for layer in range(2):
        swiglu(c, "ffn_norm_2", 2 * layer)
        pre_norm(c, "mix_norm_2", layer)
        (mla, fox)[layer](c)
        swiglu(c, "ffn_norm_2", 2 * layer + 1)
        pre_norm(c, "ple_norm", layer)
        gate, gated, pT = c.at(0, TT, D), c.at(2048, TT, D), c.at(4096, 2, SEQ)
        load = Prefetch(c, "embeddings", pT, c.dram["pT"][layer])
        Project(c, c.xT, KD, [PIECE] * 2, gate, [ACT.Sigmoid] * 2).feeding()
        SplitOperand(c, pT, 0).after(load)
        GatedAdd(c, parts(c.xT, slice(None), slice(0, 2)), 2, gate, gated)
    final_norm(c, ROWS["final_2"])


def mla(c):
    low, chunked = c.at(0, TT, 512), c.at(12800, 3 * P)
    mask_load = Prefetch(c, "tables", chunked, c.dram["fetched"][:, 2048:2432])
    load = Prefetch(c, "positions", c.small[:, 8:10].bitcast(I32),
                    c.dram["positions"].rearrange("one (t p) -> p (one t)", p=P), slow=True)
    Project(c, c.xT, KD, [448], low)
    Norm(c, [(low[:, t, a:b], low[:, t, a:b]) for t in range(TT) for a, b in ((0, 256), (256, 384))], "rms", 1e-6)
    cos, sin = c.at(12288, TT, 32), c.at(12352, TT, 32)
    PositionAngles(c, cos, sin, c.at(12416, 4, 64)).after(load)
    TransposeSplit(c, low[:, :, 0:384], 3, c.col["mla_norms"])
    c_q, c_kv = parts(c.xT, slice(None), slice(0, 2)), parts(c.xT, slice(None), slice(2, 3))
    qT = c.at(4096, 8, SEQ)
    FeatureMajor(c, c_q, 2, 8, qT).feeding()
    q_rope = c.at(6144, TT, 512)
    Project(c, c_q, 2, [PIECE], q_rope).feeding()
    kT = c.at(8192, 8, SEQ)
    FeatureMajor(c, c_kv, 1, 8, kT).feeding()
    v = c.at(10240, TT, D)
    Project(c, c_kv, 1, [PIECE] * 2, v)
    Rotate(c, [heads(q_rope, 8), heads(low[:, :, 384:448], 1)], 32, cos, sin, 24576)
    padded = c.at(1024, TT, 2, P)
    ZeroPadded(c, padded.rearrange("p t m d -> p (t m d)"),
               [(padded[:, :, m, 64 * m:64 * m + 64], low[:, :, 384:448]) for m in range(2)])
    q_ropeT, k_ropeT = c.at(7168, 4, SEQ), c.at(3072, 2, SEQ)
    Transpose(c, q_rope, q_ropeT, 4)
    Transpose(c, padded.rearrange("p t m d -> p t (m d)"), k_ropeT, 2)
    o = c.at(22528, TT, D)
    Attention(c, lambda h, m: [(at_tile(qT[:, h, :]), kT[:, h, :]),
                               (at_tile(q_ropeT[:, h // 2, :]), k_ropeT[:, h % 2, :])],
              chunked, 192.0 ** -0.5, lambda h, t: v[:, t, h * P:(h + 1) * P], o, P, 16384).after(mask_load)
    TransposeSplit(c, o)
    AddTo(c, c.xT, KD)


def fox(c):
    qkT, v = c.at(0, 16, SEQ), c.at(4096, TT, D)
    row = ROWS["b_f"]
    load = Prefetch(c, "forget_bias", c.small[:, 16:24], c.dram["rows"][row:row + 1, 0:8].to_broadcast([P, 8]))
    FeatureMajor(c, c.xT, KD, 16, qkT, [128.0 ** -0.5] * 8 + [1.0] * 8).feeding()
    Project(c, c.xT, KD, [PIECE] * 2, v).feeding()
    cum, neg, pick = c.at(6144, TT, 8), c.at(6400, TT, P), c.at(7168, 8, P)
    ForgetGates(c, cum, neg, pick, c.at(8192, 4, TT, 8)).after(load)
    negT = c.at(8448, 1, SEQ)
    Transpose(c, neg, negT, 1)
    o = c.at(22528, TT, D)
    Attention(c, lambda h, m: [(at_tile(qkT[:, h, :]), qkT[:, 8 + h, :]), (lambda i: pick[:, h, :], negT[:, 0, :])],
              c.tables["causal"], 1.0, lambda h, t: v[:, t, h * P:(h + 1) * P], o, P, 16384,
              row_add=lambda h, i: cum[:, i, h:h + 1])
    TransposeSplit(c, o)
    AddTo(c, c.xT, KD)


def third_block(c):
    for layer in range(2):
        swiglu(c, "ffn_norm_3", 2 * layer)
        pre_norm(c, "mix_norm_3", layer)
        (sparse_and_conv, conformer)[layer](c)
        swiglu(c, "ffn_norm_3", 2 * layer + 1, ahead=1 + layer)
    final_norm(c, ROWS["final_3"])


def sparse_and_conv(c):
    tab = c.tables
    z, bcu = c.at(0, TT, 1024), c.at(2048, 12, SEQ)
    Project(c, c.xT, KD, [512, 424], z).feeding()
    FeatureMajor(c, c.xT, KD, 12, bcu)
    Rotate(c, [heads(z[:, :, 0:576], 9)], 8, shaped(tab["cos_att"], TT, 8), shaped(tab["sin_att"], TT, 8), 28672)
    Rotate(c, [heads(z[:, :, 640:928], 9)], 4, shaped(tab["cos_idx"], TT, 4), shaped(tab["sin_idx"], TT, 4), 28672)
    convolved = c.at(24576, 4, SEQ)
    conv = ShortConv(c, bcu, c.at(5120, 4, 258), c.at(20480, 4, SEQ), c.at(6400, 4, SEQ), convolved)
    padded = c.at(8192, TT, 6, P)
    ZeroPadded(c, padded.rearrange("p t m d -> p (t m d)"),
               [(padded[:, :, m, 64 * m:64 * m + 64], z[:, :, 512:576]) for m in range(2)]
               + [(padded[:, :, 2 + m, 32 * m:32 * m + 32], z[:, :, 896:928]) for m in range(4)])
    qT, qiT, kT = c.at(10240, 4, SEQ), c.at(11264, 2, SEQ), c.at(12288, 6, SEQ)
    Transpose(c, z[:, :, 0:512], qT, 4)
    Transpose(c, z[:, :, 640:896], qiT, 2)
    Transpose(c, padded.rearrange("p t m d -> p t (m d)"), kT, 6)
    mask = c.at(14336, 3 * P)
    SelectKeys(c, qiT, kT[:, 2:6], z[:, :, 928:936], mask, 15360)
    o = c.at(22528, TT, 512)
    Attention(c, lambda h, m: [(at_tile(qT[:, h // 2, :]), kT[:, h % 2, :])], mask, 64.0 ** -0.5,
              lambda h, t: z[:, t, 576:640], o, 64, 16896)
    SplitOperand(c, convolved, 4).after(conv)
    TransposeSplit(c, o, 4)
    AddTo(c, c.xT, KD)


def conformer(c):
    ag, sig = c.at(0, 16, SEQ), c.at(4096, KD, SEQ)
    FeatureMajor(c, c.xT, KD, 16, ag)
    convolved = c.at(9216, KD, SEQ)
    GluConv(c, ag, sig, c.at(6144, KD, SEQ + 30), c.at(16384, 2, SEQ), c.at(18432, 2, 3, P), convolved)
    turned = c.at(12288, TT, D)
    BackTranspose(c, convolved, turned)
    Norm(c, [(turned[:, t, :], turned[:, t, :]) for t in range(TT)], "ln", 1e-6)
    TransposeSwish(c, turned, c.at(14336, KD, SEQ), c.col["conf_ln_g"], c.col["conf_ln_b"])
    AddTo(c, c.xT, KD)
    AddRow(c, ROWS["b_pw2"])




def build(nc, dram, plan=None):
    with ExitStack() as ctx:
        c = Core(nc, ctx, dram)
        Load(c)
        if plan:
            plan(c)
        else:
            first_block(c)
            second_block(c)
            third_block(c)
        Store(c)
        first = next(n for n, stage in enumerate(c.stages) if stage.index == 1)
        c.stages.insert(first + 1, FirstUnits(c))
        units = c.units + HIGHS
        vector_own, scalar_own, pool_own = c.sem("vector_own"), c.sem("scalar_own"), c.sem("pool_own")
        block = ctx.enter_context(nc.Block())

        @block.sync
        def _(sp):
            def load(unit, i=0):
                if unit >= RING:
                    sp.wait_ge(c.unit_ready[unit % LOWS], i * (RING // LOWS) + (unit - RING) // LOWS + 1)
                src = dram["stream"][bass.ds(i * RING + unit, 1), :, :].rearrange("one p n -> (one p) n")
                sp.dma_start(c.ring[:, unit % RING, :], src).then_inc(c.unit_landed[unit % RING], 16)

            sp.wait_ge(c.inputs_loaded, 48)
            for unit in range(min(RING, units)):
                load(unit)
            if units >= 2 * RING:
                with sp.Fori(0, units // RING - 1) as i:
                    for slot in range(RING):
                        load(RING + slot, i)
            for unit in range(max(units // RING, 1) * RING, units):
                load(unit)

        @block.gpsimd
        def _(pool):
            own = Own(pool, pool_own)
            for stage in c.stages:
                stage.gpsimd(pool, own)

        @block.scalar
        def _(act):
            own = Own(act, scalar_own)
            for stage in c.stages:
                stage.scalar(act, own)

        @block.vector
        def _(dve):
            own = Own(dve, vector_own)
            for stage in c.stages:
                stage.vector(dve, own)

        @block.tensor
        def _(pe):
            for stage in c.stages:
                stage.tensor(pe)

        return units




def moving_units(w):
    k, n = w.shape
    blocks = -(-n // PIECE)
    if n < blocks * PIECE:
        w = np.concatenate([w, np.zeros((k, blocks * PIECE - n), w.dtype)], 1)
    pieces = w.reshape(k // P, P, blocks, PIECE).transpose(2, 0, 1, 3).reshape(-1, P, PIECE)
    return pieces.reshape(-1, 2, P, PIECE).transpose(0, 2, 1, 3).reshape(-1, P, UNIT)


def standing_units(w):
    k, n = w.shape
    chunks = -(-n // P)
    if n < chunks * P:
        w = np.concatenate([w, np.zeros((k, chunks * P - n), w.dtype)], 1)
    pieces = w.reshape(k // P, P, chunks, P).transpose(2, 0, 1, 3).reshape(-1, P, P)
    if len(pieces) % 8:
        pieces = np.concatenate([pieces, np.zeros((-len(pieces) % 8, P, P), w.dtype)])
    return pieces.reshape(-1, 8, P, P).transpose(0, 2, 1, 3).reshape(-1, P, UNIT)


def loop_units(firsts, last):
    n = len(last)
    out = [f[0] for f in firsts]
    for c in range(n):
        if c + 1 < n:
            out += [f[c + 1] for f in firsts]
        out.append(last[c])
    return np.stack(out)


def peer_units(w_q, u, v):
    yield standing_units(w_q)
    first = u.reshape(N_KEYS, N_KEYS, KD, P).transpose(1, 3, 2, 0).reshape(N_KEYS, P, UNIT)
    last = v.reshape(N_KEYS, N_KEYS, D).transpose(1, 0, 2)
    yield np.concatenate([first[:AHEAD], last[:AHEAD], loop_units([first[AHEAD:]], last[AHEAD:])])


def swiglu_units(gate, up, down):
    return loop_units([standing_units(gate), standing_units(up)], down.reshape(-1, P, D))


def stream_of(i):
    yield moving_units(i["ret_w_in"][0])
    yield moving_units(i["ret_w_out"][0][:D])
    yield moving_units(i["ret_w_out"][0][D:])
    yield from peer_units(i["peer_w_q"][0], i["peer_u"][0], i["peer_v"][0])
    yield moving_units(i["diff_w_q"][0])
    yield moving_units(i["kv_w"])
    yield moving_units(i["diff_w_out"][0])
    yield from peer_units(i["peer_w_q"][1], i["peer_u"][1], i["peer_v"][1])
    for layer in range(2):
        w_in, w_out = i["ffn_w_in_2"][layer], i["ffn_w_out_2"][layer]
        yield swiglu_units(w_in[0, :, :D_FF], w_in[0, :, D_FF:], w_out[0])
        if layer == 0:
            yield moving_units(i["mla_w_down_2"][0])
            w_uq = i["mla_w_uq_2"][0].reshape(256, 8, 192)
            yield standing_units(w_uq[:, :, :128].reshape(256, 1024))
            yield moving_units(w_uq[:, :, 128:].reshape(256, 512))
            w_ukv = i["mla_w_ukv_2"][0].reshape(128, 8, 256)
            yield standing_units(w_ukv[:, :, :128].reshape(128, 1024))
            yield moving_units(w_ukv[:, :, 128:].reshape(128, 1024))
            yield moving_units(i["mla_w_o_2"][0])
        else:
            w = i["fox_w_in_2"][0]
            yield standing_units(w[:, :2048])
            yield moving_units(w[:, 2048:3072])
            yield standing_units(w[:, 3072:])
            yield moving_units(i["fox_w_o_2"][0])
        yield swiglu_units(w_in[1, :, :D_FF], w_in[1, :, D_FF:], w_out[1])
        yield moving_units(i["ple_w_gate_2"][layer])
        yield moving_units(i["ple_w_proj_2"][layer])
    for layer in range(2):
        gate, up, down = (i[f"ffn_w_{n}_3"][layer] for n in ("gate", "up", "down"))
        yield swiglu_units(gate[0], up[0], down[0])
        if layer == 0:
            w = i["hyb_w_in_3"][0]
            yield moving_units(w[:, :936])
            yield standing_units(w[:, 936:])
            yield moving_units(i["hyb_w_out_3"][0])
        else:
            yield standing_units(i["conf_w_pw1_3"][0])
            yield moving_units(i["conf_w_pw2_3"][0])
        yield swiglu_units(gate[1], up[1], down[1])
    yield np.zeros((HIGHS, P, UNIT), i["x"].dtype)


def columns_of(i):
    def col(a):
        return a.reshape(-1, P).T

    conv = i["hyb_conv_w_3"][0].reshape(3, 4, P).transpose(2, 1, 0).reshape(P, 12)
    conf = i["conf_conv_w_3"][0].reshape(31, KD, P).transpose(2, 1, 0).reshape(P, 248)
    return np.ascontiguousarray(np.concatenate([
        col(i["diff_subln_g"][0]), col(i["mla_q_norm_2"][0]), col(i["mla_kv_norm_2"][0]), conv,
        col(i["conf_b_pw1_3"][0]), conf, col(i["conf_conv_b_3"][0]), col(i["conf_ln_g_3"][0]),
        col(i["conf_ln_b_3"][0])], 1))


def rows_from(i):
    def padded(a):
        a = a.reshape(1, -1)
        return np.concatenate([a, np.zeros((1, D - a.shape[1]), a.dtype)], 1)

    return np.concatenate([i["ln_g"].reshape(4, D), i["ln_b"].reshape(4, D), i["final_norm_2"][None],
                           i["final_norm_3"][None], i["conf_b_pw2_3"], padded(i["diff_lambda"]),
                           padded(i["fox_b_f_2"]), *(i[n].reshape(-1, D) for n in (
                               "ffn_norm_2", "mix_norm_2", "ple_norm_2", "ffn_norm_3", "mix_norm_3"))], 0)


def arrays_of(i):
    tables = constant_tables()
    return {
        "x_dram": i["x"].reshape(SEQ, D),
        "stream_dram": np.concatenate(list(stream_of(i)), 0),
        "const_dram": np.concatenate([tables[name] for name in RESIDENT], 1),
        "fetched_dram": np.concatenate([tables[name] for name in FETCHED], 1),
        "subkeysT_dram": np.ascontiguousarray(i["peer_subkeys"].reshape(2, 16, N_KEYS, P).transpose(0, 3, 1, 2)),
        "cols_dram": columns_of(i),
        "rows_dram": rows_from(i),
        "positions_dram": i["positions_2"],
        "pT_dram": np.ascontiguousarray(i["p_2"][:, 0].reshape(2, SEQ, 2, P).transpose(0, 3, 2, 1)),
    }


def kernel(**inputs):
    import concourse.bacc as bacc
    from concourse.bass_utils import run_bass_kernel_spmd

    arrays = arrays_of({k: np.asarray(v) for k, v in inputs.items()})
    nc = bacc.Bacc("TRN2", target_bir_lowering=False, num_devices=1)
    dram = {n.removesuffix("_dram"): nc.dram_tensor(n, a.shape, mybir.dt.from_np(a.dtype), kind="ExternalInput").ap()
            for n, a in arrays.items()}
    dram["out"] = nc.dram_tensor("out_dram", (SEQ, D), F32, kind="ExternalOutput").ap()
    units = build(nc, dram)
    assert units == len(arrays["stream_dram"]), (units, len(arrays["stream_dram"]))
    r = run_bass_kernel_spmd(nc, [arrays], core_ids=[0])
    return r.results[0]["out_dram"].reshape(1, SEQ, D)
```
